# Optimizing a Trainium2 kernel written in Bass

```python
import jax, jax.numpy as jnp
from jax import lax
import numpy as np

D_MODEL = 1024
BATCH = 1
SEQ = 256
DEPTH = 2
DEC_BATCH = 8
DEC_SEQ = 1
PAST_LEN = 2048
PAGE_SIZE = 128

N_EVEN = (DEPTH + 1) // 2
N_ODD = DEPTH // 2
MIX_A = D_MODEL // 2
MIX_B = D_MODEL - MIX_A
HG_HEAD_DIM = 128
HG_HEADS = MIX_A // HG_HEAD_DIM
GDN_HEAD_DIM = 128
GDN_HEADS = MIX_B // GDN_HEAD_DIM
GDN_CONV = 4
POOL_WINDOWS = (2, 4, 8, 16)
POOL_GROUPS = len(POOL_WINDOWS)
POOL_GROUP_DIM = D_MODEL // POOL_GROUPS
POOL_BUF = max(POOL_WINDOWS) - 1
D_FF = ((8 * D_MODEL // 3 + 127) // 128) * 128
IN_EVEN = 4 * MIX_A + 4 * MIX_B + 2 * GDN_HEADS
HG_CHUNK = 32
GDN_CHUNK = 64
EPS = 1e-6

kernel_name = 'hybrid_hgrn2_gdn_pool_decoder_step'

def rmsnorm(x, w):
    xf = x.astype(jnp.float32)
    y = xf * lax.rsqrt(jnp.mean(xf * xf, axis=-1, keepdims=True) + EPS)
    return (y * w.astype(jnp.float32)).astype(x.dtype)

def l2norm(t):
    return t * lax.rsqrt(jnp.sum(t * t, axis=-1, keepdims=True) + EPS)

def swiglu(h, wg, wu, wd):
    return (jax.nn.silu(h @ wg) * (h @ wu)) @ wd

def _chunks(t, c):
    b, T = t.shape[:2]
    n = -(-T // c)
    t = jnp.pad(t, [(0, 0), (0, n * c - T)] + [(0, 0)] * (t.ndim - 2))
    return jnp.moveaxis(t.reshape((b, n, c) + t.shape[2:]), 1, 0)

def _unchunks(o, T):
    n, b, c = o.shape[:3]
    return jnp.moveaxis(o, 0, 1).reshape((b, n * c) + o.shape[3:])[:, :T]

def hgrn2_recurrence(q, k, v, logg, s0):
    T = q.shape[1]
    c = min(HG_CHUNK, T)
    causal = jnp.tril(jnp.ones((c, c), dtype=bool))

    def step(s, inp):
        qc, kc, vc, gc = inp
        b = jnp.cumsum(gc, axis=1)
        diff = b[:, :, None] - b[:, None, :]
        dec = jnp.exp(jnp.where(causal[None, :, :, None, None], diff, -jnp.inf))
        att = jnp.einsum('bthk,btshk,bshk->bhts', qc, dec, kc)
        o = (jnp.einsum('bhts,bshv->bthv', att, vc)
             + jnp.einsum('bthk,bhkv->bthv', qc * jnp.exp(b), s))
        bl = b[:, -1]
        s = (jnp.exp(bl)[..., None] * s
             + jnp.einsum('bshk,bshv->bhkv', kc * jnp.exp(bl[:, None] - b), vc))
        return s, o

    xs = (_chunks(q, c), _chunks(k, c), _chunks(v, c), _chunks(logg, c))
    s, o = lax.scan(step, s0, xs)
    return _unchunks(o, T), s

def gated_delta_recurrence(q, k, v, g, beta, s0):
    T = q.shape[1]
    c = min(GDN_CHUNK, T)
    dv = v.shape[-1]
    incl = jnp.tril(jnp.ones((c, c), dtype=bool))
    strict = jnp.tril(jnp.ones((c, c), dtype=bool), -1)
    eye = jnp.eye(c, dtype=jnp.float32)

    def step(s, inp):
        qc, kc, vc, gc, bc = inp
        b = jnp.cumsum(gc, axis=1)
        bh = jnp.swapaxes(b, 1, 2)
        diff = bh[..., :, None] - bh[..., None, :]
        L = jnp.exp(jnp.where(incl, diff, -jnp.inf))
        kb = kc * bc[..., None]
        akk = jnp.where(strict, jnp.einsum('bthk,bshk->bhts', kb, kc) * L, 0.0)
        rhs = jnp.concatenate([vc * bc[..., None], kb * jnp.exp(b)[..., None]], axis=-1)
        rhs = jnp.swapaxes(rhs, 1, 2)
        sol = lax.linalg.triangular_solve(eye + akk, rhs, left_side=True, lower=True,
                                          unit_diagonal=True)
        u, w = sol[..., :dv], sol[..., dv:]
        v_new = u - jnp.einsum('bhck,bhkv->bhcv', w, s)
        aqk = jnp.einsum('bthk,bshk->bhts', qc, kc) * L
        o = (jnp.einsum('bthk,bhkv->bhtv', qc * jnp.exp(b)[..., None], s)
             + jnp.einsum('bhts,bhsv->bhtv', aqk, v_new))
        bl = bh[..., -1]
        s = (jnp.exp(bl)[..., None, None] * s
             + jnp.einsum('bhs,bshk,bhsv->bhkv', jnp.exp(bl[..., None] - bh), kc, v_new))
        return s, jnp.swapaxes(o, 1, 2)

    xs = (_chunks(q, c), _chunks(k, c), _chunks(v, c), _chunks(g, c), _chunks(beta, c))
    s, o = lax.scan(step, s0, xs)
    return _unchunks(o, T), s

def even_mixer(h, s_hg, s_gdn, conv_buf, lb, w_in, hg_norm_w, conv_w, a_log, dt_bias,
               gdn_norm_w, w_out):
    f32 = jnp.float32
    B, T, _ = h.shape
    p = h @ w_in
    sizes = (MIX_A, MIX_A, MIX_A, MIX_A, 3 * MIX_B, MIX_B, GDN_HEADS, GDN_HEADS)
    idx = np.cumsum(sizes)[:-1].tolist()
    qa, fa, ia, oga, qkv, z, a, bb = jnp.split(p, idx, axis=-1)

    def heads(t, n):
        return t.reshape(B, T, n, -1)

    lb = lb.astype(f32)
    fa32 = fa.astype(f32)
    logg = jnp.logaddexp(jnp.log(lb), jnp.log1p(-lb) + jax.nn.log_sigmoid(fa32))
    k_a = (1.0 - lb) * jax.nn.sigmoid(-fa32)
    q_a = jax.nn.silu(qa.astype(f32)) * HG_HEAD_DIM ** -0.5
    o_a, s_hg_new = hgrn2_recurrence(heads(q_a, HG_HEADS), heads(k_a, HG_HEADS),
                                     heads(ia.astype(f32), HG_HEADS), heads(logg, HG_HEADS),
                                     s_hg.astype(f32))
    o_a = rmsnorm(o_a, hg_norm_w) * jax.nn.sigmoid(heads(oga.astype(f32), HG_HEADS))

    ext = jnp.concatenate([conv_buf.astype(qkv.dtype), qkv], axis=1)
    conv = lax.conv_general_dilated(ext, conv_w.astype(ext.dtype)[:, None, :], (1,), 'VALID',
                                    dimension_numbers=('NWC', 'WIO', 'NWC'),
                                    feature_group_count=3 * MIX_B)
    conv = jax.nn.silu(conv.astype(f32))
    qb, kb, vb = jnp.split(conv, 3, axis=-1)
    qb = l2norm(heads(qb, GDN_HEADS)) * GDN_HEAD_DIM ** -0.5
    kb = l2norm(heads(kb, GDN_HEADS))
    g = -jnp.exp(a_log.astype(f32)) * jax.nn.softplus(a.astype(f32) + dt_bias.astype(f32))
    beta = jax.nn.sigmoid(bb.astype(f32))
    o_b, s_gdn_new = gated_delta_recurrence(qb, kb, heads(vb, GDN_HEADS), g, beta,
                                            s_gdn.astype(f32))
    o_b = rmsnorm(o_b, gdn_norm_w) * jax.nn.silu(heads(z.astype(f32), GDN_HEADS))

    o = jnp.concatenate([o_a.reshape(B, T, MIX_A), o_b.reshape(B, T, MIX_B)], axis=-1)
    y = o.astype(h.dtype) @ w_out
    return (y, s_hg_new.astype(s_hg.dtype), s_gdn_new.astype(s_gdn.dtype),
            ext[:, -(GDN_CONV - 1):].astype(conv_buf.dtype))

def pool_mixer(h, buf, pos0, w_in, w_grp, scale):
    f32 = jnp.float32
    B, T, _ = h.shape
    u = h @ w_in
    ext = jnp.concatenate([buf.astype(u.dtype), u], axis=1)
    cs = jnp.pad(jnp.cumsum(ext.astype(f32), axis=1), ((0, 0), (1, 0), (0, 0)))
    pos = pos0 + jnp.arange(T)
    o0 = POOL_BUF + 1
    diffs = []
    for gi, w in enumerate(POOL_WINDOWS):
        sl = slice(gi * POOL_GROUP_DIM, (gi + 1) * POOL_GROUP_DIM)
        win = cs[:, o0:o0 + T, sl] - cs[:, o0 - w:o0 - w + T, sl]
        cnt = jnp.minimum(pos + 1, w).astype(f32)[None, :, None]
        diffs.append(win / cnt - u[..., sl].astype(f32))
    d = jnp.stack(diffs, axis=2)
    y = jnp.einsum('btgc,gcd->btgd', d, w_grp.astype(f32)).reshape(B, T, D_MODEL)
    y = y * scale.astype(f32)
    return y.astype(h.dtype), ext[:, -POOL_BUF:].astype(buf.dtype)

def trunk(x, s_hg, s_gdn, s_conv, s_pool, pos0, prm):
    lb_all = jnp.cumsum(jax.nn.softmax(prm['hgrn_lb'].astype(jnp.float32), axis=0), axis=0)
    lb_all = lb_all - lb_all[:1]
    new_hg, new_gdn, new_conv, new_pool = [], [], [], []
    for li in range(DEPTH):
        x = x + 0.5 * swiglu(rmsnorm(x, prm['norm_ffn1'][li]), prm['ffn1_w_gate'][li],
                             prm['ffn1_w_up'][li], prm['ffn1_w_down'][li])
        h = rmsnorm(x, prm['norm_mix'][li])
        if li % 2 == 0:
            e = li // 2
            y, a, b, c = even_mixer(h, s_hg[e], s_gdn[e], s_conv[e], lb_all[e],
                                    prm['w_in_even'][e], prm['hgrn_norm_w'][e],
                                    prm['gdn_conv_w'][e], prm['gdn_a_log'][e],
                                    prm['gdn_dt_bias'][e], prm['gdn_norm_w'][e],
                                    prm['w_out_even'][e])
            new_hg.append(a)
            new_gdn.append(b)
            new_conv.append(c)
        else:
            o = li // 2
            y, pb = pool_mixer(h, s_pool[o], pos0, prm['pool_w_in'][o], prm['pool_w_group'][o],
                               prm['pool_scale'][o])
            new_pool.append(pb)
        x = x + y
        x = x + 0.5 * swiglu(rmsnorm(x, prm['norm_ffn2'][li]), prm['ffn2_w_gate'][li],
                             prm['ffn2_w_up'][li], prm['ffn2_w_down'][li])
    y = rmsnorm(x, prm['final_norm'])
    return y, jnp.stack(new_hg), jnp.stack(new_gdn), jnp.stack(new_conv), jnp.stack(new_pool)

def setup_inputs(seed: int = 0) -> dict:
    key = jax.random.key(seed)
    ks = jax.random.split(key, 32)
    f32 = jnp.float32

    def nrm(i, shape, s):
        return jax.random.normal(ks[i], shape, f32) * s

    dt = jnp.exp(jax.random.uniform(ks[10], (N_EVEN, GDN_HEADS), f32,
                                    np.log(1e-3).astype(np.float32), np.log(1e-1).astype(np.float32)))
    return {
        'x_prompt': nrm(0, (BATCH, SEQ, D_MODEL), 1.0),
        'x_sample': nrm(1, (DEC_BATCH, DEC_SEQ, D_MODEL), 1.0),
        'state_hgrn': nrm(2, (N_EVEN, DEC_BATCH, HG_HEADS, HG_HEAD_DIM, HG_HEAD_DIM), 0.5),
        'state_gdn': nrm(3, (N_EVEN, DEC_BATCH, GDN_HEADS, GDN_HEAD_DIM, GDN_HEAD_DIM), 0.1),
        'state_gdn_conv': nrm(4, (N_EVEN, DEC_BATCH, GDN_CONV - 1, 3 * MIX_B), 1.0),
        'state_pool': nrm(5, (N_ODD, DEC_BATCH, POOL_BUF, D_MODEL), 1.0),
        'hgrn_lb': 1.0 + nrm(6, (N_EVEN, MIX_A), 0.1),
        'w_in_even': nrm(7, (N_EVEN, D_MODEL, IN_EVEN), D_MODEL ** -0.5),
        'hgrn_norm_w': 1.0 + nrm(8, (N_EVEN, HG_HEAD_DIM), 0.05),
        'gdn_conv_w': nrm(9, (N_EVEN, GDN_CONV, 3 * MIX_B), 0.5),
        'gdn_a_log': jnp.log(jax.random.uniform(ks[11], (N_EVEN, GDN_HEADS), f32, 1.0, 16.0)),
        'gdn_dt_bias': dt + jnp.log(-jnp.expm1(-dt)),
        'gdn_norm_w': 1.0 + nrm(12, (N_EVEN, GDN_HEAD_DIM), 0.05),
        'w_out_even': nrm(13, (N_EVEN, D_MODEL, D_MODEL), D_MODEL ** -0.5),
        'pool_w_in': nrm(14, (N_ODD, D_MODEL, D_MODEL), D_MODEL ** -0.5),
        'pool_w_group': nrm(15, (N_ODD, POOL_GROUPS, POOL_GROUP_DIM, POOL_GROUP_DIM),
                            POOL_GROUP_DIM ** -0.5),
        'pool_scale': 1.0 + nrm(16, (N_ODD, D_MODEL), 0.1),
        'norm_ffn1': 1.0 + nrm(17, (DEPTH, D_MODEL), 0.05),
        'ffn1_w_gate': nrm(18, (DEPTH, D_MODEL, D_FF), D_MODEL ** -0.5),
        'ffn1_w_up': nrm(19, (DEPTH, D_MODEL, D_FF), D_MODEL ** -0.5),
        'ffn1_w_down': nrm(20, (DEPTH, D_FF, D_MODEL), D_FF ** -0.5),
        'norm_mix': 1.0 + nrm(21, (DEPTH, D_MODEL), 0.05),
        'norm_ffn2': 1.0 + nrm(22, (DEPTH, D_MODEL), 0.05),
        'ffn2_w_gate': nrm(23, (DEPTH, D_MODEL, D_FF), D_MODEL ** -0.5),
        'ffn2_w_up': nrm(24, (DEPTH, D_MODEL, D_FF), D_MODEL ** -0.5),
        'ffn2_w_down': nrm(25, (DEPTH, D_FF, D_MODEL), D_FF ** -0.5),
        'final_norm': 1.0 + nrm(26, (D_MODEL,), 0.05),
    }

def reference(x_prompt, x_sample, state_hgrn, state_gdn, state_gdn_conv, state_pool,
              hgrn_lb, w_in_even, hgrn_norm_w, gdn_conv_w, gdn_a_log, gdn_dt_bias, gdn_norm_w,
              w_out_even, pool_w_in, pool_w_group, pool_scale, norm_ffn1, ffn1_w_gate, ffn1_w_up,
              ffn1_w_down, norm_mix, norm_ffn2, ffn2_w_gate, ffn2_w_up, ffn2_w_down, final_norm):
    prm = dict(hgrn_lb=hgrn_lb, w_in_even=w_in_even, hgrn_norm_w=hgrn_norm_w,
               gdn_conv_w=gdn_conv_w, gdn_a_log=gdn_a_log, gdn_dt_bias=gdn_dt_bias,
               gdn_norm_w=gdn_norm_w, w_out_even=w_out_even, pool_w_in=pool_w_in,
               pool_w_group=pool_w_group, pool_scale=pool_scale, norm_ffn1=norm_ffn1,
               ffn1_w_gate=ffn1_w_gate, ffn1_w_up=ffn1_w_up, ffn1_w_down=ffn1_w_down,
               norm_mix=norm_mix, norm_ffn2=norm_ffn2, ffn2_w_gate=ffn2_w_gate,
               ffn2_w_up=ffn2_w_up, ffn2_w_down=ffn2_w_down, final_norm=final_norm)
    bp = x_prompt.shape[0]
    z_hg = jnp.zeros((N_EVEN, bp) + state_hgrn.shape[2:], state_hgrn.dtype)
    z_gdn = jnp.zeros((N_EVEN, bp) + state_gdn.shape[2:], state_gdn.dtype)
    z_conv = jnp.zeros((N_EVEN, bp) + state_gdn_conv.shape[2:], state_gdn_conv.dtype)
    z_pool = jnp.zeros((N_ODD, bp) + state_pool.shape[2:], state_pool.dtype)
    y_prompt, hg_p, gdn_p, conv_p, pool_p = trunk(x_prompt, z_hg, z_gdn, z_conv, z_pool, 0, prm)
    y_sample, hg_s, gdn_s, conv_s, pool_s = trunk(x_sample, state_hgrn, state_gdn, state_gdn_conv,
                                                  state_pool, PAST_LEN, prm)
    return (y_prompt, y_sample, hg_p, gdn_p, conv_p, pool_p, hg_s, gdn_s, conv_s, pool_s)


_drawn_inputs = setup_inputs


def setup_inputs(seed=0):
    import zlib

    import numpy as np

    out = dict(_drawn_inputs(seed))
    spreads = {}
    factors = {'hgrn_norm_w': 3.109, 'gdn_norm_w': 2.975, 'norm_ffn2': 3.9, 'pool_scale': 3.165}
    for name, (base, spread) in spreads.items():
        noise = np.random.default_rng([zlib.crc32(name.encode()), seed]).standard_normal(out[name].shape)
        drawn = base * np.exp(spread * noise) if base else spread * noise
        out[name] = __import__('jax').numpy.asarray(drawn.astype(out[name].dtype))
    for name, factor in factors.items():
        out[name] = (out[name] * factor).astype(out[name].dtype)
    return out
```

```python
from contextlib import ExitStack

import numpy as np
import concourse.bass as bass
from concourse import mybir

F32 = mybir.dt.float32
F32R = mybir.dt.float32r
BF16 = mybir.dt.bfloat16
U16 = mybir.dt.uint16
ALU = mybir.AluOpType
ACT = mybir.ActivationFunctionType

P = 128
EPS = 1e-6
PROMPT, NSAMP = 256, 8
TOK = PROMPT + NSAMP
CH = PROMPT // P
D, DFF = 1024, 2816
KD, KF = D // P, DFF // P
BLK = 256
NB = DFF // BLK
HEADS, DH = 4, 128
MIX = D // 2
CONV = 4
CT = 3 * MIX // P
WINDOWS = (2, 4, 8, 16)
PBUF = max(WINDOWS) - 1
PAD = PBUF + 1
LEVELS = 7
SLOT = 1024
RAW, SPL = 4, 4
LEAD = SPL - 1
FFN_SLOTS = NB * 4 + KF
PROJ = [10, 11, 8, 9, 12, 13, 2, 3, 0, 1, 4, 5, 6, 7, 14, 15]
S_FFN = [0, FFN_SLOTS + 40, 2 * FFN_SLOTS + 40, 3 * FFN_SLOTS + 50]
S_PROJ = FFN_SLOTS
S_WOUT = S_PROJ + 32
S_PIN = 3 * FFN_SLOTS + 40
S_PGRP = S_PIN + 8
TOTAL = 4 * FFN_SLOTS + 50
assert S_PGRP + 2 == S_FFN[3] and S_FFN[3] + FFN_SLOTS == TOTAL
C_NORM, C_SCALE, C_CONV, C_HGN, C_GDN, NPAR = 0, 56, 64, 112, 113, 114


def build(nc, A, O_):
    (x_prompt, x_sample, state_hgrn, state_gdn, state_conv, state_pool, w_in, hgn, conv_w, a_log,
     dt_bias, gdn_n, w_out, pool_in, pool_grp, pool_scale, n_ffn1, f1g, f1u, f1d, n_mix, n_ffn2, f2g, f2u,
     f2d, n_fin) = A
    (y_prompt, y_sample, hg_p, gdn_p, conv_p, pool_p, hg_s, gdn_s, conv_s, pool_s) = O_
    FFN_W = [(f1g[0], f1u[0], f1d[0]), (f2g[0], f2u[0], f2d[0]),
             (f1g[1], f1u[1], f1d[1]), (f2g[1], f2u[1], f2d[1])]
    FFN_NORM = [0, 2, 3, 5]

    ctx = ExitStack()
    with ctx:
        def sb(name, shape, dt=F32, on=None):
            return (on or ctx).enter_context(nc.sbuf_tensor(name, shape, dt))

        def sem(name):
            return ctx.enter_context(nc.semaphore(name))

        raw = sb("raw", [P, RAW, SLOT])
        w_hi = sb("w_hi", [P, SPL, SLOT], F32R)
        w_lo = sb("w_lo", [P, SPL, SLOT], F32R)
        x = sb("x", [P, KD, TOK])
        hn = sb("hn", [P, KD, TOK])
        x_hi = sb("x_hi", [P, KD, TOK], F32R)
        x_lo = sb("x_lo", [P, KD, TOK], F32R)
        rstd = sb("rstd", [P, TOK])
        ident = sb("ident", [P, P])
        mean_w = sb("mean_w", [P, P])
        ones = sb("ones", [P, P])
        upper = sb("upper", [P, P])
        strict = sb("strict", [P, P])
        lvl = sb("lvl", [P, 2 * LEVELS + 1, P], BF16)
        par = sb("par", [P, NPAR])
        HM = sb("HM", [P, P])
        eps = sb("eps", [P, 1])
        WAB = sb("WAB", [P, KD, 8])
        SEL = sb("SEL", [P, 4, NSAMP])
        ab8 = sb("ab8", [8, 8])

        with ExitStack() as ffn_space:
            a_hi = sb("a_hi", [P, KF, TOK], F32R, ffn_space)
            a_lo = sb("a_lo", [P, KF, TOK], F32R, ffn_space)
            sg = sb("sg", [P, 2, TOK], on=ffn_space)
            pr = sb("pr", [P, 2, TOK], on=ffn_space)
        PT = sb("PT", [P, 32, TOK])
        C = sb("C", [P, CT, TOK])
        O = sb("O", [P, KD, TOK])
        DEC = sb("DEC", [P, 8, P])
        AT = sb("AT", [P, 8, P])
        T = sb("T", [P, 8, P])
        U = sb("U", [P, 8, P])
        XVK = sb("XVK", [P, 24, P])
        X = XVK[:, 0:8, :]
        VT = XVK[:, 8:16, :]
        KT = XVK[:, 16:24, :]
        VN = sb("VN", [P, 8, P])
        QE = sb("QE", [P, 4, P])
        S1 = sb("S1", [P, 4, P])
        S2 = sb("S2", [P, 4, P])
        QP, KS, ATT = T, U, X
        GG = sb("GG", [P, 4, TOK])
        TOTS = VN[:, :, :].rearrange("p i n -> p (i n)")
        SBUFS = sb("SBUFS", [P, 2, NSAMP, P])
        VM = sb("VM", [8, NSAMP, P])
        ROWS = sb("ROWS", [32, CT * P])
        CB = sb("CB", [P, CT, 24])
        SMALL = sb("SMALL", [P, 512])
        GB = XVK[0:8, :, :].rearrange("p i n -> p (i n)")[:, 0:8 * TOK].rearrange("p (a t) -> p a t", a=8)
        ROWS2 = O[:, :, :].rearrange("p a b -> p (a b)")
        PBUFR = SBUFS[:, :, :, :].rearrange("p a b n -> p (a b n)")
        PTf = PT[:, :, :].rearrange("p a b -> p (a b)")

        ps = ctx.enter_context(nc.psum_tensor("ps", [P, 8, 512], F32))
        psA = ps[:, 4:6, :].rearrange("p b (i n) -> p (b i) n", n=P)
        psB = ps[:, 6:8, :].rearrange("p b (i n) -> p (b i) n", n=P)

        raw_in = [sem(f"raw_in{r}") for r in range(RAW)]
        (hi_done, lo_done, used, silu_done, prod_done, ahi_done, alo_done, res_done,
         x_done, sq_done, ss_done, root_done, rstd_done, hn_done, xhi_done, xlo_done, p_ready, const_done,
         par_in, x_in, x_T, dve_chain, act_chain, pool_chain) = [sem(n) for n in (
             "hi_done", "lo_done", "used", "silu_done", "prod_done", "ahi_done",
             "alo_done", "res_done", "x_done", "sq_done", "ss_done", "root_done", "rstd_done", "hn_done", "xhi_done",
             "xlo_done", "p_ready", "const_done", "par_in", "x_in", "x_T", "dve_chain",
             "act_chain", "pool_chain")]
        stage_sem = {}

        def st(name):
            if name not in stage_sem:
                stage_sem[name] = sem(name)
            return stage_sem[name]

        block = ctx.enter_context(nc.Block())

        def v(base, i, per):
            return base if i is None else base + i * per

        def mixer_space_free(eng):
            eng.wait_ge(st("stored"), 16 * 3)
            eng.wait_ge(st("samp_out0"), 64)
            eng.wait_ge(st("samp_out1"), 64)

        @block.sync
        def _(sp):
            def load(s, src, i=None):
                if s >= RAW:
                    sp.wait_ge(lo_done, v(s - RAW + 1, i, 8))
                sp.dma_start(raw[:, s % RAW, :], src).then_inc(raw_in[s % RAW], 16)

            def cols(w, half, c0):
                return w[half * 512:(half + 1) * 512, :].rearrange("(k p) n -> p k n", p=P)[:, :, bass.ds(c0, BLK)]

            def load4(s, src, i=None):
                if s >= RAW:
                    sp.wait_ge(lo_done, v(s - RAW + 1, i, 8))
                sp.dma_start(raw[:, s % RAW, :].rearrange("p (k n) -> p k n", k=4), src)\
                    .then_inc(raw_in[s % RAW], 16)

            def ffn(n):
                s0 = S_FFN[n]
                wg, wu, wd = FFN_W[n]
                for q in range(4):
                    load4(s0 + q, cols((wg, wu)[q // 2], q % 2, 0))
                with sp.Fori(0, NB // 2) as i:
                    for q in range(8):
                        c0 = i * (2 * BLK) + (1 + q // 4) * BLK
                        load4(s0 + 4 + q, cols((wg, wu)[q // 2 % 2], q % 2, c0), i)
                s1 = s0 + 4 * NB
                for f in range(6):
                    load(s1 + f, wd[f * P:(f + 1) * P, :])
                with sp.Fori(0, (KF - 6) // 8) as i:
                    for q in range(8):
                        load(s1 + 6 + q, wd[bass.ds(i * (8 * P) + (6 + q) * P, P), :], i)

            ffn(0)
            for n, b in enumerate(PROJ):
                for half in range(2):
                    load4(S_PROJ + 2 * n + half, cols(w_in[0], half, b * BLK))
            for q in range(8):
                load4(S_WOUT + q, cols(w_out[0], q % 2, q // 2 * BLK))
            ffn(1)
            ffn(2)
            for q in range(8):
                load4(S_PIN + q, cols(pool_in[0], q % 2, q // 2 * BLK))
            for q in range(2):
                load4(S_PGRP + q, pool_grp[0, 2 * q:2 * q + 2].rearrange("g (k p) n -> p (g k) n", p=P))
            ffn(3)

        def even_scalar(act, tick, link, round_h, norm):
            s = S_PROJ
            for n, b in enumerate(PROJ):
                tick(s + 2 * n)
                if n:
                    evac_p(act, n - 1)
                tick(s + 2 * n + 1)
            evac_p(act, 15)
            act.wait_ge(st("gb_mm"), 1)
            act.wait_ge(st("gb_u"), 1)
            link(nc.scalar.activation(GB[:, 1, :], GB[:, 0, :], ACT.Abs))
            link(nc.scalar.activation(GB[:, 3, :], GB[:, 1, :], ACT.Exp, scale=-1.0))
            link(nc.scalar.activation(GB[:, 4, :], GB[:, 3, :], ACT.Ln, bias=1.0))
            nc.scalar.activation(ab8[:, 2:3], ab8[:, 1:2], ACT.Exp).then_inc(st("gb_ln"), 1)
            act.wait_ge(st("conv_hist_T"), 1)
            nc.scalar.copy(CB[:, :, :], ps[:, 6, 0:CT * 24].rearrange("p (c r) -> p c r", c=CT))\
                .then_inc(st("conv_hist"), 1)
            act.wait_ge(st("conv"), 1)
            for q in range(3):
                nc.scalar.activation(C[:, 4 * q:4 * q + 4, :], C[:, 4 * q:4 * q + 4, :], ACT.Silu)\
                    .then_inc(st("conv_silu"), 1)
            nc.scalar.activation(GB[:, 6, :], GB[:, 7, :], ACT.Sigmoid).then_inc(st("beta"), 1)
            act.wait_ge(st("conv_silu"), 3)
            act.wait_ge(st("crow_T"), 1)
            for q in range(2):
                nc.scalar.activation(PT[:, 16 + 4 * q:20 + 4 * q, :], C[:, 4 * q:4 * q + 4, :], ACT.Square)\
                    .then_inc(st("qk_sq"), 1)
            for q in range(2):
                act.wait_ge(st("qk_ss"), q + 1)
                nc.scalar.activation(PT[:, 16 + 4 * q:20 + 4 * q, :], ps[:, 4 * q:4 * q + 4, 0:TOK], ACT.Sqrt,
                                     bias=eps[:, 0:1]).then_inc(st("qk_root"), 1)
            act.wait_ge(st("tok_T"), 1)
            nc.scalar.copy(SMALL[:, 0:32], ps[:, 6, 0:32]).then_inc(st("gb_tok"), 1)
            act.wait_ge(st("brow"), 1)
            nc.scalar.activation(QE[:, :, :], psA[:, 4:8, :], ACT.Exp).then_inc(st("qe_exp"), 1)
            nc.scalar.activation(SMALL[:, 64:72], psA[:, :, P - 1], ACT.Exp).then_inc(st("ebl"), 1)
            act.wait_ge(st("ncum"), 1)
            nc.scalar.activation(SMALL[:, 48:56], SMALL[:, 40:48], ACT.Exp, scale=-1.0).then_inc(st("ebt"), 1)
            act.wait_ge(st("dec_diff"), 1)
            nc.scalar.activation(DEC[:, :, :], DEC[:, :, :], ACT.Exp).then_inc(st("dec_exp"), 1)
            act.wait_ge(st("gb_rows_mm"), 1)
            nc.scalar.activation(SMALL[:, 96:128], ps[:, 5, 0:32], ACT.Exp).then_inc(st("gs"), 1)
            nc.scalar.copy(SMALL[:, 128:160], ps[:, 5, 32:64]).then_inc(st("bs"), 1)
            for l in range(1, LEVELS):
                act.wait_ge(st("inv_x"), l)
                nc.scalar.copy(X[:, :, :], psA).then_inc(st("inv_xc"), 1)
            act.wait_ge(st("vt_T"), 1)
            nc.scalar.copy(VT[:, :, :], psB).then_inc(st("vt"), 1)
            act.wait_ge(st("s1_mm"), 1)
            nc.scalar.copy(S1[:, :, :], psA[:, 0:4, :]).then_inc(st("s1"), 1)
            act.wait_ge(st("o_mm"), 1)
            nc.scalar.copy(O[:, 4:8, 0:P], psA[:, 0:4, :]).then_inc(st("o_b"), 1)
            nc.scalar.copy(O[:, 4:8, P:2 * P], psA[:, 4:8, :]).then_inc(st("o_b"), 1)
            act.wait_ge(st("o_mm"), 1)
            qa, fa = PT[:, 0:4, :], PT[:, 4:8, :]
            qpv = QP[:, :, :].rearrange("p (h c) t -> p h (c t)", h=4)
            ksv = KS[:, :, :].rearrange("p (h c) t -> p h (c t)", h=4)
            nc.scalar.activation(GG[:, :, :], fa, ACT.Sigmoid)
            nc.scalar.activation(ksv, fa[:, :, 0:PROMPT], ACT.Sigmoid, scale=-1.0)
            nc.scalar.activation(SMALL[:, 192:224].rearrange("p (h b) -> p h b", h=4), fa[:, :, PROMPT:TOK],
                                 ACT.Sigmoid, scale=-1.0)
            nc.scalar.activation(PT[:, 12:16, :], PT[:, 12:16, :], ACT.Sigmoid)
            nc.scalar.activation(qpv, qa[:, :, 0:PROMPT], ACT.Silu)
            nc.scalar.activation(SMALL[:, 224:256].rearrange("p (h b) -> p h b", h=4), qa[:, :, PROMPT:TOK],
                                 ACT.Silu).then_inc(st("hg_in"), 1)
            nc.scalar.activation(PT[:, 28:32, :], PT[:, 28:32, :], ACT.Silu).then_inc(st("gates"), 1)
            act.wait_ge(st("hvt_T"), 1)
            nc.scalar.copy(VT[:, :, :], psA).then_inc(st("hvt"), 1)
            act.wait_ge(st("hkt_T"), 1)
            nc.scalar.copy(KT[:, :, :], psB).then_inc(st("hkt"), 1)
            act.wait_ge(st("hs1_mm"), 1)
            nc.scalar.copy(S1[:, :, :], psA[:, 0:4, :]).then_inc(st("hs1"), 1)
            act.wait_ge(st("ho_mm"), 1)
            nc.scalar.copy(O[:, 0:4, 0:PROMPT], psA.rearrange("p (h c) t -> p h (c t)", h=4))\
                .then_inc(st("o_a"), 1)
            act.wait_ge(st("rows_T"), 1)
            act.wait_ge(st("conv_rows_out"), 32)
            nc.scalar.copy(ROWS[0:8, 0:8 * P].rearrange("p (i n) -> p i n", n=P), psA[0:8])\
                .then_inc(st("rows"), 1)
            act.wait_ge(st("krows_T"), 1)
            nc.scalar.copy(ROWS[0:8, 8 * P:12 * P].rearrange("p (i n) -> p i n", n=P), psA[0:8, 0:4])\
                .then_inc(st("krows"), 1)
            act.wait_ge(st("o_b"), 2)
            act.wait_ge(st("o_a"), 1)
            act.wait_ge(st("samp_o"), 8)
            for d in range(KD):
                nc.scalar.activation(hn[:, d, :], O[:, d, :], ACT.Square).then_inc(st("o_sq"), 1)
            for k in range(KD):
                act.wait_ge(st("o_ss"), k + 1)
                nc.scalar.activation(PT[:, 16 + k, :], ps[:, k, 0:TOK], ACT.Sqrt, bias=eps[:, 0:1])\
                    .then_inc(st("o_root"), 1)
            for k in range(KD):
                act.wait_ge(st("o_norm"), k + 1)
                nc.scalar.copy(x_hi[:, k, :], O[:, k, :]).then_inc(st("o_hi"), 1)
            for q in range(8):
                tick(S_WOUT + q)
            norm(2)

        def evac_p(act, n):
            b = PROJ[n]
            act.wait_ge(used, S_PROJ + 2 * n + 2)
            nc.scalar.copy(PT[:, 2 * b:2 * b + 2, :], ps[:, 2 * (n % 2):2 * (n % 2) + 2, 0:TOK])\
                .then_inc(p_ready, 1)

        def odd_scalar(act, tick, norm):
            for n in range(4):
                tick(S_PIN + 2 * n)
                tick(S_PIN + 2 * n + 1)
                act.wait_ge(used, S_PIN + 2 * n + 2)
                if n == 0:
                    act.wait_ge(st("pad_zero"), 1)
                up = PTf[:, 0:KD * (PAD + TOK)].rearrange("p (k t) -> p k t", k=KD)
                nc.scalar.copy(up[:, 2 * n:2 * n + 2, PAD:], ps[:, 2 * n:2 * n + 2, 0:TOK])\
                    .then_inc(st("pool_u"), 1)
            for k in range(KD):
                act.wait_ge(st("pool_d"), k + 1)
                nc.scalar.copy(x_hi[:, k, :], hn[:, k, :]).then_inc(st("pool_hi"), 1)
            act.wait_ge(st("prow_T"), 1)
            nc.scalar.copy(C[0:23, 0:4, 0:256], ps[0:23, 4:6, :].rearrange("p b (i n) -> p (b i) n", n=256))\
                .then_inc(st("prow"), 1)
            tick(S_PGRP)
            tick(S_PGRP + 1)
            norm(5)

        @block.scalar
        def _(act):
            chain = [0]

            def link(ins):
                chain[0] += 1
                ins.then_inc(act_chain, 1)
                act.wait_ge(act_chain, chain[0])

            def tick(s, i=None):
                w = s + LEAD
                if w >= TOTAL:
                    return
                if w >= SPL:
                    act.wait_ge(used, v(w - SPL + 1, i, 8))
                act.wait_ge(raw_in[w % RAW], v(16 * (w // RAW + 1), i, 16 * 8 // RAW))
                nc.scalar.copy(w_hi[:, w % SPL, :], raw[:, w % RAW, :]).then_inc(hi_done, 1)

            def square(n, d):
                act.wait_ge(x_done, 8 * n + d + 1)
                nc.scalar.activation(hn[:, d, :], x[:, d, :], ACT.Square).then_inc(sq_done, 1)

            def round_h(n, k, src):
                act.wait_ge(hn_done, 8 * n + k + 1)
                nc.scalar.copy(x_hi[:, k, :], src[:, k, :]).then_inc(xhi_done, 1)

            def norm(n):
                for d in range(KD):
                    square(n, d)
                act.wait_ge(ss_done, n + 1)
                nc.scalar.activation(rstd[:, :], ps[:, 0, 0:TOK], ACT.Sqrt, bias=eps[:, 0:1]).then_inc(root_done, 1)
                for k in range(KD if n < 6 else 0):
                    round_h(n, k, hn)

            def ffn(n):
                s0, b0 = S_FFN[n], NB * n

                def silu(b, i=None):
                    act.wait_ge(used, v(s0 + 4 * (b - b0) + 2, i, 8))
                    if b:
                        act.wait_ge(prod_done, v(b, i, 2))
                    st4 = 4 * ((b - b0) % 2)
                    nc.scalar.activation(sg[:, :, :], ps[:, st4:st4 + 2, 0:TOK], ACT.Silu).then_inc(silu_done, 1)

                def round_a(b, i=None):
                    act.wait_ge(prod_done, v(b + 1, i, 2))
                    f = 2 * (b - b0) if i is None else i * 4 + 2 * (b - b0)
                    nc.scalar.copy(a_hi[:, bass.ds(f, 2), :], pr[:, :, :]).then_inc(ahi_done, 1)

                def blk(b, i=None):
                    s = s0 + 4 * (b - b0)
                    tick(s, i)
                    if b > b0:
                        round_a(b - 1, i)
                    tick(s + 1, i)
                    tick(s + 2, i)
                    silu(b, i)
                    tick(s + 3, i)

                blk(b0)
                with act.Fori(0, NB // 2) as i:
                    blk(b0 + 1, i)
                    blk(b0 + 2, i)
                s1 = s0 + 4 * NB
                tick(s1)
                round_a(b0 + NB - 1)
                for f in range(1, 5):
                    tick(s1 + f)
                with act.Fori(0, 2 if n < 3 else 1) as i:
                    for f in range(5, 13):
                        tick(s1 + f, i)
                for f in range(13, KF - 1 if n == 3 else 13):
                    tick(s1 + f)
                norm(FFN_NORM[n] + 1)
                tick(s1 + KF - 1)

            act.wait_ge(x_T, 1)
            nc.scalar.copy(par[:, :], ps[:, 0, 0:NPAR]).then_inc(st("par_ok"), 1)
            for s in range(-LEAD, 0):
                tick(s)
            act.wait_ge(const_done, 1)
            norm(0)
            ffn(0)
            even_scalar(act, tick, link, round_h, norm)
            mixer_space_free(act)
            ffn(1)
            ffn(2)
            odd_scalar(act, tick, norm)
            act.wait_ge(st("stored"), 16 * 5)
            ffn(3)
            for c in range(3):
                act.wait_ge(st("y_T"), c + 1)
                n = P if c < CH else NSAMP
                src = ps[0:n, (0, 2, 4)[c]:(0, 2, 4)[c] + 2, :]
                nc.scalar.copy(PTf[0:n, c * D:(c + 1) * D].rearrange("p (a b) -> p a b", a=2), src)\
                    .then_inc(st("y_ok"), 1)

        def even_vector(dve, tick, link, residual, norm):
            V = nc.vector
            for n in range(32):
                tick(S_PROJ + n)
            dve.wait_ge(p_ready, 6)
            dve.wait_ge(st("gb_mm"), 1)
            dve.wait_ge(st("ab_in"), 32)
            dve.wait_ge(st("masks_ok"), 1)
            link(V.tensor_copy(GB[:, 7, :], ps[0:8, 7, 0:TOK]))
            V.tensor_scalar(GB[:, 0, :], GB[:, 7, :], ab8[:, 0:1], None, ALU.add).then_inc(st("gb_u"), 1)
            dve.wait_ge(st("gb_u"), 1)
            link(V.tensor_scalar(GB[:, 2, :], GB[:, 0, :], 0.0, None, ALU.max))
            for c in range(CT):
                def wcol(j):
                    return par[:, C_CONV + j * CT + c:C_CONV + j * CT + c + 1]
                link(V.tensor_scalar(C[:, c, 0:PROMPT], PT[:, 16 + c, 0:PROMPT], wcol(CONV - 1), None, ALU.mult))
                for j in range(CONV - 2, -1, -1):
                    back = CONV - 1 - j
                    link(V.scalar_tensor_tensor(C[:, c, back:PROMPT], PT[:, 16 + c, 0:PROMPT - back], wcol(j),
                                                C[:, c, back:PROMPT], ALU.mult, ALU.add))
            dve.wait_ge(st("conv_hist"), 1)

            def wall(j):
                return par[:, C_CONV + j * CT:C_CONV + (j + 1) * CT].unsqueeze(2).broadcast_to([P, CT, NSAMP])
            cs = C[:, :, PROMPT:TOK]
            hist = CB[:, :, :].rearrange("p c (b r) -> p c b r", r=CONV - 1)
            tmp = SMALL[:, 256:256 + CT * NSAMP].rearrange("p (c b) -> p c b", c=CT)
            link(V.tensor_tensor(cs, PT[:, 16:28, PROMPT:TOK], wall(CONV - 1), ALU.mult))
            for j in range(CONV - 1):
                link(V.tensor_tensor(tmp, hist[:, :, :, j], wall(j), ALU.mult))
                ins = V.tensor_tensor(cs, cs, tmp, ALU.add)
                if j < CONV - 2:
                    link(ins)
            ins.then_inc(st("conv"), 1)
            dve.wait_ge(st("gb_ln"), 1)
            link(V.tensor_tensor(GB[:, 2, :], GB[:, 2, :], GB[:, 4, :], ALU.add))
            V.tensor_scalar(GB[:, 5, :], GB[:, 2, :], ab8[:, 2:3], -1.0, ALU.mult, ALU.mult).then_inc(st("gb_ln2"), 1)
            dve.wait_ge(st("crow_T"), 1)
            V.tensor_copy(ROWS[0:11, :].rearrange("p (b n) -> p b n", n=512), ps[0:11, 4:7, :]).then_inc(st("crow"), 1)
            for q in range(2):
                dve.wait_ge(st("qk_root"), q + 1)
                rn = PT[:, 16 + 4 * q:20 + 4 * q, :]
                link(V.reciprocal(rn, rn))
                V.scalar_tensor_tensor(C[:, 4 * q:4 * q + 4, :], C[:, 4 * q:4 * q + 4, :],
                                       DH ** -0.5 if q == 0 else 1.0, rn, ALU.mult, ALU.mult)\
                    .then_inc(st("qk_n"), 1)
            dve.wait_ge(st("gb_tok"), 1)
            dve.wait_ge(st("cum_mm"), 1)
            tokv = SMALL[:, 0:32].rearrange("p (c y j) -> p c y j", c=2, y=2)
            V.tensor_scalar(SMALL[:, 40:48], ps[:, 6, 32:40], -1.0, None, ALU.mult).then_inc(st("ncum"), 1)
            dve.wait_ge(st("ncum"), 1)
            beta = SMALL[:, 56:64]
            V.tensor_copy(beta.rearrange("p (c h) -> p c h", c=2), tokv[:, :, 1, 4:8])
            link(V.tensor_scalar(SMALL[:, 72:80].rearrange("p (c h) -> p c h", c=2), tokv[:, :, 1, 4:8], -1.0,
                                 None, ALU.mult))
            dve.wait_ge(st("brow"), 1)
            dve.wait_ge(st("ebl"), 1)
            for i in range(8):
                ins = V.tensor_scalar(DEC[:, i, :], psA[:, i, :], SMALL[:, 40 + i:41 + i], 0.0, ALU.add, ALU.min)
            ins.then_inc(st("dec_diff"), 1)
            dve.wait_ge(st("dec_exp"), 1)
            link(V.tensor_copy(SMALL[:, 80:88], DEC[:, :, P - 1]))
            V.tensor_tensor(AT[:, :, :], DEC[:, :, :], strict[:, :].unsqueeze(1).broadcast_to([P, 8, P]), ALU.mult)
            link(V.tensor_tensor(DEC[:, :, :], DEC[:, :, :], upper[:, :].unsqueeze(1).broadcast_to([P, 8, P]),
                                 ALU.mult))
            dve.wait_ge(st("kk_mm"), 1)
            for i in range(8):
                ins = V.scalar_tensor_tensor(AT[:, i, :], psA[:, i, :], SMALL[:, 72 + i:73 + i], AT[:, i, :],
                                             ALU.mult, ALU.mult)
            ins.then_inc(st("at"), 1)
            dve.wait_ge(st("kq_mm"), 1)
            V.tensor_tensor(DEC[:, :, :], DEC[:, :, :], psB, ALU.mult).then_inc(st("aqk"), 1)
            dve.wait_ge(st("qe_exp"), 1)
            V.tensor_tensor(QE[:, :, :], QE[:, :, :], C[:, 0:4, P:2 * P], ALU.mult).then_inc(st("qe"), 1)
            idb = ident[:, :].unsqueeze(1).broadcast_to([P, 8, P])

            def mask(m):
                return lvl[:, m, :].bitcast(U16).unsqueeze(1).broadcast_to([P, 8, P])
            V.tensor_copy(T[:, :, :], idb)
            link(V.tensor_copy(U[:, :, :], idb))
            dve.wait_ge(st("at"), 1)
            V.copy_predicated(U[:, :, :], mask(0), AT[:, :, :])
            dve.wait_ge(st("a_T"), 1)
            V.copy_predicated(T[:, :, :], mask(LEVELS), psA).then_inc(st("inv"), 1)
            for l in range(1, LEVELS):
                dve.wait_ge(st("inv_tu"), l)
                if l < LEVELS - 1:
                    V.copy_predicated(T[:, :, :], mask(LEVELS + l), psB)
                V.copy_predicated(U[:, :, :], mask(l), psA).then_inc(st("inv"), 1)
            dve.wait_ge(st("kt_T"), 1)
            V.tensor_tensor(KT[:, :, :], psA, SMALL[:, 80:88].unsqueeze(2).broadcast_to([P, 8, P]), ALU.mult)\
                .then_inc(st("kt"), 1)
            dve.wait_ge(st("vn0_mm"), 1)
            V.tensor_tensor(VN[:, 0:4, :], psB[:, 0:4, :], beta[:, 0:4].unsqueeze(2).broadcast_to([P, 4, P]), ALU.mult)\
                .then_inc(st("vn0"), 1)
            dve.wait_ge(st("ks_mm"), 1)
            dve.wait_ge(st("ebt"), 1)
            link(V.tensor_tensor(VN[:, 4:8, :], psB[:, 4:8, :],
                                 SMALL[:, 52:56].unsqueeze(2).broadcast_to([P, 4, P]), ALU.mult))
            V.tensor_tensor(VT[:, 4:8, :], VT[:, 4:8, :], VN[:, 4:8, :], ALU.subtract).then_inc(st("rhs1"), 1)
            dve.wait_ge(st("vn1_mm"), 1)
            V.tensor_tensor(VN[:, 4:8, :], psB[:, 0:4, :], beta[:, 4:8].unsqueeze(2).broadcast_to([P, 4, P]), ALU.mult)\
                .then_inc(st("vn1"), 1)
            dve.wait_ge(st("s2_mm"), 1)
            link(V.tensor_tensor(S2[:, :, :], S1[:, :, :], SMALL[:, 68:72].unsqueeze(2).broadcast_to([P, 4, P]),
                                 ALU.mult))
            V.tensor_tensor(S2[:, :, :], S2[:, :, :], psB[:, 4:8, :], ALU.add).then_inc(st("s2"), 1)
            dve.wait_ge(st("hg_in"), 1)
            V.memset(ATT[:, :, :], 0.0)
            V.tensor_scalar(SMALL[:, 224:256], SMALL[:, 224:256], DH ** -0.5, None, ALU.mult)
            V.tensor_scalar(QP[:, :, :], QP[:, :, :], DH ** -0.5, None, ALU.mult).then_inc(st("hg_q"), 1)
            flat = "p i t -> p (i t)"
            qp, ks = QP[:, :, :].rearrange(flat), KS[:, :, :].rearrange(flat)
            dve.wait_ge(st("hg_q"), 1)
            dve.wait_ge(st("hg_att"), 1)
            V.copy_predicated(ATT[:, :, :], mask(2 * LEVELS), psA).then_inc(st("hg_merge"), 1)
            g = GG[:, :, 0:PROMPT]
            V.tensor_tensor(qp.rearrange("p (h t) -> p h t", h=4), qp.rearrange("p (h t) -> p h t", h=4), g,
                            ALU.mult).then_inc(st("hg_lvl"), 1)
            off = 0
            tot = None
            for l in range(LEVELS):
                half = 1 << l
                dve.wait_ge(st("hg_att"), l + 2)
                dve.wait_ge(st("hg_lvl"), l + 1)
                n = 1024 // (2 * half)
                if l == 0:
                    gv = g.rearrange("p h (j two) -> p h j two", two=2)
                    left, right = gv[:, :, :, 0], gv[:, :, :, 1]
                    nxt = TOTS[:, 0:n].rearrange("p (h j) -> p h j", h=4)
                    q4 = qp.rearrange("p (h j two) -> p h j two", h=4, two=2)
                    k4 = ks.rearrange("p (h j two) -> p h j two", h=4, two=2)
                    V.tensor_tensor(q4[:, :, :, 1], q4[:, :, :, 1], left, ALU.mult)
                    V.tensor_tensor(k4[:, :, :, 0], k4[:, :, :, 0], right, ALU.mult)
                    V.tensor_tensor(nxt, left, right, ALU.mult).then_inc(st("hg_lvl"), 1)
                else:
                    tv = tot.rearrange("p (j two) -> p j two", two=2)
                    q4 = qp.rearrange("p (j two r) -> p j two r", two=2, r=half)
                    k4 = ks.rearrange("p (j two r) -> p j two r", two=2, r=half)
                    V.tensor_tensor(q4[:, :, 1, :], q4[:, :, 1, :],
                                    tv[:, :, 0].unsqueeze(2).broadcast_to([P, n, half]), ALU.mult)
                    V.tensor_tensor(k4[:, :, 0, :], k4[:, :, 0, :],
                                    tv[:, :, 1].unsqueeze(2).broadcast_to([P, n, half]), ALU.mult)
                    V.tensor_tensor(TOTS[:, off:off + n], tv[:, :, 0], tv[:, :, 1], ALU.mult)\
                        .then_inc(st("hg_lvl"), 1)
                tot = TOTS[:, off:off + n]
                off += n
                dve.wait_ge(st("hg_merge"), l + 1)
                V.copy_predicated(ATT[:, :, :], mask(l), psB if l % 2 == 0 else psA).then_inc(st("hg_merge"), 1)
            dve.wait_ge(st("hs2_mm"), 1)
            dve.wait_ge(st("s2_out"), 16)
            dve.wait_ge(st("hs1"), 1)
            totc = tot.rearrange("p (h c) -> p h c", h=4)[:, :, 1:2]
            link(V.tensor_tensor(S2[:, :, :], S1[:, :, :], totc.broadcast_to([P, 4, P]), ALU.mult))
            V.tensor_tensor(S2[:, :, :], S2[:, :, :], psA[:, 4:8, :], ALU.add).then_inc(st("hs2"), 1)
            rows = ROWS[0:8, :].rearrange("p (i n) -> p i n", n=P)
            dve.wait_ge(st("rows"), 1)
            dve.wait_ge(st("krows"), 1)
            dve.wait_ge(st("gs"), 1)
            dve.wait_ge(st("bs"), 1)
            diag = ident[0:8, 0:8].unsqueeze(2).broadcast_to([8, NSAMP, P])
            for j in range(8):
                h = j % 4
                Sv = SBUFS[:, j % 2]
                if j < 4:
                    vrow = rows[:, 4 + h, :]
                    decay = GG[:, h, PROMPT:TOK]
                else:
                    eg, bt = SMALL[:, 96 + 8 * h:104 + 8 * h], SMALL[:, 128 + 8 * h:136 + 8 * h]
                    decay = eg
                    w1, w2 = SMALL[:, 160:168], SMALL[:, 168:176]
                    dve.wait_ge(st("samp_ks"), h + 1)
                    link(V.tensor_tensor(w1, ps[:, 4, 0:8], eg, ALU.mult))
                    link(V.tensor_tensor(w2, C[:, 8 + h, PROMPT:TOK], w1, ALU.subtract))
                    V.tensor_tensor(w1, w2, bt, ALU.mult).then_inc(st("samp_vn"), 1)
                    dve.wait_ge(st("samp_vnT"), h + 1)
                    vrow = rows[:, h, :]
                    link(V.tensor_copy(vrow, ps[0:8, 5, 0:P]))
                if j:
                    dve.wait_ge(st("samp_outer"), j)
                V.tensor_tensor(VM[:, :, :], vrow.unsqueeze(1).broadcast_to([8, NSAMP, P]), diag, ALU.mult)\
                    .then_inc(st("samp_vm"), 1)
                dve.wait_ge(st(f"samp_in{j % 2}"), 16 * (j // 2 + 1))
                if j >= 4:
                    dve.wait_ge(st("samp_ks"), h + 1)
                link(V.tensor_tensor(Sv, Sv, decay.unsqueeze(2).broadcast_to([P, NSAMP, P]), ALU.mult))
                dve.wait_ge(st("samp_outer"), j + 1)
                V.tensor_tensor(Sv, Sv, psB, ALU.add).then_inc(st("samp_new"), 1)
                dve.wait_ge(st("samp_o_mm"), j + 1)
                V.tensor_copy(O[:, j, PROMPT:TOK], ps[:, 4, 16:24]).then_inc(st("samp_o"), 1)
            gate = [PT[:, 12 + h, :] for h in range(4)] + [PT[:, 28 + h, :] for h in range(4)]
            dve.wait_ge(st("gates"), 1)
            dve.wait_ge(st("samp_o"), 8)
            for k in range(KD):
                wn = par[:, C_HGN:C_HGN + 1] if k < 4 else par[:, C_GDN:C_GDN + 1]
                dve.wait_ge(st("o_root"), k + 1)
                tmp = PT[:, 16 + k, :]
                link(V.reciprocal(tmp, tmp))
                link(V.scalar_tensor_tensor(tmp, O[:, k, :], wn, tmp, ALU.mult, ALU.mult))
                V.tensor_tensor(O[:, k, :], tmp, gate[k], ALU.mult).then_inc(st("o_norm"), 1)
            for k in range(KD):
                dve.wait_ge(st("o_norm"), k + 1)
                dve.wait_ge(st("o_hi"), k + 1)
                V.tensor_tensor(x_lo[:, k, :], O[:, k, :], x_hi[:, k, :].bitcast(F32), ALU.subtract)\
                    .then_inc(st("o_lo"), 1)
            for q in range(8):
                tick(S_WOUT + q)
            residual(1.0, lambda d: (used, S_WOUT + 2 * (d // 2) + 2))
            norm(2)

        def odd_vector(dve, tick, link, residual, norm):
            V = nc.vector
            W = PAD + TOK
            up = PTf[:, 0:KD * W].rearrange("p (k t) -> p k t", k=KD)
            wa = PTf[:, KD * W:2 * KD * W].rearrange("p (k t) -> p k t", k=KD)
            wb = PTf[:, 2 * KD * W:3 * KD * W].rearrange("p (k t) -> p k t", k=KD)
            cnt = SMALL[:, 0:64].rearrange("p (g t) -> p g t", g=4)
            dve.wait_ge(x_done, 8 * 5)
            V.memset(up[:, :, 0:PAD], 0.0).then_inc(st("pad_zero"), 1)
            for gi, w in enumerate(WINDOWS):
                link(V.memset(cnt[:, gi, :], 1.0 / w))
                for t in range(w - 1):
                    ins = V.memset(cnt[:, gi, t:t + 1], 1.0 / (t + 1))
                link(ins)
            for q in range(8):
                tick(S_PIN + q)
            dve.wait_ge(st("pool_u"), 4)
            src, dst = up, wa
            end = PAD + PROMPT
            for gi, w in enumerate(WINDOWS):
                lo, back = w - 1, w // 2
                link(V.tensor_tensor(dst[:, 2 * gi:, lo:end], src[:, 2 * gi:, lo:end],
                                     src[:, 2 * gi:, lo - back:end - back], ALU.add))
                win = dst[:, 2 * gi:2 * gi + 2, PAD:PAD + PROMPT]
                u = up[:, 2 * gi:2 * gi + 2, PAD:PAD + PROMPT]
                out = hn[:, 2 * gi:2 * gi + 2, :]
                V.scalar_tensor_tensor(out[:, :, 16:PROMPT], win[:, :, 16:], 1.0 / w, u[:, :, 16:], ALU.mult,
                                       ALU.subtract)
                link(V.tensor_tensor(out[:, :, 0:16], win[:, :, 0:16],
                                     cnt[:, gi, :].unsqueeze(1).broadcast_to([P, 2, 16]), ALU.mult))
                V.tensor_tensor(out[:, :, 0:16], out[:, :, 0:16], u[:, :, 0:16], ALU.subtract)
                if gi == 0:
                    dve.wait_ge(st("pool_hist"), 1)
                us = up[:, 2 * gi:2 * gi + 2, PAD + PROMPT:]
                hs = ps[:, 1, 16 * gi:16 * gi + 16].rearrange("p (k b) -> p k b", k=2)
                tmp = SMALL[:, 64 + 16 * gi:80 + 16 * gi].rearrange("p (k b) -> p k b", k=2)
                link(V.tensor_tensor(tmp, hs, us, ALU.add))
                V.scalar_tensor_tensor(out[:, :, PROMPT:TOK], tmp, 1.0 / w, us, ALU.mult, ALU.subtract)\
                    .then_inc(st("pool_d"), 2)
                src, dst = dst, (wb if dst is wa else wa)
            dve.wait_ge(st("pool_d"), 8)
            for k in range(KD):
                dve.wait_ge(st("pool_hi"), k + 1)
                V.tensor_tensor(x_lo[:, k, :], hn[:, k, :], x_hi[:, k, :].bitcast(F32), ALU.subtract)\
                    .then_inc(st("pool_lo"), 1)
            tick(S_PGRP)
            tick(S_PGRP + 1)
            residual(par[:, C_SCALE:C_SCALE + 8], lambda d: (used, S_PGRP + d // 4 + 1))
            norm(5)

        @block.vector
        def _(dve):
            chain = [0]

            def link(ins):
                chain[0] += 1
                ins.then_inc(dve_chain, 1)
                dve.wait_ge(dve_chain, chain[0])

            def tick(s, i=None):
                w = s + LEAD
                if w >= TOTAL:
                    return
                dve.wait_ge(hi_done, v(w + 1, i, 8))
                nc.vector.tensor_tensor(w_lo[:, w % SPL, :], raw[:, w % RAW, :],
                                        w_hi[:, w % SPL, :].bitcast(F32), ALU.subtract).then_inc(lo_done, 1)

            def lo_h(n, k):
                dve.wait_ge(xhi_done, 8 * n + k + 1)
                nc.vector.tensor_tensor(x_lo[:, k, :], hn[:, k, :], x_hi[:, k, :].bitcast(F32), ALU.subtract)\
                    .then_inc(xlo_done, 1)

            def residual(scale, ended):
                for d in range(KD):
                    dve.wait_ge(*ended(d))
                    sc = scale if isinstance(scale, float) else scale[:, d:d + 1]
                    nc.vector.scalar_tensor_tensor(x[:, d, :], ps[:, d, 0:TOK], sc, x[:, d, :], ALU.mult, ALU.add)\
                        .then_inc(x_done, 1)

            def norm(n):
                dve.wait_ge(root_done, n + 1)
                nc.vector.reciprocal(rstd[:, :], rstd[:, :]).then_inc(rstd_done, 1)
                dve.wait_ge(rstd_done, n + 1)
                for k in range(KD):
                    nc.vector.scalar_tensor_tensor(hn[:, k, :], x[:, k, :], par[:, 8 * n + k:8 * n + k + 1],
                                                   rstd[:, :], ALU.mult, ALU.mult).then_inc(hn_done, 1)
                    if k and n < 6:
                        lo_h(n, k - 1)
                if n < 6:
                    lo_h(n, KD - 1)

            def ffn(n):
                s0, b0 = S_FFN[n], NB * n

                def prod(b, i=None):
                    dve.wait_ge(silu_done, v(b + 1, i, 2))
                    dve.wait_ge(used, v(s0 + 4 * (b - b0) + 4, i, 8))
                    st4 = 4 * ((b - b0) % 2) + 2
                    nc.vector.tensor_tensor(pr[:, :, :], sg[:, :, :], ps[:, st4:st4 + 2, 0:TOK], ALU.mult)\
                        .then_inc(prod_done, 1)

                def lo_a(b, i=None):
                    dve.wait_ge(ahi_done, v(b + 1, i, 2))
                    f = 2 * (b - b0) if i is None else i * 4 + 2 * (b - b0)
                    nc.vector.tensor_tensor(a_lo[:, bass.ds(f, 2), :], pr[:, :, :],
                                            a_hi[:, bass.ds(f, 2), :].bitcast(F32), ALU.subtract)\
                        .then_inc(alo_done, 1)

                def blk(b, i=None):
                    s = s0 + 4 * (b - b0)
                    if b > b0:
                        prod(b - 1, i)
                    tick(s, i)
                    tick(s + 1, i)
                    if b > b0:
                        lo_a(b - 1, i)
                    tick(s + 2, i)
                    tick(s + 3, i)
                    if b > b0:
                        dve.wait_ge(alo_done, v(b, i, 2))

                blk(b0)
                with dve.Fori(0, NB // 2) as i:
                    blk(b0 + 1, i)
                    blk(b0 + 2, i)
                s1 = s0 + 4 * NB
                prod(b0 + NB - 1)
                tick(s1)
                lo_a(b0 + NB - 1)
                for f in range(1, 5):
                    tick(s1 + f)
                dve.wait_ge(alo_done, b0 + NB)
                with dve.Fori(0, 2 if n < 3 else 1) as i:
                    for f in range(5, 13):
                        tick(s1 + f, i)
                for f in range(13, KF - 1 if n == 3 else 13):
                    tick(s1 + f)
                residual(0.5, lambda d: (res_done, 8 * n + d + 1))
                norm(FFN_NORM[n] + 1)
                tick(s1 + KF - 1)

            nc.vector.memset(mean_w[:, :], 1.0 / D)
            nc.vector.memset(eps[:, :], EPS)
            nc.vector.memset(ones[:, :], 1.0).then_inc(const_done, 1)
            dve.wait_ge(x_T, 2)
            for d in range(KD):
                nc.vector.tensor_copy(x[:, d, :], ps[:, d, 0:TOK]).then_inc(x_done, 1)
            dve.wait_ge(st("par_ok"), 1)
            for s in range(-LEAD, 0):
                tick(s)
            norm(0)
            ffn(0)
            even_vector(dve, tick, link, residual, norm)
            mixer_space_free(dve)
            ffn(1)
            ffn(2)
            odd_vector(dve, tick, link, residual, norm)
            dve.wait_ge(st("stored"), 16 * 5)
            ffn(3)

        def even_tensor(pe, mm, three, blk_slot, norm):
            tr = nc.tensor.transpose
            nwait = (lambda k: (xlo_done, 8 * 1 + k + 1))
            for n in range(16):
                if n >= 2:
                    pe.wait_ge(p_ready, n - 1)
                for half in range(2):
                    blk_slot(S_PROJ + 2 * n + half, half, 2 * (n % 2), None, nwait if n == 0 else None)
            pe.wait_ge(st("wab_in"), 16)
            pe.wait_ge(st("masks_ok"), 1)
            for k in range(KD):
                ins = mm(ps[0:8, 7, 0:TOK], WAB[:, k, :], hn[:, k, :], start=k == 0, stop=k == KD - 1)
            ins.then_inc(st("gb_mm"), 1)
            pe.wait_ge(st("hist_in"), 16)
            for c in range(CT):
                ins = tr(ps[:, 6, c * 24:(c + 1) * 24], ROWS2[0:24, c * P:(c + 1) * P], ident[0:24, 0:24])
            ins.then_inc(st("conv_hist_T"), 1)
            pe.wait_ge(p_ready, 16)
            pe.wait_ge(st("conv_hist"), 1)
            for c in range(CT):
                ins = tr(ps[0:11, 4 + c // 4, c % 4 * P:(c % 4 + 1) * P], PT[:, 16 + c, PROMPT - 3:TOK], ident[:, :])
            ins.then_inc(st("crow_T"), 1)
            pe.wait_ge(st("crow"), 1)
            pe.wait_ge(st("gb_ln2"), 1)
            for q in range(2):
                pe.wait_ge(st("qk_sq"), q + 1)
                for h in range(4):
                    ins = mm(ps[:, 4 * q + h, 0:TOK], ones[:, :], PT[:, 16 + 4 * q + h, :], start=True, stop=True)
                ins.then_inc(st("qk_ss"), 1)
            pe.wait_ge(st("beta"), 1)
            pe.wait_ge(st("qk_n"), 2)
            for c in range(2):
                for y, row in ((0, 5), (1, 6)):
                    ins = tr(ps[:, 6, 16 * c + 8 * y:16 * c + 8 * y + 8], GB[:, row, c * P:(c + 1) * P], ident[0:8, 0:8])
            ins.then_inc(st("tok_T"), 1)
            pe.wait_ge(st("gb_tok"), 1)
            gt = SMALL[:, 0:32].rearrange("p (c y j) -> p c y j", c=2, y=2)
            mm(ps[:, 6, 32:40].rearrange("p (c h) -> p c h", c=2), upper[:, :], gt[:, :, 0, 0:4], start=True,
               stop=True).then_inc(st("cum_mm"), 1)
            for c in range(2):
                for h in range(4):
                    ins = mm(psA[:, 4 * c + h, :], gt[:, c, 0, h:h + 1].broadcast_to([P, P]), upper[:, :],
                             start=True, stop=True)
            ins.then_inc(st("brow"), 1)
            pe.wait_ge(st("dec_diff"), 1)
            pe.wait_ge(st("qe_exp"), 1)
            for j in range(8):
                row = 5 if j < 4 else 6
                ins = mm(ps[:, 5, 8 * j:8 * j + 8], ident[0:8, j:j + 1].broadcast_to([8, P]),
                         GB[:, row, PROMPT:TOK], start=True, stop=True)
            ins.then_inc(st("gb_rows_mm"), 1)
            pe.wait_ge(st("bs"), 1)
            pe.wait_ge(st("gs"), 1)
            pe.wait_ge(st("ncum"), 1)
            ch = [(c, h) for c in range(2) for h in range(4)]
            for i, (c, h) in enumerate(ch):
                kk = C[:, 4 + h, c * P:(c + 1) * P]
                ins = mm(psA[:, i, :], kk, kk, start=True, stop=True)
            ins.then_inc(st("kk_mm"), 1)
            for i, (c, h) in enumerate(ch):
                ins = mm(psB[:, i, :], C[:, 4 + h, c * P:(c + 1) * P], C[:, h, c * P:(c + 1) * P], start=True,
                         stop=True)
            ins.then_inc(st("kq_mm"), 1)
            pe.wait_ge(st("at"), 1)
            for i in range(8):
                ins = tr(psA[:, i, :], AT[:, i, :], ident[:, :])
            ins.then_inc(st("a_T"), 1)
            pe.wait_ge(st("aqk"), 1)
            for l in range(1, LEVELS):
                pe.wait_ge(st("inv"), l)
                for i in range(8):
                    ins = mm(psA[:, i, :], AT[:, i, :], T[:, i, :], start=True, stop=True)
                ins.then_inc(st("inv_x"), 1)
                pe.wait_ge(st("inv_xc"), l)
                if l < LEVELS - 1:
                    for i in range(8):
                        mm(psB[:, i, :], U[:, i, :], X[:, i, :], start=True, stop=True)
                for i in range(8):
                    ins = mm(psA[:, i, :], X[:, i, :], U[:, i, :], start=True, stop=True)
                ins.then_inc(st("inv_tu"), 1)
            for i, (c, h) in enumerate(ch):
                ins = tr(psB[:, i, :], C[:, 8 + h, c * P:(c + 1) * P], ident[:, :])
            ins.then_inc(st("vt_T"), 1)
            pe.wait_ge(st("inv"), LEVELS)
            for i, (c, h) in enumerate(ch):
                ins = tr(psA[:, i, :], C[:, 4 + h, c * P:(c + 1) * P], ident[:, :])
            ins.then_inc(st("kt_T"), 1)
            pe.wait_ge(st("vt"), 1)
            for h in range(4):
                ins = mm(psB[:, h, :], U[:, h, :], VT[:, h, :], start=True, stop=True)
            ins.then_inc(st("vn0_mm"), 1)
            pe.wait_ge(st("kt"), 1)
            pe.wait_ge(st("vn0"), 1)
            for h in range(4):
                ins = mm(psA[:, h, :], KT[:, h, :], VN[:, h, :], start=True, stop=True)
            ins.then_inc(st("s1_mm"), 1)
            pe.wait_ge(st("s1"), 1)
            for h in range(4):
                ins = mm(psB[:, 4 + h, :], C[:, 4 + h, P:2 * P], S1[:, h, :], start=True, stop=True)
            ins.then_inc(st("ks_mm"), 1)
            pe.wait_ge(st("rhs1"), 1)
            for h in range(4):
                ins = mm(psB[:, h, :], U[:, 4 + h, :], VT[:, 4 + h, :], start=True, stop=True)
            ins.then_inc(st("vn1_mm"), 1)
            pe.wait_ge(st("vn1"), 1)
            for h in range(4):
                ins = mm(psB[:, 4 + h, :], KT[:, 4 + h, :], VN[:, 4 + h, :], start=True, stop=True)
            ins.then_inc(st("s2_mm"), 1)
            pe.wait_ge(st("qe"), 1)
            for h in range(4):
                mm(psA[:, h, :], VN[:, h, :], DEC[:, h, :], start=True, stop=True)
            for h in range(4):
                mm(psA[:, 4 + h, :], S1[:, h, :], QE[:, h, :], start=True, stop=False)
                ins = mm(psA[:, 4 + h, :], VN[:, 4 + h, :], DEC[:, 4 + h, :], start=False, stop=True)
            ins.then_inc(st("o_mm"), 1)
            hc = [(h, c) for h in range(4) for c in range(2)]
            pe.wait_ge(st("hg_q"), 1)
            pe.wait_ge(st("o_b"), 2)
            pe.wait_ge(st("s2"), 1)
            for i in range(8):
                ins = mm(psA[:, i, :], KS[:, i, :], QP[:, i, :], start=True, stop=True)
            ins.then_inc(st("hg_att"), 1)
            for l in range(LEVELS):
                pe.wait_ge(st("hg_lvl"), l + 1)
                if l:
                    pe.wait_ge(st("hg_merge"), l)
                out = psB if l % 2 == 0 else psA
                for i in range(8):
                    ins = mm(out[:, i, :], KS[:, i, :], QP[:, i, :], start=True, stop=True)
                ins.then_inc(st("hg_att"), 1)
            pe.wait_ge(st("hg_merge"), LEVELS + 1)
            for i, (h, c) in enumerate(hc):
                ins = tr(psA[:, i, :], PT[:, 8 + h, c * P:(c + 1) * P], ident[:, :])
            ins.then_inc(st("hvt_T"), 1)
            pe.wait_ge(st("hg_lvl"), LEVELS + 1)
            for i in range(8):
                ins = tr(psB[:, i, :], KS[:, i, :], ident[:, :])
            ins.then_inc(st("hkt_T"), 1)
            pe.wait_ge(st("hvt"), 1)
            pe.wait_ge(st("hkt"), 1)
            for h in range(4):
                ins = mm(psA[:, h, :], KT[:, 2 * h, :], VT[:, 2 * h, :], start=True, stop=True)
            ins.then_inc(st("hs1_mm"), 1)
            for h in range(4):
                ins = mm(psA[:, 4 + h, :], KT[:, 2 * h + 1, :], VT[:, 2 * h + 1, :], start=True, stop=True)
            ins.then_inc(st("hs2_mm"), 1)
            pe.wait_ge(st("hs1"), 1)
            pe.wait_ge(st("hs2"), 1)
            for h in range(4):
                mm(psA[:, 2 * h, :], VT[:, 2 * h, :], ATT[:, 2 * h, :], start=True, stop=True)
                mm(psA[:, 2 * h + 1, :], S1[:, h, :], QP[:, 2 * h + 1, :], start=True, stop=False)
                ins = mm(psA[:, 2 * h + 1, :], VT[:, 2 * h + 1, :], ATT[:, 2 * h + 1, :], start=False, stop=True)
            ins.then_inc(st("ho_mm"), 1)
            pe.wait_ge(st("o_a"), 1)
            for h in range(4):
                tr(psA[0:8, h, :], SMALL[:, 192 + 8 * h:200 + 8 * h], ident[:, :])
                ins = tr(psA[0:8, 4 + h, :], PT[:, 8 + h, PROMPT:TOK], ident[:, :])
            ins.then_inc(st("rows_T"), 1)
            pe.wait_ge(st("rows"), 1)
            for h in range(4):
                ins = tr(psA[0:8, h, :], C[:, 4 + h, PROMPT:TOK], ident[:, :])
            ins.then_inc(st("krows_T"), 1)
            pe.wait_ge(st("krows"), 1)
            rows = ROWS[0:8, :].rearrange("p (i n) -> p i n", n=P)
            for j in range(8):
                h = j % 4
                Sv = SBUFS[:, j % 2]
                if j >= 4:
                    pe.wait_ge(st(f"samp_in{j % 2}"), 16 * (j // 2 + 1))
                    pe.wait_ge(st("samp_o"), j)
                    for b in range(NSAMP):
                        ins = mm(ps[:, 4, b:b + 1], Sv[:, b, :], C[:, 4 + h, PROMPT + b:PROMPT + b + 1], start=True,
                                 stop=True)
                    ins.then_inc(st("samp_ks"), 1)
                    pe.wait_ge(st("samp_vn"), h + 1)
                    tr(ps[0:8, 5, 0:P], SMALL[:, 160:168], ident[:, :]).then_inc(st("samp_vnT"), 1)
                pe.wait_ge(st("samp_vm"), j + 1)
                if j:
                    pe.wait_ge(st("samp_new"), j)
                krow = rows[:, h, :] if j < 4 else rows[:, 8 + h, :]
                vm = VM[:, :, :].rearrange("p b n -> p (b n)")
                for y in range(2):
                    ins = mm(ps[:, 6 + y, :], krow, vm[:, 512 * y:512 * (y + 1)], start=True, stop=True)
                ins.then_inc(st("samp_outer"), 1)
                pe.wait_ge(st("samp_new"), j + 1)
                if j:
                    pe.wait_ge(st("samp_o"), j)
                for b in range(NSAMP):
                    q = SMALL[:, 224 + 8 * h + b:225 + 8 * h + b] if j < 4 else C[:, h, PROMPT + b:PROMPT + b + 1]
                    ins = mm(ps[:, 4, 16 + b:17 + b], Sv[:, b, :], q, start=True, stop=True)
                ins.then_inc(st("samp_o_mm"), 1)
            pe.wait_ge(st("samp_o"), 8)
            for d in range(KD):
                pe.wait_ge(st("o_sq"), d + 1)
                mm(ps[:, d, 0:TOK], HM[:, :], hn[:, d, :], start=True, stop=True).then_inc(st("o_ss"), 1)
            pe.wait_ge(st("o_norm"), 8)
            for n in range(4):
                for half in range(2):
                    s = S_WOUT + 2 * n + half
                    pe.wait_ge(lo_done, s + 1)
                    for k4 in range(4):
                        k = 4 * half + k4
                        if n == 0:
                            pe.wait_ge(st("o_lo"), k + 1)
                        for j in range(2):
                            ins = three(ps[:, 2 * n + j, 0:TOK], s, k4 * BLK + j * P, x_hi[:, k, :], x_lo[:, k, :],
                                        k == 0, k == KD - 1)
                    ins.then_inc(used, 1)
            norm(2)

        def odd_tensor(pe, mm, three, blk_slot, norm):
            tr = nc.tensor.transpose
            W = PAD + TOK
            up = PTf[:, 0:KD * W].rearrange("p (k t) -> p k t", k=KD)
            for n in range(4):
                for half in range(2):
                    kw = (lambda k: (xlo_done, 8 * 4 + k + 1)) if n == 0 else None
                    blk_slot(S_PIN + 2 * n + half, half, 2 * n, None, kw)
            pe.wait_ge(st("pool_u"), 4)
            pe.wait_ge(st("pbuf_in"), 16)
            pe.wait_ge(st("sel_ok"), 1)
            for d in range(KD):
                ins = mm(ps[:, 1, 8 * d:8 * d + 8], PBUFR[0:120, d * P:(d + 1) * P], SEL[0:120, d // 2, :],
                         start=True, stop=True)
            ins.then_inc(st("pool_hist"), 1)
            for d in range(KD):
                ins = tr(ps[0:23, 4 + d // 4, d % 4 * P:(d % 4 + 1) * P], up[:, d, PAD + PROMPT - PBUF:PAD + TOK],
                         ident[:, :])
            ins.then_inc(st("prow_T"), 1)
            pe.wait_ge(st("pool_d"), 8)
            pe.wait_ge(st("prow"), 1)
            for q in range(2):
                pe.wait_ge(lo_done, S_PGRP + q + 1)
                for g2 in range(2):
                    g = 2 * q + g2
                    for j in range(2):
                        for kk in range(2):
                            pe.wait_ge(st("pool_lo"), 2 * g + kk + 1)
                            ins = three(ps[:, 2 * g + j, 0:TOK], S_PGRP + q, (2 * g2 + kk) * BLK + j * P,
                                        x_hi[:, 2 * g + kk, :], x_lo[:, 2 * g + kk, :], kk == 0, kk == 1)
                ins.then_inc(used, 1)
            norm(5)

        @block.tensor
        def _(pe):
            mm = nc.tensor.matmul

            def three(out, s, c0, hi, lo, first, last):
                wh = w_hi[:, s % SPL, c0:c0 + P]
                wl = w_lo[:, s % SPL, c0:c0 + P]
                mm(out, wh, hi, start=first, stop=False)
                mm(out, wh, lo, start=False, stop=False)
                return mm(out, wl, hi, start=False, stop=last)

            def blk_slot(s, half, banks, i=None, k_wait=None):
                pe.wait_ge(lo_done, v(s + 1, i, 8))
                for k4 in range(4):
                    k = 4 * half + k4
                    if k_wait:
                        pe.wait_ge(*k_wait(k))
                    for j in range(2):
                        ins = three(ps[:, banks + j, 0:TOK], s, k4 * BLK + j * P, x_hi[:, k, :], x_lo[:, k, :],
                                    k == 0, k == KD - 1)
                ins.then_inc(used, 1)
                return ins

            def norm(n, frees_slot=False):
                for d in range(KD):
                    pe.wait_ge(sq_done, 8 * n + d + 1)
                    ins = mm(ps[:, 0, 0:TOK], mean_w[:, :], hn[:, d, :], start=d == 0, stop=d == KD - 1)
                    if d == 0 and frees_slot:
                        ins.then_inc(used, 1)
                ins.then_inc(ss_done, 1)

            def ffn(n):
                s0, b0, nn = S_FFN[n], NB * n, FFN_NORM[n]

                def blk(b, i=None):
                    s = s0 + 4 * (b - b0)
                    banks = 4 * ((b - b0) % 2)
                    for q in range(4):
                        if b and q == 0:
                            pe.wait_ge(silu_done, v(b, i, 2))
                        if b and q == 2:
                            pe.wait_ge(prod_done, v(b, i, 2))
                        kw = (lambda k: (xlo_done, 8 * nn + k + 1)) if (b == b0 and q < 2) else None
                        blk_slot(s + q, q % 2, banks + 2 * (q // 2), i, kw)

                blk(b0)
                with pe.Fori(0, NB // 2) as i:
                    blk(b0 + 1, i)
                    blk(b0 + 2, i)
                s1 = s0 + 4 * NB

                def down(f, ds, i=None):
                    hi, lo = (a_hi[:, f, :], a_lo[:, f, :]) if i is None else \
                        [a[:, bass.ds(i * 8 + f, 1), :].rearrange("p a t -> p (a t)") for a in (a_hi, a_lo)]
                    for d in ds:
                        ins = three(ps[:, d, 0:TOK], s1 + f, d * P, hi, lo, f == 0, f == KF - 1)
                    return ins

                pe.wait_ge(lo_done, s1 + 2)
                pe.wait_ge(alo_done, b0 + NB - 1)
                down(0, range(4, 8))
                down(1, range(4, 8))
                pe.wait_ge(prod_done, b0 + NB)
                down(0, range(4)).then_inc(used, 1)
                down(1, range(4)).then_inc(used, 1)
                with pe.Fori(0, 2) as i:
                    for f in range(2, 10):
                        pe.wait_ge(lo_done, v(s1 + f + 1, i, 8))
                        down(f, range(8), i).then_inc(used, 1)
                for f in range(18, KF - 2):
                    pe.wait_ge(lo_done, s1 + f + 1)
                    down(f, range(8)).then_inc(used, 1)
                pe.wait_ge(lo_done, s1 + KF)
                pe.wait_ge(alo_done, b0 + NB)
                for d in range(KD):
                    ins = down(KF - 2, [d])
                    if d == KD - 1:
                        ins.then_inc(used, 1)
                    down(KF - 1, [d]).then_inc(res_done, 1)
                norm(nn + 1, frees_slot=True)

            pe.wait_ge(st("ident_ok"), 1)
            pe.wait_ge(par_in, 16 * 11)
            nc.tensor.transpose(ps[:, 0, 0:NPAR], X[0:NPAR, 0, :], ident[0:NPAR, 0:NPAR]).then_inc(x_T, 1)
            pe.wait_ge(x_in, 48)
            pe.wait_ge(st("par_ok"), 1)
            for d in range(KD):
                for c in range(3):
                    n = P if c < CH else NSAMP
                    ins = nc.tensor.transpose(ps[:, d, c * P:c * P + n], PTf[0:n, c * D + d * P:c * D + (d + 1) * P],
                                              ident[0:n, 0:n])
            ins.then_inc(x_T, 1)
            pe.wait_ge(const_done, 1)
            norm(0)
            ffn(0)
            even_tensor(pe, mm, three, blk_slot, norm)
            ffn(1)
            ffn(2)
            odd_tensor(pe, mm, three, blk_slot, norm)
            ffn(3)
            pe.wait_ge(hn_done, 8 * 7)
            for c in range(3):
                n = P if c < CH else NSAMP
                for d in range(KD):
                    b = (0, 2, 4)[c] + d // 4
                    ins = nc.tensor.transpose(ps[0:n, b, d % 4 * P:(d % 4 + 1) * P], hn[:, d, c * P:c * P + n],
                                              ident[:, :])
                ins.then_inc(st("y_T"), 1)

        @block.gpsimd
        def _(pool):
            G = nc.gpsimd
            n_chain = [0]

            def link(ins):
                n_chain[0] += 1
                ins.then_inc(pool_chain, 1)
                pool.wait_ge(pool_chain, n_chain[0])

            prow = X[:, 0, :]
            rows = [(n_ffn1[0], 0), (n_mix[0], 1), (n_ffn2[0], 2), (n_ffn1[1], 3), (n_mix[1], 4), (n_ffn2[1], 5),
                    (n_fin, 6), (pool_scale[0], 7)]
            for src, r in rows:
                pool.dma_start(prow[8 * r:8 * r + 8, :], src.rearrange("(k p) -> k p", p=P)).then_inc(par_in, 16)
            pool.dma_start(prow[C_CONV:C_HGN, :], conv_w[0].rearrange("j (c p) -> (j c) p", p=P)).then_inc(par_in, 16)
            pool.dma_start(prow[C_HGN:C_HGN + 1, :], hgn).then_inc(par_in, 16)
            pool.dma_start(prow[C_GDN:C_GDN + 1, :], gdn_n).then_inc(par_in, 16)
            for c in range(2):
                pool.dma_start(PTf[:, c * D:(c + 1) * D], x_prompt[0, c * P:(c + 1) * P, :]).then_inc(x_in, 16)
            pool.dma_start(PTf[0:NSAMP, 2 * D:3 * D], x_sample[:, 0, :]).then_inc(x_in, 16)
            link(G.memset(ident[:, :], 0.0))
            G.affine_select(out=ident[:, :], in_=ident[:, :], compare_op=ALU.not_equal, fill=1.0, base=0,
                            pattern=[[-1, P]], channel_multiplier=1).then_inc(st("ident_ok"), 1)
            link(G.memset(ab8[:, :], 0.0))
            pool.dma_start(ab8[0:4, 0:1], dt_bias.rearrange("a h -> h a")).then_inc(st("ab_in"), 16)
            pool.dma_start(ab8[0:4, 1:2], a_log.rearrange("a h -> h a")).then_inc(st("ab_in"), 16)
            pool.dma_start(WAB[:, :, :], w_in[0, :, 4096:4104].rearrange("(k p) n -> p k n", p=P))\
                .then_inc(st("wab_in"), 16)
            G.memset(upper[:, :], 1.0)
            link(G.memset(strict[:, :], 1.0))
            G.affine_select(out=upper[:, :], in_=upper[:, :], compare_op=ALU.is_ge, fill=0.0, base=0,
                            pattern=[[1, P]], channel_multiplier=-1)
            G.affine_select(out=strict[:, :], in_=strict[:, :], compare_op=ALU.is_gt, fill=0.0, base=0,
                            pattern=[[1, P]], channel_multiplier=-1)
            G.memset(lvl[:, 0:2 * LEVELS, :], 0.0)
            link(G.tensor_copy(lvl[:, 2 * LEVELS, :], ident[:, :]))
            for l in range(LEVELS):
                h = 1 << l
                pat = [[-2 * h, P // (2 * h)], [0, h]]
                neg = [[2 * h, P // (2 * h)], [0, h]]
                for m, side, lo, hi in ((l, 1, 0, h - 1), (LEVELS + l, 0, h, 2 * h - 1)):
                    part = lvl[:, m, :].rearrange("p (j two r) -> p j two r", two=2, r=h)[:, :, side, :]
                    link(G.memset(part, 1.0))
                    link(G.affine_select(out=part, in_=part, compare_op=ALU.is_ge, fill=0.0, base=-lo,
                                         pattern=pat, channel_multiplier=1))
                    link(G.affine_select(out=part, in_=part, compare_op=ALU.is_ge, fill=0.0, base=hi,
                                         pattern=neg, channel_multiplier=-1))
            ins = G.memset(HM[:, :], 1.0 / DH)
            ins.then_inc(st("masks_ok"), 1)
            link(G.memset(SEL[:, :, :], 1.0))
            for gi, w in enumerate(WINDOWS):
                link(G.affine_select(out=SEL[:, gi, :], in_=SEL[:, gi, :], compare_op=ALU.is_ge, fill=0.0,
                                     base=-(PBUF - (w - 1)), pattern=[[-PBUF, NSAMP]], channel_multiplier=1))
                ins = G.affine_select(out=SEL[:, gi, :], in_=SEL[:, gi, :], compare_op=ALU.is_ge, fill=0.0,
                                      base=PBUF - 1, pattern=[[PBUF, NSAMP]], channel_multiplier=-1)
            ins.then_inc(st("sel_ok"), 1)
            outs = [0]

            def store(dst, src):
                outs[0] += 16
                pool.dma_start(dst, src).then_inc(st("stored"), 16)

            store(conv_s[0, :, 0:CONV - 2, :], state_conv[0, :, 1:CONV - 1, :])
            store(pool_s[0, :, 0:PBUF - 1, :], state_pool[0, :, 1:PBUF, :])
            pool.wait_ge(x_done, 8 * 2)
            pool.dma_start(ROWS2[0:24, 0:CT * P], state_conv[0].rearrange("b r n -> (b r) n")).then_inc(st("hist_in"), 16)

            def load_state(j):
                src = (state_hgrn if j < 4 else state_gdn)[0, :, j % 4]
                pool.dma_start(SBUFS[:, j % 2], src.rearrange("b k v -> k b v")).then_inc(st(f"samp_in{j % 2}"), 16)

            load_state(0)
            load_state(1)
            pool.wait_ge(st("crow"), 1)
            pool.dma_start(conv_p[0, 0], ROWS[0:3, :]).then_inc(st("conv_rows_out"), 16)
            pool.dma_start(conv_s[0, :, CONV - 2, :], ROWS[3:11, :]).then_inc(st("conv_rows_out"), 16)
            pool.wait_ge(st("s2"), 1)
            pool.dma_start(gdn_p[0, 0].rearrange("h k v -> k h v"), S2[:, :, :]).then_inc(st("s2_out"), 16)
            pool.wait_ge(st("hs2"), 1)
            store(hg_p[0, 0].rearrange("h k v -> k h v"), S2[:, :, :])
            for j in range(8):
                pool.wait_ge(st("samp_new"), j + 1)
                dst = (hg_s if j < 4 else gdn_s)[0, :, j % 4]
                pool.dma_start(dst.rearrange("b k v -> k b v"), SBUFS[:, j % 2]).then_inc(st(f"samp_out{j % 2}"), 16)
                if j + 2 < 8:
                    pool.wait_ge(st(f"samp_out{j % 2}"), 16 * (j // 2 + 1))
                    pool.wait_ge(st("samp_o_mm"), j + 1)
                    load_state(j + 2)
            for r in range(2):
                pool.wait_ge(st(f"samp_out{r}"), 64)
            pool.wait_ge(st("conv_rows_out"), 32)
            pool.wait_ge(st("s2_out"), 16)
            pool.wait_ge(x_done, 8 * 5)
            pool.dma_start(PBUFR[0:NSAMP * PBUF, 0:D], state_pool[0].rearrange("b r n -> (b r) n"))\
                .then_inc(st("pbuf_in"), 16)
            pool.wait_ge(st("prow"), 1)
            prows = C[:, 0:4, 0:256]
            store(pool_p[0, 0].rearrange("t (a n) -> t a n", a=4), prows[0:PBUF])
            store(pool_s[0, :, PBUF - 1, :].rearrange("t (a n) -> t a n", a=4), prows[PBUF:PBUF + NSAMP])
            pool.wait_ge(st("stored"), outs[0])
            for c in range(3):
                pool.wait_ge(st("y_ok"), c + 1)
                if c < CH:
                    store(y_prompt[0, c * P:(c + 1) * P, :], PTf[:, c * D:(c + 1) * D])
                else:
                    store(y_sample[:, 0, :], PTf[0:NSAMP, c * D:(c + 1) * D])
            pool.wait_ge(st("stored"), outs[0])


_INS = ["x_prompt", "x_sample", "state_hgrn", "state_gdn", "state_gdn_conv", "state_pool", "w_in_even",
        "hgrn_norm_w", "gdn_conv_w", "gdn_a_log", "gdn_dt_bias", "gdn_norm_w", "w_out_even", "pool_w_in",
        "pool_w_group", "pool_scale", "norm_ffn1", "ffn1_w_gate", "ffn1_w_up", "ffn1_w_down", "norm_mix",
        "norm_ffn2", "ffn2_w_gate", "ffn2_w_up", "ffn2_w_down", "final_norm"]
_OUTS = [(1, PROMPT, D), (NSAMP, 1, D), (1, 1, HEADS, DH, DH), (1, 1, HEADS, DH, DH), (1, 1, CONV - 1, 3 * MIX),
         (1, 1, PBUF, D), (1, NSAMP, HEADS, DH, DH), (1, NSAMP, HEADS, DH, DH), (1, NSAMP, CONV - 1, 3 * MIX),
         (1, NSAMP, PBUF, D)]


def kernel(**inputs):
    from concourse import bacc
    from concourse.bass_utils import run_bass_kernel_spmd

    nc = bacc.Bacc("TRN2", target_bir_lowering=False, num_devices=1)
    arrays, ins, outs = {}, [], []
    for name in _INS:
        a = np.ascontiguousarray(inputs[name])
        arrays[f"in_{name}"] = a
        ins.append(nc.dram_tensor(f"in_{name}", a.shape, mybir.dt.from_np(a.dtype), kind="ExternalInput").ap())
    for i, shape in enumerate(_OUTS):
        outs.append(nc.dram_tensor(f"out_{i}", shape, F32, kind="ExternalOutput").ap())
    build(nc, ins, outs)
    r = run_bass_kernel_spmd(nc, [arrays], core_ids=[0])
    return tuple(r.results[0][f"out_{i}"] for i in range(len(_OUTS)))
```

```python
from contextlib import ExitStack

import numpy as np
import concourse.bass as bass
from concourse import mybir

F32 = mybir.dt.float32
F32R = mybir.dt.float32r
BF16 = mybir.dt.bfloat16
U16 = mybir.dt.uint16
ALU = mybir.AluOpType
ACT = mybir.ActivationFunctionType

P = 128
EPS = 1e-6
PROMPT, NSAMP = 256, 8
TOK = PROMPT + NSAMP
CH = PROMPT // P
D, DFF = 1024, 2816
KD, KF = D // P, DFF // P
BLK = 256
NB = DFF // BLK
HEADS, DH = 4, 128
MIX = D // 2
CONV = 4
CT = 3 * MIX // P
WINDOWS = (2, 4, 8, 16)
PBUF = max(WINDOWS) - 1
PAD = PBUF + 1
LEVELS = 7
SLOT = 1024
RAW, SPL = 4, 4
LEAD = SPL - 1
FFN_SLOTS = NB * 4 + KF
PROJ = [10, 11, 8, 9, 12, 13, 2, 3, 0, 1, 4, 5, 6, 7, 14, 15]
S_FFN = [0, FFN_SLOTS + 40, 2 * FFN_SLOTS + 40, 3 * FFN_SLOTS + 50]
S_PROJ = FFN_SLOTS
S_WOUT = S_PROJ + 32
S_PIN = 3 * FFN_SLOTS + 40
S_PGRP = S_PIN + 8
TOTAL = 4 * FFN_SLOTS + 50
assert S_PGRP + 2 == S_FFN[3] and S_FFN[3] + FFN_SLOTS == TOTAL
C_NORM, C_SCALE, C_CONV, C_HGN, C_GDN, NPAR = 0, 56, 64, 112, 113, 114


def build(nc, A, O_):
    (x_prompt, x_sample, state_hgrn, state_gdn, state_conv, state_pool, w_in, hgn, conv_w, a_log,
     dt_bias, gdn_n, w_out, pool_in, pool_grp, pool_scale, n_ffn1, f1g, f1u, f1d, n_mix, n_ffn2, f2g, f2u,
     f2d, n_fin) = A
    (y_prompt, y_sample, hg_p, gdn_p, conv_p, pool_p, hg_s, gdn_s, conv_s, pool_s) = O_
    FFN_W = [(f1g[0], f1u[0], f1d[0]), (f2g[0], f2u[0], f2d[0]),
             (f1g[1], f1u[1], f1d[1]), (f2g[1], f2u[1], f2d[1])]
    FFN_NORM = [0, 2, 3, 5]

    ctx = ExitStack()
    with ctx:
        def sb(name, shape, dt=F32, on=None):
            return (on or ctx).enter_context(nc.sbuf_tensor(name, shape, dt))

        def sem(name):
            return ctx.enter_context(nc.semaphore(name))

        raw = sb("raw", [P, RAW, SLOT])
        w_hi = sb("w_hi", [P, SPL, SLOT], F32R)
        w_lo = sb("w_lo", [P, SPL, SLOT], F32R)
        x = sb("x", [P, KD, TOK])
        hn = sb("hn", [P, KD, TOK])
        rstd = sb("rstd", [P, TOK])
        ident = sb("ident", [P, P])
        mean_w = sb("mean_w", [P, P])
        ones = sb("ones", [P, P])
        upper = sb("upper", [P, P])
        strict = sb("strict", [P, P])
        lvl = sb("lvl", [P, 2 * LEVELS + 1, P], BF16)
        par = sb("par", [P, NPAR])
        HM = sb("HM", [P, P])
        eps = sb("eps", [P, 1])
        WAB = sb("WAB", [P, KD, 8])
        SEL = sb("SEL", [P, 4, NSAMP])
        ab8 = sb("ab8", [8, 8])

        with ExitStack() as ffn_space:
            x_hi = sb("x_hi", [P, KD, TOK], F32R, ffn_space)
            x_lo = sb("x_lo", [P, KD, TOK], F32R, ffn_space)
            a_hi = sb("a_hi", [P, KF, TOK], F32R, ffn_space)
            a_lo = sb("a_lo", [P, KF, TOK], F32R, ffn_space)
            sg = sb("sg", [P, 2, TOK], on=ffn_space)
            pr = sb("pr", [P, 2, TOK], on=ffn_space)
        XH = sb("XH", [P, KD * TOK])
        XL = sb("XL", [P, KD * TOK])
        HS1, HS2, TOTS = XL[:, 0:512], XL[:, 512:1024], XL[:, 1024:2048]
        PT = sb("PT", [P, 32, TOK])
        C = sb("C", [P, CT, TOK])
        O = sb("O", [P, KD, TOK])
        DEC = sb("DEC", [P, 8, P])
        AT = sb("AT", [P, 8, P])
        TU = sb("TU", [P, 16, P])
        T = TU[:, 0:8, :]
        U = TU[:, 8:16, :]
        CROW = TU[:, :, :].rearrange("p i n -> p (i n)")[:, 0:CT * P]
        XVK = sb("XVK", [P, 24, P])
        X = XVK[:, 0:8, :]
        VT = XVK[:, 8:16, :]
        KT = XVK[:, 16:24, :]
        VN = sb("VN", [P, 8, P])
        QE = sb("QE", [P, 4, P])
        S1 = sb("S1", [P, 4, P])
        S2 = sb("S2", [P, 4, P])
        PTf = PT[:, :, :].rearrange("p a b -> p (a b)")
        QP, KS = PTf[:, 16 * TOK:16 * TOK + 1024], PTf[:, 16 * TOK + 1024:16 * TOK + 2048]
        ATT = PTf[:, 16 * TOK + 2048:16 * TOK + 3072].rearrange("p (i n) -> p i n", n=P)
        HVT = PTf[:, 0:1024].rearrange("p (i n) -> p i n", n=P)
        HKT = PTf[:, 1024:2048].rearrange("p (i n) -> p i n", n=P)
        GG = sb("GG", [P, 4, TOK])
        SBUFS = sb("SBUFS", [P, 2, NSAMP, P])

        def SV(j):
            if j % 4 < 2:
                return XH[:, j % 4 * 1024:(j % 4 + 1) * 1024].rearrange("p (b n) -> p b n", n=P)
            return SBUFS[:, j % 4 - 2]

        RN = sb("RN", [8, TOK])
        esel = sb("esel", [P, 8, 8])
        emean = sb("emean", [P, 8, 8])
        qscale = sb("qscale", [8, 1])
        VM = sb("VM", [8, NSAMP, P])
        ROWS = sb("ROWS", [32, CT * P])
        CB = sb("CB", [P, CT, 24])
        SMALL = sb("SMALL", [P, 400])
        GB = XVK[0:8, :, :].rearrange("p i n -> p (i n)")[:, 0:8 * TOK].rearrange("p (a t) -> p a t", a=8)
        ROWS2 = O[:, :, :].rearrange("p a b -> p (a b)")
        PBUFR = SBUFS[:, :, :, :].rearrange("p a b n -> p (a b n)")
        ps = ctx.enter_context(nc.psum_tensor("ps", [P, 8, 512], F32))
        psA = ps[:, 4:6, :].rearrange("p b (i n) -> p (b i) n", n=P)
        psC = ps[:, 0:2, :].rearrange("p b (i n) -> p (b i) n", n=P)
        psD = ps[:, 2:4, :].rearrange("p b (i n) -> p (b i) n", n=P)
        psB = ps[:, 6:8, :].rearrange("p b (i n) -> p (b i) n", n=P)

        raw_in = [sem(f"raw_in{r}") for r in range(RAW)]
        (hi_done, lo_done, used, silu_done, prod_done, ahi_done, alo_done, res_done,
         x_done, sq_done, ss_done, root_done, rstd_done, hn_done, xhi_done, xlo_done, p_ready, const_done,
         par_in, x_in, x_T, dve_chain, act_chain, pool_chain) = [sem(n) for n in (
             "hi_done", "lo_done", "used", "silu_done", "prod_done", "ahi_done",
             "alo_done", "res_done", "x_done", "sq_done", "ss_done", "root_done", "rstd_done", "hn_done", "xhi_done",
             "xlo_done", "p_ready", "const_done", "par_in", "x_in", "x_T", "dve_chain",
             "act_chain", "pool_chain")]
        stage_sem = {}

        def st(name):
            if name not in stage_sem:
                stage_sem[name] = sem(name)
            return stage_sem[name]

        block = ctx.enter_context(nc.Block())

        def v(base, i, per):
            return base if i is None else base + i * per

        def mixer_space_free(eng):
            eng.wait_ge(st("stored"), 16 * 4)
            for r in range(4):
                eng.wait_ge(st(f"samp_out{r}"), 32)

        @block.sync
        def _(sp):
            def load(s, src, i=None):
                if s >= RAW:
                    sp.wait_ge(lo_done, v(s - RAW + 1, i, 8))
                sp.dma_start(raw[:, s % RAW, :], src).then_inc(raw_in[s % RAW], 16)

            def cols(w, half, c0):
                return w[half * 512:(half + 1) * 512, :].rearrange("(k p) n -> p k n", p=P)[:, :, bass.ds(c0, BLK)]

            def load4(s, src, i=None):
                if s >= RAW:
                    sp.wait_ge(lo_done, v(s - RAW + 1, i, 8))
                sp.dma_start(raw[:, s % RAW, :].rearrange("p (k n) -> p k n", k=4), src)\
                    .then_inc(raw_in[s % RAW], 16)

            def ffn(n):
                s0 = S_FFN[n]
                wg, wu, wd = FFN_W[n]
                for q in range(4):
                    load4(s0 + q, cols((wg, wu)[q // 2], q % 2, 0))
                with sp.Fori(0, NB // 2) as i:
                    for q in range(8):
                        c0 = i * (2 * BLK) + (1 + q // 4) * BLK
                        load4(s0 + 4 + q, cols((wg, wu)[q // 2 % 2], q % 2, c0), i)
                s1 = s0 + 4 * NB
                for f in range(6):
                    load(s1 + f, wd[f * P:(f + 1) * P, :])
                with sp.Fori(0, (KF - 6) // 8) as i:
                    for q in range(8):
                        load(s1 + 6 + q, wd[bass.ds(i * (8 * P) + (6 + q) * P, P), :], i)

            ffn(0)
            for n, b in enumerate(PROJ):
                for half in range(2):
                    load4(S_PROJ + 2 * n + half, cols(w_in[0], half, b * BLK))
            for q in range(8):
                load4(S_WOUT + q, cols(w_out[0], q % 2, q // 2 * BLK))
            ffn(1)
            ffn(2)
            for q in range(8):
                load4(S_PIN + q, cols(pool_in[0], q % 2, q // 2 * BLK))
            for q in range(2):
                load4(S_PGRP + q, pool_grp[0, 2 * q:2 * q + 2].rearrange("g (k p) n -> p (g k) n", p=P))
            ffn(3)

        def even_scalar(act, tick, link, round_h, norm):
            A = nc.scalar

            def slots(lo, hi):
                for q in range(lo, hi):
                    tick(S_PROJ + q)
                    if q % 2 == 0 and q:
                        evac(q // 2 - 1)

            def evac(n):
                b = PROJ[n]
                act.wait_ge(used, S_PROJ + 2 * n + 2)
                A.copy(PT[:, 2 * b:2 * b + 2, :], ps[:, 2 * (n % 2):2 * (n % 2) + 2, 0:TOK]).then_inc(p_ready, 1)

            def tap0(c0):
                act.wait_ge(p_ready, c0 // 2 + 2 if c0 == 8 else (2 if c0 == 4 else 4))
                for c in range(c0, c0 + 4):
                    w = C_CONV + (CONV - 1) * CT + c
                    ins = A.activation(C[:, c, 0:PROMPT], PT[:, 16 + c, 0:PROMPT], ACT.Identity, scale=par[:, w:w + 1])
                ins.then_inc(st("tap0"), 1)

            slots(0, 6)
            act.wait_ge(st("conv_hist_T"), 1)
            A.copy(CB[:, :, :], ps[:, 6, 0:CT * 24].rearrange("p (c r) -> p c r", c=CT)).then_inc(st("conv_hist"), 1)
            tap0(4)
            act.wait_ge(st("gb_u"), 1)
            A.activation(GB[:, 6, :], GB[:, 7, :], ACT.Sigmoid).then_inc(st("beta"), 1)
            link(A.activation(GB[:, 1, :], GB[:, 0, :], ACT.Abs))
            link(A.activation(GB[:, 3, :], GB[:, 1, :], ACT.Exp, scale=-1.0))
            A.activation(ab8[:, 2:3], ab8[:, 1:2], ACT.Exp)
            A.activation(GB[:, 4, :], GB[:, 3, :], ACT.Ln, bias=1.0).then_inc(st("gb_ln"), 1)
            slots(6, 10)
            tap0(0)
            slots(10, 14)
            tap0(8)
            act.wait_ge(st("conv"), 1)
            A.activation(C[:, 0:8, :], C[:, 0:8, :], ACT.Silu).then_inc(st("conv_silu"), 1)
            slots(14, 15)
            act.wait_ge(st("conv_silu"), 1)
            A.activation(hn[:, :, :], C[:, 0:8, :], ACT.Square).then_inc(st("qk_sq"), 1)
            slots(15, 16)
            act.wait_ge(st("tok_T"), 1)
            A.copy(SMALL[:, 0:32], ps[:, 6, 0:32]).then_inc(st("gb_tok"), 1)
            act.wait_ge(st("conv"), 2)
            A.activation(C[:, 8:12, :], C[:, 8:12, :], ACT.Silu).then_inc(st("conv_silu"), 1)
            act.wait_ge(st("gb_rows_mm"), 1)
            A.activation(SMALL[:, 96:128], ps[:, 7, 0:32], ACT.Exp).then_inc(st("gs"), 1)
            A.copy(SMALL[:, 128:160], ps[:, 7, 32:64]).then_inc(st("bs"), 1)
            act.wait_ge(st("brow"), 1)
            A.activation(QE[:, :, :], psA[:, 4:8, :], ACT.Exp).then_inc(st("qe_exp"), 1)
            A.activation(SMALL[:, 64:72], psA[:, :, P - 1], ACT.Exp).then_inc(st("ebl"), 1)
            slots(16, 18)
            act.wait_ge(st("ncum"), 1)
            A.activation(SMALL[:, 48:56], SMALL[:, 40:48], ACT.Exp, scale=-1.0).then_inc(st("ebt"), 1)
            act.wait_ge(st("dec_diff"), 1)
            A.activation(DEC[:, :, :], DEC[:, :, :], ACT.Exp).then_inc(st("dec_exp"), 1)
            act.wait_ge(st("qk_ss"), 1)
            A.activation(RN[:, 0:TOK], ps[0:8, 7, 0:TOK], ACT.Sqrt, bias=eps[0:8, 0:1]).then_inc(st("qk_root"), 1)
            slots(18, 26)
            act.wait_ge(p_ready, 10)
            act.wait_ge(st("conv"), 2)
            act.wait_ge(st("crow_T"), 1)
            qa, fa = PT[:, 0:4, :], PT[:, 4:8, :]
            qpv = QP.rearrange("p (h t) -> p h t", h=4)
            ksv = KS.rearrange("p (h t) -> p h t", h=4)
            A.activation(GG[:, :, :], fa, ACT.Sigmoid)
            A.activation(ksv, fa[:, :, 0:PROMPT], ACT.Sigmoid, scale=-1.0)
            A.activation(SMALL[:, 192:224].rearrange("p (h b) -> p h b", h=4), fa[:, :, PROMPT:TOK],
                         ACT.Sigmoid, scale=-1.0)
            slots(26, 28)
            A.activation(qpv, qa[:, :, 0:PROMPT], ACT.Silu)
            A.activation(SMALL[:, 224:256].rearrange("p (h b) -> p h b", h=4), qa[:, :, PROMPT:TOK],
                         ACT.Silu).then_inc(st("hg_in"), 1)
            slots(28, 30)
            act.wait_ge(st("vt_T"), 1)
            A.copy(VT[:, :, :], psB).then_inc(st("vt"), 1)
            slots(30, 32)
            evac(15)
            act.wait_ge(p_ready, 16)
            act.wait_ge(st("hvt_T"), 1)
            act.wait_ge(st("hg_in"), 1)
            A.copy(HVT, psC).then_inc(st("hvt"), 1)
            act.wait_ge(st("rows_T"), 1)
            A.copy(ROWS[0:8, 0:8 * P].rearrange("p (i n) -> p i n", n=P), psD[0:8]).then_inc(st("rows"), 1)
            act.wait_ge(st("krows_T"), 1)
            A.copy(ROWS[0:8, 8 * P:12 * P].rearrange("p (i n) -> p i n", n=P), psC[0:8, 0:4]).then_inc(st("krows"), 1)

            def decay_state(j):
                act.wait_ge(st(f"samp_in{j % 4}"), 16 * (j // 4 + 1))
                if j == 4:
                    act.wait_ge(st("samp_ks"), 1)
                for b in range(NSAMP):
                    h = j % 4
                    col = GG[:, h, PROMPT + b:PROMPT + b + 1] if j < 4 else SMALL[:, 96 + 8 * h + b:97 + 8 * h + b]
                    ins = A.activation(SV(j)[:, b, :], SV(j)[:, b, :], ACT.Identity, scale=col)
                ins.then_inc(st("samp_dec"), 1)

            gates = [lambda: A.activation(PT[:, 12:16, :], PT[:, 12:16, :], ACT.Sigmoid),
                     lambda: A.activation(PT[:, 28:32, :], PT[:, 28:32, :], ACT.Silu).then_inc(st("gates"), 1)]
            for l in range(1, LEVELS):
                act.wait_ge(st("inv_x"), l)
                A.copy(X[:, :, :], psA).then_inc(st("inv_xc"), 1)
                if l <= 2:
                    gates[l - 1]()
                if l == 3:
                    act.wait_ge(st("gates"), 1)
                    A.activation(PT[:, 12:16, :], PT[:, 12:16, :], ACT.Identity, scale=par[:, C_HGN:C_HGN + 1])
                    A.activation(PT[:, 28:32, :], PT[:, 28:32, :], ACT.Identity, scale=par[:, C_GDN:C_GDN + 1])\
                        .then_inc(st("gates"), 1)
                if l >= 4:
                    decay_state(l - 4)
            act.wait_ge(st("hkt_T"), 1)
            A.copy(HKT, psC).then_inc(st("hkt"), 1)
            act.wait_ge(st("hs1_mm"), 1)
            A.copy(HS1, ps[:, 2, :]).then_inc(st("hs1"), 1)
            act.wait_ge(st("s1_mm"), 1)
            A.copy(S1[:, :, :], psA[:, 0:4, :]).then_inc(st("s1"), 1)
            act.wait_ge(st("ho_mm"), 1)
            A.copy(O[:, 0:4, 0:PROMPT], psC.rearrange("p (h c) t -> p h (c t)", h=4)).then_inc(st("o_a"), 1)
            decay_state(3)
            act.wait_ge(st("o_mm"), 1)
            A.copy(O[:, 4:8, 0:P], psA[:, 0:4, :])
            A.copy(O[:, 4:8, P:2 * P], psA[:, 4:8, :]).then_inc(st("o_b"), 1)
            act.wait_ge(st("o_b"), 1)
            act.wait_ge(st("qk_ss"), 1)
            A.activation(hn[:, :, 0:PROMPT], O[:, :, 0:PROMPT], ACT.Square).then_inc(st("o_sq"), 1)
            act.wait_ge(st("o_ss"), 1)
            act.wait_ge(st("qk_n"), 2)
            A.activation(RN[:, 0:PROMPT], ps[0:8, 5, 0:PROMPT], ACT.Sqrt, bias=eps[0:8, 0:1]).then_inc(st("o_root"), 1)
            for j in range(4, 8):
                decay_state(j)
            act.wait_ge(st("samp_o_mm"), 8)
            SO = O[:, :, PROMPT:TOK]
            A.copy(SO, ps[:, 6, 0:64].rearrange("p (h b) -> p h b", h=8)).then_inc(st("so"), 1)
            act.wait_ge(st("so"), 1)
            A.activation(SMALL[:, 256:320].rearrange("p (h b) -> p h b", h=8), SO, ACT.Square).then_inc(st("so_sq"), 1)
            act.wait_ge(st("so_ss"), 1)
            A.activation(SMALL[:, 320:384], ps[:, 6, 64:128], ACT.Sqrt, bias=eps[:, 0:1]).then_inc(st("so_root"), 1)
            act.wait_ge(st("o_norm"), 6)
            for r in range(4):
                act.wait_ge(st(f"samp_out{r}"), 32)
            for k in range(KD):
                A.copy(x_hi[:, k, :], O[:, k, :]).then_inc(st("o_hi"), 1)
            for q in range(8):
                tick(S_WOUT + q)
            norm(2)

        def odd_scalar(act, tick, norm):
            for n in range(4):
                tick(S_PIN + 2 * n)
                tick(S_PIN + 2 * n + 1)
                act.wait_ge(used, S_PIN + 2 * n + 2)
                if n == 0:
                    act.wait_ge(st("pad_zero"), 1)
                up = PTf[:, 0:KD * (PAD + TOK)].rearrange("p (k t) -> p k t", k=KD)
                nc.scalar.copy(up[:, 2 * n:2 * n + 2, PAD:], ps[:, 2 * n:2 * n + 2, 0:TOK])\
                    .then_inc(st("pool_u"), 1)
            for k in range(KD):
                act.wait_ge(st("pool_d"), k + 1)
                nc.scalar.copy(x_hi[:, k, :], hn[:, k, :]).then_inc(st("pool_hi"), 1)
            act.wait_ge(st("prow_T"), 1)
            nc.scalar.copy(C[0:23, 0:4, 0:256], ps[0:23, 4:6, :].rearrange("p b (i n) -> p (b i) n", n=256))\
                .then_inc(st("prow"), 1)
            tick(S_PGRP)
            tick(S_PGRP + 1)
            norm(5)

        @block.scalar
        def _(act):
            chain = [0]

            def link(ins):
                chain[0] += 1
                ins.then_inc(act_chain, 1)
                act.wait_ge(act_chain, chain[0])

            def tick(s, i=None):
                w = s + LEAD
                if w >= TOTAL:
                    return
                if w >= SPL:
                    act.wait_ge(used, v(w - SPL + 1, i, 8))
                act.wait_ge(raw_in[w % RAW], v(16 * (w // RAW + 1), i, 16 * 8 // RAW))
                nc.scalar.copy(w_hi[:, w % SPL, :], raw[:, w % RAW, :]).then_inc(hi_done, 1)

            def square(n, d):
                act.wait_ge(x_done, 8 * n + d + 1)
                nc.scalar.activation(hn[:, d, :], x[:, d, :], ACT.Square).then_inc(sq_done, 1)

            def round_h(n, k, src):
                act.wait_ge(hn_done, 8 * n + k + 1)
                nc.scalar.copy(x_hi[:, k, :], src[:, k, :]).then_inc(xhi_done, 1)

            def norm(n):
                for d in range(KD):
                    square(n, d)
                act.wait_ge(ss_done, n + 1)
                nc.scalar.activation(rstd[:, :], ps[:, 0, 0:TOK], ACT.Sqrt, bias=eps[:, 0:1]).then_inc(root_done, 1)
                for k in range(KD if n < 6 else 0):
                    round_h(n, k, hn)

            def ffn(n):
                s0, b0 = S_FFN[n], NB * n

                def silu(b, i=None):
                    act.wait_ge(used, v(s0 + 4 * (b - b0) + 2, i, 8))
                    if b:
                        act.wait_ge(prod_done, v(b, i, 2))
                    st4 = 4 * ((b - b0) % 2)
                    nc.scalar.activation(sg[:, :, :], ps[:, st4:st4 + 2, 0:TOK], ACT.Silu).then_inc(silu_done, 1)

                def round_a(b, i=None):
                    act.wait_ge(prod_done, v(b + 1, i, 2))
                    f = 2 * (b - b0) if i is None else i * 4 + 2 * (b - b0)
                    nc.scalar.copy(a_hi[:, bass.ds(f, 2), :], pr[:, :, :]).then_inc(ahi_done, 1)

                def blk(b, i=None):
                    s = s0 + 4 * (b - b0)
                    tick(s, i)
                    if b > b0:
                        round_a(b - 1, i)
                    tick(s + 1, i)
                    tick(s + 2, i)
                    silu(b, i)
                    tick(s + 3, i)

                blk(b0)
                with act.Fori(0, NB // 2) as i:
                    blk(b0 + 1, i)
                    blk(b0 + 2, i)
                s1 = s0 + 4 * NB
                tick(s1)
                round_a(b0 + NB - 1)
                for f in range(1, 5):
                    tick(s1 + f)
                with act.Fori(0, 2 if n < 3 else 1) as i:
                    for f in range(5, 13):
                        tick(s1 + f, i)
                for f in range(13, KF - 1 if n == 3 else 13):
                    tick(s1 + f)
                norm(FFN_NORM[n] + 1)
                tick(s1 + KF - 1)

            act.wait_ge(x_T, 1)
            nc.scalar.copy(par[:, :], ps[:, 0, 0:NPAR]).then_inc(st("par_ok"), 1)
            for s in range(-LEAD, 0):
                tick(s)
            act.wait_ge(const_done, 1)
            norm(0)
            ffn(0)
            even_scalar(act, tick, link, round_h, norm)
            mixer_space_free(act)
            ffn(1)
            ffn(2)
            odd_scalar(act, tick, norm)
            act.wait_ge(st("stored"), 16 * 6)
            ffn(3)
            for c in range(3):
                act.wait_ge(st("y_T"), c + 1)
                n = P if c < CH else NSAMP
                src = ps[0:n, (0, 2, 4)[c]:(0, 2, 4)[c] + 2, :]
                nc.scalar.copy(PTf[0:n, c * D:(c + 1) * D].rearrange("p (a b) -> p a b", a=2), src)\
                    .then_inc(st("y_ok"), 1)

        def even_vector(dve, tick, link, residual, norm):
            V = nc.vector

            def slots(lo, hi):
                for q in range(lo, hi):
                    tick(S_PROJ + q)

            def conv(c0, n):
                dve.wait_ge(st("tap0"), n)
                for j in range(CONV - 2, -1, -1):
                    back = CONV - 1 - j
                    for c in range(c0, c0 + 4):
                        w = C_CONV + j * CT + c
                        ins = V.scalar_tensor_tensor(C[:, c, back:PROMPT], PT[:, 16 + c, 0:PROMPT - back],
                                                     par[:, w:w + 1], C[:, c, back:PROMPT], ALU.mult, ALU.add)
                    if j:
                        link(ins)
                return ins

            slots(0, 6)
            dve.wait_ge(st("gb_mm"), 1)
            dve.wait_ge(st("ab_in"), 32)
            dve.wait_ge(st("masks_ok"), 1)
            link(V.tensor_copy(GB[:, 7, :], ps[0:8, 7, 0:TOK]))
            V.tensor_scalar(GB[:, 0, :], GB[:, 7, :], ab8[:, 0:1], None, ALU.add).then_inc(st("gb_u"), 1)
            dve.wait_ge(st("gb_u"), 1)
            link(V.tensor_scalar(GB[:, 2, :], GB[:, 0, :], 0.0, None, ALU.max))
            link(conv(4, 1))
            slots(6, 8)
            dve.wait_ge(st("gb_ln"), 1)
            link(V.tensor_tensor(GB[:, 2, :], GB[:, 2, :], GB[:, 4, :], ALU.add))
            V.tensor_scalar(GB[:, 5, :], GB[:, 2, :], ab8[:, 2:3], -1.0, ALU.mult, ALU.mult).then_inc(st("gb_g"), 1)
            slots(8, 10)
            link(conv(0, 2))
            slots(10, 12)
            dve.wait_ge(st("conv_hist"), 1)
            dve.wait_ge(p_ready, 6)

            def wall(j):
                return par[:, C_CONV + j * CT:C_CONV + (j + 1) * CT].unsqueeze(2).broadcast_to([P, CT, NSAMP])
            cs = C[:, :, PROMPT:TOK]
            hist = CB[:, :, :].rearrange("p c (b r) -> p c b r", r=CONV - 1)
            tmp = SMALL[:, 256:256 + CT * NSAMP].rearrange("p (c b) -> p c b", c=CT)
            link(V.tensor_tensor(cs, PT[:, 16:28, PROMPT:TOK], wall(CONV - 1), ALU.mult))
            for j in range(CONV - 1):
                link(V.tensor_tensor(tmp, hist[:, :, :, j], wall(j), ALU.mult))
                ins = V.tensor_tensor(cs, cs, tmp, ALU.add)
                if j < CONV - 2:
                    link(ins)
            ins.then_inc(st("conv"), 1)
            slots(12, 14)
            dve.wait_ge(st("conv"), 1)
            conv(8, 3).then_inc(st("conv"), 1)
            dve.wait_ge(st("crow_T"), 1)
            V.tensor_copy(CROW[0:11, :].rearrange("p (b n) -> p b n", n=512), ps[0:11, 4:7, :]).then_inc(st("crow"), 1)
            slots(14, 16)
            dve.wait_ge(st("gb_tok"), 1)
            tokv = SMALL[:, 0:32].rearrange("p (c y j) -> p c y j", c=2, y=2)
            beta = SMALL[:, 56:64]
            V.tensor_copy(beta.rearrange("p (c h) -> p c h", c=2), tokv[:, :, 1, 4:8])
            link(V.tensor_scalar(SMALL[:, 72:80].rearrange("p (c h) -> p c h", c=2), tokv[:, :, 1, 4:8], -1.0,
                                 None, ALU.mult))
            dve.wait_ge(st("cum_mm"), 1)
            V.tensor_scalar(SMALL[:, 40:48], ps[:, 6, 32:40], -1.0, None, ALU.mult).then_inc(st("ncum"), 1)
            dve.wait_ge(st("ncum"), 1)
            dve.wait_ge(st("ebl"), 1)
            for i in range(8):
                ins = V.tensor_scalar(DEC[:, i, :], psA[:, i, :], SMALL[:, 40 + i:41 + i], 0.0, ALU.add, ALU.min)
            ins.then_inc(st("dec_diff"), 1)
            slots(16, 18)
            dve.wait_ge(st("qk_root"), 1)
            link(V.reciprocal(RN[:, 0:TOK], RN[:, 0:TOK]))
            V.tensor_scalar(RN[:, 0:TOK], RN[:, 0:TOK], qscale[:, 0:1], None, ALU.mult).then_inc(st("qk_r"), 1)
            slots(18, 20)
            dve.wait_ge(st("dec_exp"), 1)
            link(V.tensor_copy(SMALL[:, 80:88], DEC[:, :, P - 1]))
            V.tensor_tensor(AT[:, :, :], DEC[:, :, :], strict[:, :].unsqueeze(1).broadcast_to([P, 8, P]), ALU.mult)\
                .then_inc(st("at_dec"), 1)
            dve.wait_ge(st("at_dec"), 1)
            link(V.tensor_tensor(DEC[:, :, :], DEC[:, :, :], upper[:, :].unsqueeze(1).broadcast_to([P, 8, P]),
                                 ALU.mult))
            for y, t0 in ((0, 4), (1, 0)):
                dve.wait_ge(st("qk_bc"), y + 1)
                V.tensor_tensor(C[:, t0:t0 + 4, :], C[:, t0:t0 + 4, :], ps[:, 4:8, 0:TOK], ALU.mult)\
                    .then_inc(st("qk_n"), 1)
                slots(20 + y, 21 + y)
            slots(22, 24)
            dve.wait_ge(st("kk_mm"), 1)
            for i in range(8):
                ins = V.scalar_tensor_tensor(AT[:, i, :], psA[:, i, :], SMALL[:, 72 + i:73 + i], AT[:, i, :],
                                             ALU.mult, ALU.mult)
            ins.then_inc(st("at"), 1)
            slots(24, 25)
            dve.wait_ge(st("kq_mm"), 1)
            V.tensor_tensor(DEC[:, :, :], DEC[:, :, :], psB, ALU.mult).then_inc(st("aqk"), 1)
            slots(25, 26)
            dve.wait_ge(st("qe_exp"), 1)
            dve.wait_ge(st("qk_n"), 2)
            V.tensor_tensor(QE[:, :, :], QE[:, :, :], C[:, 0:4, P:2 * P], ALU.mult).then_inc(st("qe"), 1)
            idb = ident[:, :].unsqueeze(1).broadcast_to([P, 8, P])

            def mask(m):
                return lvl[:, m, :].bitcast(U16).unsqueeze(1).broadcast_to([P, 8, P])
            dve.wait_ge(st("conv_rows_out"), 32)
            V.tensor_copy(T[:, :, :], idb)
            slots(26, 27)
            link(V.tensor_copy(U[:, :, :], idb))
            slots(27, 28)
            dve.wait_ge(st("at"), 1)
            V.copy_predicated(U[:, :, :], mask(0), AT[:, :, :])
            slots(28, 29)
            dve.wait_ge(st("a_T"), 1)
            V.copy_predicated(T[:, :, :], mask(LEVELS), psA).then_inc(st("inv"), 1)
            slots(29, 30)
            dve.wait_ge(st("hg_in"), 1)
            link(V.tensor_scalar(SMALL[:, 224:256], SMALL[:, 224:256], DH ** -0.5, None, ALU.mult))
            V.tensor_scalar(QP, QP, DH ** -0.5, None, ALU.mult).then_inc(st("hg_q"), 1)
            slots(30, 31)
            V.memset(ATT[:, :, :], 0.0).then_inc(st("hg_merge"), 1)
            slots(31, 32)

            g = GG[:, :, 0:PROMPT]
            tots = []

            def level_update(l):
                half = 1 << l
                n = 1024 // (2 * half)
                off = sum(1024 >> (m + 1) for m in range(l))
                if l == 0:
                    gv = g.rearrange("p h (j two) -> p h j two", two=2)
                    left, right = gv[:, :, :, 0], gv[:, :, :, 1]
                    nxt = TOTS[:, 0:n].rearrange("p (h j) -> p h j", h=4)
                    q4 = QP.rearrange("p (h j two) -> p h j two", h=4, two=2)[:, :, :, 1]
                    k4 = KS.rearrange("p (h j two) -> p h j two", h=4, two=2)[:, :, :, 0]
                    lb, rb = left, right
                else:
                    tv = tots[-1].rearrange("p (j two) -> p j two", two=2)
                    left, right, nxt = tv[:, :, 0], tv[:, :, 1], TOTS[:, off:off + n]
                    q4 = QP.rearrange("p (j two r) -> p j two r", two=2, r=half)[:, :, 1, :]
                    k4 = KS.rearrange("p (j two r) -> p j two r", two=2, r=half)[:, :, 0, :]
                    lb = left.unsqueeze(2).broadcast_to([P, n, half])
                    rb = right.unsqueeze(2).broadcast_to([P, n, half])
                V.tensor_tensor(q4, q4, lb, ALU.mult)
                V.tensor_tensor(k4, k4, rb, ALU.mult)
                V.tensor_tensor(nxt, left, right, ALU.mult).then_inc(st("hg_lvl"), 1)
                tots.append(TOTS[:, off:off + n])

            dve.wait_ge(used, S_PROJ + 32)
            for r in range(LEVELS + 1):
                dve.wait_ge(st("hg_att"), r + 1)
                if r == 0:
                    V.tensor_tensor(QP.rearrange("p (h t) -> p h t", h=4), QP.rearrange("p (h t) -> p h t", h=4), g,
                                    ALU.mult).then_inc(st("hg_lvl"), 1)
                else:
                    dve.wait_ge(st("hg_lvl"), r)
                    level_update(r - 1)
                if 1 <= r < LEVELS:
                    dve.wait_ge(st("inv"), r)
                    if r < LEVELS - 1:
                        dve.wait_ge(st("inv_t"), r)
                        V.copy_predicated(T[:, :, :], mask(LEVELS + r), psB)
                    dve.wait_ge(st("inv_u"), r)
                    V.copy_predicated(U[:, :, :], mask(r), psA).then_inc(st("inv"), 1)
                dve.wait_ge(st("hg_merge"), r + 1)
                V.copy_predicated(ATT[:, :, :], mask(2 * LEVELS if r == 0 else r - 1), psC if r % 2 == 0 else psD)\
                    .then_inc(st("hg_merge"), 1)
            rows = ROWS[0:8, :].rearrange("p (i n) -> p i n", n=P)
            diag = ident[0:8, 0:8].unsqueeze(2).broadcast_to([8, NSAMP, P])

            def value_rows(j):
                if j == 0:
                    dve.wait_ge(st("rows"), 1)
                    dve.wait_ge(st("krows"), 1)
                else:
                    dve.wait_ge(st("samp_outer"), j)
                V.tensor_tensor(VM[:, :, :], rows[:, 4 + j if j < 4 else j - 4, :].unsqueeze(1)
                                .broadcast_to([8, NSAMP, P]), diag, ALU.mult).then_inc(st("samp_vm"), 1)

            def new_state(j):
                dve.wait_ge(st("samp_dec"), j + 1)
                dve.wait_ge(st("samp_outer"), j + 1)
                V.tensor_tensor(SV(j), SV(j), psD if j % 2 == 0 else psC, ALU.add).then_inc(st("samp_new"), 1)

            value_rows(0)
            dve.wait_ge(st("kt_T"), 1)
            V.tensor_tensor(KT[:, :, :], psA, SMALL[:, 80:88].unsqueeze(2).broadcast_to([P, 8, P]), ALU.mult)\
                .then_inc(st("kt"), 1)
            dve.wait_ge(st("vn0_mm"), 1)
            V.tensor_tensor(VN[:, 0:4, :], psB[:, 0:4, :], beta[:, 0:4].unsqueeze(2).broadcast_to([P, 4, P]), ALU.mult)\
                .then_inc(st("vn0"), 1)
            totc = tots[-1].rearrange("p (h c) -> p h c", h=4)[:, :, 1:2].broadcast_to([P, 4, P])
            hs1v, hs2v = [a.rearrange("p (h n) -> p h n", h=4) for a in (HS1, HS2)]
            dve.wait_ge(st("hs1"), 1)
            dve.wait_ge(st("hg_lvl"), LEVELS + 1)
            link(V.tensor_tensor(hs2v, hs1v, totc, ALU.mult))
            dve.wait_ge(st("hs2_mm"), 1)
            V.tensor_tensor(HS2, HS2, ps[:, 3, :], ALU.add).then_inc(st("hs2"), 1)
            dve.wait_ge(st("ks_mm"), 1)
            dve.wait_ge(st("ebt"), 1)
            link(V.tensor_tensor(VN[:, 4:8, :], psB[:, 4:8, :],
                                 SMALL[:, 52:56].unsqueeze(2).broadcast_to([P, 4, P]), ALU.mult))
            V.tensor_tensor(VT[:, 4:8, :], VT[:, 4:8, :], VN[:, 4:8, :], ALU.subtract).then_inc(st("rhs1"), 1)
            new_state(0)
            value_rows(1)
            dve.wait_ge(st("vn1_mm"), 1)
            dve.wait_ge(st("rhs1"), 1)
            V.tensor_tensor(VN[:, 4:8, :], psB[:, 0:4, :], beta[:, 4:8].unsqueeze(2).broadcast_to([P, 4, P]), ALU.mult)\
                .then_inc(st("vn1"), 1)
            link(V.tensor_tensor(S2[:, :, :], S1[:, :, :], SMALL[:, 68:72].unsqueeze(2).broadcast_to([P, 4, P]),
                                 ALU.mult))
            new_state(1)
            value_rows(2)
            dve.wait_ge(st("s2_mm"), 1)
            V.tensor_tensor(S2[:, :, :], S2[:, :, :], psB[:, 4:8, :], ALU.add).then_inc(st("s2"), 1)
            for j in (2, 3):
                new_state(j)
                if j == 2:
                    value_rows(3)
            dve.wait_ge(st("o_root"), 1)
            V.reciprocal(RN[:, 0:PROMPT], RN[:, 0:PROMPT]).then_inc(st("o_r"), 1)
            dve.wait_ge(st("samp_ks"), 1)
            w1, w2 = SMALL[:, 160:192].rearrange("p (h b) -> p h b", h=4), \
                SMALL[:, 256:288].rearrange("p (h b) -> p h b", h=4)
            ksv = ps[:, 6, 64:96].rearrange("p (h b) -> p h b", h=4)
            egv = SMALL[:, 96:128].rearrange("p (h b) -> p h b", h=4)
            btv = SMALL[:, 128:160].rearrange("p (h b) -> p h b", h=4)
            link(V.tensor_tensor(w1, ksv, egv, ALU.mult))
            link(V.tensor_tensor(w2, C[:, 8:12, PROMPT:TOK], w1, ALU.subtract))
            V.tensor_tensor(w1, w2, btv, ALU.mult).then_inc(st("samp_vn"), 1)
            dve.wait_ge(st("samp_vnT"), 1)
            dve.wait_ge(st("samp_outer"), 4)
            link(V.tensor_copy(rows[:, 0:4, :], ps[0:8, 7, :].rearrange("p (h n) -> p h n", h=4)))
            dve.wait_ge(st("gates"), 2)

            def gated(y, step):
                o, gate = O[:, 4 * y:4 * y + 4, 0:PROMPT], PT[:, 12 + 16 * y:16 + 16 * y, 0:PROMPT]
                if step == 0:
                    dve.wait_ge(st("o_bc"), y + 1)
                    V.tensor_tensor(o, o, ps[:, 4:6, :].rearrange("p b (i n) -> p (b i) n", n=PROMPT), ALU.mult)\
                        .then_inc(st("o_norm"), 1)
                else:
                    dve.wait_ge(st("o_norm"), 2 * y + 1)
                    V.tensor_tensor(o, o, gate, ALU.mult).then_inc(st("o_norm"), 1)

            steps = [(0, 0), (0, 1), (1, 0), (1, 1)]
            for j in range(4, 8):
                value_rows(j)
                gated(*steps[j - 4])
                new_state(j)
            sn = SMALL[:, 320:384]
            snv = sn.rearrange("p (h b) -> p h b", h=8)
            so = O[:, :, PROMPT:TOK]
            dve.wait_ge(st("so_root"), 1)
            link(V.reciprocal(sn, sn))
            link(V.tensor_tensor(so, so, snv, ALU.mult))
            V.tensor_tensor(O[:, 0:4, PROMPT:TOK], O[:, 0:4, PROMPT:TOK], PT[:, 12:16, PROMPT:TOK], ALU.mult)\
                .then_inc(st("o_norm"), 1)
            V.tensor_tensor(O[:, 4:8, PROMPT:TOK], O[:, 4:8, PROMPT:TOK], PT[:, 28:32, PROMPT:TOK], ALU.mult)\
                .then_inc(st("o_norm"), 1)
            dve.wait_ge(st("o_norm"), 6)
            dve.wait_ge(st("stored"), 16 * 4)
            for k in range(KD):
                dve.wait_ge(st("o_hi"), k + 1)
                V.tensor_tensor(x_lo[:, k, :], O[:, k, :], x_hi[:, k, :].bitcast(F32), ALU.subtract)\
                    .then_inc(st("o_lo"), 1)
            for q in range(8):
                tick(S_WOUT + q)
                if q % 2 and q > 1:
                    residual(1.0, lambda d: (used, S_WOUT + 2 * (d // 2) + 2), range(q - 3, q - 1))
            residual(1.0, lambda d: (used, S_WOUT + 2 * (d // 2) + 2), range(6, 8))
            norm(2)

        def odd_vector(dve, tick, link, residual, norm):
            V = nc.vector
            W = PAD + TOK
            up = PTf[:, 0:KD * W].rearrange("p (k t) -> p k t", k=KD)
            wa = PTf[:, KD * W:2 * KD * W].rearrange("p (k t) -> p k t", k=KD)
            wb = PTf[:, 2 * KD * W:3 * KD * W].rearrange("p (k t) -> p k t", k=KD)
            cnt = SMALL[:, 0:64].rearrange("p (g t) -> p g t", g=4)
            dve.wait_ge(x_done, 8 * 5)
            V.memset(up[:, :, 0:PAD], 0.0).then_inc(st("pad_zero"), 1)
            for gi, w in enumerate(WINDOWS):
                link(V.memset(cnt[:, gi, :], 1.0 / w))
                for t in range(w - 1):
                    ins = V.memset(cnt[:, gi, t:t + 1], 1.0 / (t + 1))
                link(ins)
            for q in range(8):
                tick(S_PIN + q)
            dve.wait_ge(st("pool_u"), 4)
            src, dst = up, wa
            end = PAD + PROMPT
            for gi, w in enumerate(WINDOWS):
                lo, back = w - 1, w // 2
                link(V.tensor_tensor(dst[:, 2 * gi:, lo:end], src[:, 2 * gi:, lo:end],
                                     src[:, 2 * gi:, lo - back:end - back], ALU.add))
                win = dst[:, 2 * gi:2 * gi + 2, PAD:PAD + PROMPT]
                u = up[:, 2 * gi:2 * gi + 2, PAD:PAD + PROMPT]
                out = hn[:, 2 * gi:2 * gi + 2, :]
                V.scalar_tensor_tensor(out[:, :, 16:PROMPT], win[:, :, 16:], 1.0 / w, u[:, :, 16:], ALU.mult,
                                       ALU.subtract)
                link(V.tensor_tensor(out[:, :, 0:16], win[:, :, 0:16],
                                     cnt[:, gi, :].unsqueeze(1).broadcast_to([P, 2, 16]), ALU.mult))
                V.tensor_tensor(out[:, :, 0:16], out[:, :, 0:16], u[:, :, 0:16], ALU.subtract)
                if gi == 0:
                    dve.wait_ge(st("pool_hist"), 1)
                us = up[:, 2 * gi:2 * gi + 2, PAD + PROMPT:]
                hs = ps[:, 1, 16 * gi:16 * gi + 16].rearrange("p (k b) -> p k b", k=2)
                tmp = SMALL[:, 64 + 16 * gi:80 + 16 * gi].rearrange("p (k b) -> p k b", k=2)
                link(V.tensor_tensor(tmp, hs, us, ALU.add))
                V.scalar_tensor_tensor(out[:, :, PROMPT:TOK], tmp, 1.0 / w, us, ALU.mult, ALU.subtract)\
                    .then_inc(st("pool_d"), 2)
                src, dst = dst, (wb if dst is wa else wa)
            dve.wait_ge(st("pool_d"), 8)
            for k in range(KD):
                dve.wait_ge(st("pool_hi"), k + 1)
                V.tensor_tensor(x_lo[:, k, :], hn[:, k, :], x_hi[:, k, :].bitcast(F32), ALU.subtract)\
                    .then_inc(st("pool_lo"), 1)
            tick(S_PGRP)
            tick(S_PGRP + 1)
            residual(par[:, C_SCALE:C_SCALE + 8], lambda d: (used, S_PGRP + d // 4 + 1))
            norm(5)

        @block.vector
        def _(dve):
            chain = [0]

            def link(ins):
                chain[0] += 1
                ins.then_inc(dve_chain, 1)
                dve.wait_ge(dve_chain, chain[0])

            def tick(s, i=None):
                w = s + LEAD
                if w >= TOTAL:
                    return
                dve.wait_ge(hi_done, v(w + 1, i, 8))
                nc.vector.tensor_tensor(w_lo[:, w % SPL, :], raw[:, w % RAW, :],
                                        w_hi[:, w % SPL, :].bitcast(F32), ALU.subtract).then_inc(lo_done, 1)

            def lo_h(n, k):
                dve.wait_ge(xhi_done, 8 * n + k + 1)
                nc.vector.tensor_tensor(x_lo[:, k, :], hn[:, k, :], x_hi[:, k, :].bitcast(F32), ALU.subtract)\
                    .then_inc(xlo_done, 1)

            def residual(scale, ended, tiles=range(KD)):
                for d in tiles:
                    dve.wait_ge(*ended(d))
                    sc = scale if isinstance(scale, float) else scale[:, d:d + 1]
                    nc.vector.scalar_tensor_tensor(x[:, d, :], ps[:, d, 0:TOK], sc, x[:, d, :], ALU.mult, ALU.add)\
                        .then_inc(x_done, 1)

            def norm(n):
                dve.wait_ge(root_done, n + 1)
                nc.vector.reciprocal(rstd[:, :], rstd[:, :]).then_inc(rstd_done, 1)
                dve.wait_ge(rstd_done, n + 1)
                for k in range(KD):
                    nc.vector.scalar_tensor_tensor(hn[:, k, :], x[:, k, :], par[:, 8 * n + k:8 * n + k + 1],
                                                   rstd[:, :], ALU.mult, ALU.mult).then_inc(hn_done, 1)
                    if k and n < 6:
                        lo_h(n, k - 1)
                if n < 6:
                    lo_h(n, KD - 1)

            def ffn(n):
                s0, b0 = S_FFN[n], NB * n

                def prod(b, i=None):
                    dve.wait_ge(silu_done, v(b + 1, i, 2))
                    dve.wait_ge(used, v(s0 + 4 * (b - b0) + 4, i, 8))
                    st4 = 4 * ((b - b0) % 2) + 2
                    nc.vector.tensor_tensor(pr[:, :, :], sg[:, :, :], ps[:, st4:st4 + 2, 0:TOK], ALU.mult)\
                        .then_inc(prod_done, 1)

                def lo_a(b, i=None):
                    dve.wait_ge(ahi_done, v(b + 1, i, 2))
                    f = 2 * (b - b0) if i is None else i * 4 + 2 * (b - b0)
                    nc.vector.tensor_tensor(a_lo[:, bass.ds(f, 2), :], pr[:, :, :],
                                            a_hi[:, bass.ds(f, 2), :].bitcast(F32), ALU.subtract)\
                        .then_inc(alo_done, 1)

                def blk(b, i=None):
                    s = s0 + 4 * (b - b0)
                    if b > b0:
                        prod(b - 1, i)
                    tick(s, i)
                    tick(s + 1, i)
                    if b > b0:
                        lo_a(b - 1, i)
                    tick(s + 2, i)
                    tick(s + 3, i)
                    if b > b0:
                        dve.wait_ge(alo_done, v(b, i, 2))

                blk(b0)
                with dve.Fori(0, NB // 2) as i:
                    blk(b0 + 1, i)
                    blk(b0 + 2, i)
                s1 = s0 + 4 * NB
                prod(b0 + NB - 1)
                tick(s1)
                lo_a(b0 + NB - 1)
                for f in range(1, 5):
                    tick(s1 + f)
                dve.wait_ge(alo_done, b0 + NB)
                with dve.Fori(0, 2 if n < 3 else 1) as i:
                    for f in range(5, 13):
                        tick(s1 + f, i)
                for f in range(13, KF - 1 if n == 3 else 13):
                    tick(s1 + f)
                residual(0.5, lambda d: (res_done, 8 * n + d + 1))
                norm(FFN_NORM[n] + 1)
                tick(s1 + KF - 1)

            nc.vector.memset(mean_w[:, :], 1.0 / D)
            nc.vector.memset(eps[:, :], EPS)
            nc.vector.memset(ones[:, :], 1.0).then_inc(const_done, 1)
            dve.wait_ge(x_T, 2)
            for d in range(KD):
                nc.vector.tensor_copy(x[:, d, :], ps[:, d, 0:TOK]).then_inc(x_done, 1)
            dve.wait_ge(st("par_ok"), 1)
            for s in range(-LEAD, 0):
                tick(s)
            norm(0)
            ffn(0)
            even_vector(dve, tick, link, residual, norm)
            mixer_space_free(dve)
            ffn(1)
            ffn(2)
            odd_vector(dve, tick, link, residual, norm)
            dve.wait_ge(st("stored"), 16 * 6)
            ffn(3)

        def even_tensor(pe, mm, three, blk_slot, norm):
            tr = nc.tensor.transpose
            nwait = (lambda k: (xlo_done, 8 * 1 + k + 1))

            def slots(lo, hi):
                for q in range(lo, hi):
                    n = q // 2
                    if n >= 2 and q % 2 == 0:
                        pe.wait_ge(p_ready, n - 1)
                    blk_slot(S_PROJ + q, q % 2, 2 * (n % 2), None, nwait if n == 0 else None)

            ch = [(c, h) for c in range(2) for h in range(4)]
            hc = [(h, c) for h in range(4) for c in range(2)]
            slots(0, 6)
            pe.wait_ge(st("masks_ok"), 1)
            pe.wait_ge(st("hist_in"), 16)
            for c in range(CT):
                ins = tr(ps[:, 6, c * 24:(c + 1) * 24], ROWS2[0:24, c * P:(c + 1) * P], ident[0:24, 0:24])
            ins.then_inc(st("conv_hist_T"), 1)
            pe.wait_ge(st("wab_in"), 16)
            for k in range(KD):
                ins = mm(ps[0:8, 7, 0:TOK], WAB[:, k, :], hn[:, k, :], start=k == 0, stop=k == KD - 1)
            ins.then_inc(st("gb_mm"), 1)
            slots(6, 14)
            pe.wait_ge(p_ready, 6)
            pe.wait_ge(st("conv_hist"), 1)
            for c in range(CT):
                ins = tr(ps[0:11, 4 + c // 4, c % 4 * P:(c % 4 + 1) * P], PT[:, 16 + c, PROMPT - 3:TOK], ident[:, :])
            ins.then_inc(st("crow_T"), 1)
            slots(14, 15)
            pe.wait_ge(st("beta"), 1)
            pe.wait_ge(st("gb_g"), 1)
            pe.wait_ge(st("crow"), 1)
            for c in range(2):
                for y, row in ((0, 5), (1, 6)):
                    ins = tr(ps[:, 6, 16 * c + 8 * y:16 * c + 8 * y + 8], GB[:, row, c * P:(c + 1) * P], ident[0:8, 0:8])
            ins.then_inc(st("tok_T"), 1)
            for j in range(8):
                ins = mm(ps[:, 7, 8 * j:8 * j + 8], ident[0:8, j:j + 1].broadcast_to([8, P]),
                         GB[:, 5 if j < 4 else 6, PROMPT:TOK], start=True, stop=True)
            ins.then_inc(st("gb_rows_mm"), 1)
            slots(15, 16)
            pe.wait_ge(st("gb_tok"), 1)
            gt = SMALL[:, 0:32].rearrange("p (c y j) -> p c y j", c=2, y=2)
            mm(ps[:, 6, 32:40].rearrange("p (c h) -> p c h", c=2), upper[:, :], gt[:, :, 0, 0:4], start=True,
               stop=True).then_inc(st("cum_mm"), 1)
            for i, (c, h) in enumerate(ch):
                ins = mm(psA[:, i, :], gt[:, c, 0, h:h + 1].broadcast_to([P, P]), upper[:, :], start=True, stop=True)
            ins.then_inc(st("brow"), 1)
            pe.wait_ge(st("qk_sq"), 1)
            pe.wait_ge(st("esel_ok"), 1)
            pe.wait_ge(st("gs"), 1)
            pe.wait_ge(st("bs"), 1)
            for d in range(8):
                ins = mm(ps[0:8, 7, 0:TOK], esel[:, d, :], hn[:, d, :], start=d == 0, stop=d == 7)
            ins.then_inc(st("qk_ss"), 1)
            slots(16, 20)
            pe.wait_ge(st("qk_r"), 1)
            pe.wait_ge(st("dec_diff"), 1)
            pe.wait_ge(st("qe_exp"), 1)
            pe.wait_ge(st("ncum"), 1)
            for y, t0 in ((0, 4), (1, 0)):
                if y:
                    pe.wait_ge(st("qk_n"), 1)
                for h in range(4):
                    ins = mm(ps[:, 4 + h, 0:TOK], ident[0:8, t0 + h:t0 + h + 1].broadcast_to([8, P]), RN[:, 0:TOK],
                             start=True, stop=True)
                ins.then_inc(st("qk_bc"), 1)
                slots(20 + y, 21 + y)
            pe.wait_ge(st("qk_n"), 2)
            for i, (c, h) in enumerate(ch):
                kk = C[:, 4 + h, c * P:(c + 1) * P]
                ins = mm(psA[:, i, :], kk, kk, start=True, stop=True)
            ins.then_inc(st("kk_mm"), 1)
            for i, (c, h) in enumerate(ch):
                ins = mm(psB[:, i, :], C[:, 4 + h, c * P:(c + 1) * P], C[:, h, c * P:(c + 1) * P], start=True,
                         stop=True)
            ins.then_inc(st("kq_mm"), 1)
            slots(22, 26)
            pe.wait_ge(st("at"), 1)
            for i in range(8):
                ins = tr(psA[:, i, :], AT[:, i, :], ident[:, :])
            ins.then_inc(st("a_T"), 1)
            slots(26, 28)
            pe.wait_ge(st("aqk"), 1)
            pe.wait_ge(st("conv_silu"), 2)
            for i, (c, h) in enumerate(ch):
                ins = tr(psB[:, i, :], C[:, 8 + h, c * P:(c + 1) * P], ident[:, :])
            ins.then_inc(st("vt_T"), 1)
            slots(28, 32)
            pe.wait_ge(p_ready, 16)
            for i, (h, c) in enumerate(hc):
                ins = tr(psC[:, i, :], PT[:, 8 + h, c * P:(c + 1) * P], ident[:, :])
            ins.then_inc(st("hvt_T"), 1)
            pe.wait_ge(st("hg_in"), 1)
            for h in range(4):
                tr(psD[0:8, h, :], SMALL[:, 192 + 8 * h:200 + 8 * h], ident[:, :])
                ins = tr(psD[0:8, 4 + h, :], PT[:, 8 + h, PROMPT:TOK], ident[:, :])
            ins.then_inc(st("rows_T"), 1)
            pe.wait_ge(st("hvt"), 1)
            for h in range(4):
                ins = tr(psC[0:8, h, :], C[:, 4 + h, PROMPT:TOK], ident[:, :])
            ins.then_inc(st("krows_T"), 1)

            def att(r, half):
                out = psC if r % 2 == 0 else psD
                for i in range(4 * half, 4 * half + 4):
                    ins = mm(out[:, i, :], KS[:, i * P:(i + 1) * P], QP[:, i * P:(i + 1) * P], start=True, stop=True)
                return ins

            for r in range(LEVELS + 1):
                if r == 0:
                    pe.wait_ge(st("hg_q"), 1)
                    pe.wait_ge(st("krows"), 1)
                    pe.wait_ge(st("rows"), 1)
                else:
                    pe.wait_ge(st("hg_lvl"), r)
                    pe.wait_ge(st("hg_merge"), r)
                att(r, 0)
                inverse = 1 <= r < LEVELS
                if inverse:
                    pe.wait_ge(st("inv"), r)
                    if r == 1:
                        pe.wait_ge(st("vt"), 1)
                    for i in range(8):
                        ins = mm(psA[:, i, :], AT[:, i, :], T[:, i, :], start=True, stop=True)
                    ins.then_inc(st("inv_x"), 1)
                att(r, 1).then_inc(st("hg_att"), 1)
                if inverse:
                    pe.wait_ge(st("inv_xc"), r)
                    if r < LEVELS - 1:
                        for i in range(8):
                            ins = mm(psB[:, i, :], U[:, i, :], X[:, i, :], start=True, stop=True)
                        ins.then_inc(st("inv_t"), 1)
                    for i in range(8):
                        ins = mm(psA[:, i, :], X[:, i, :], U[:, i, :], start=True, stop=True)
                    ins.then_inc(st("inv_u"), 1)

            rows = ROWS[0:8, :].rearrange("p (i n) -> p i n", n=P)

            def outer(j):
                pe.wait_ge(st("samp_vm"), j + 1)
                if j >= 2:
                    pe.wait_ge(st("samp_new"), j - 1)
                krow = rows[:, j, :] if j < 4 else rows[:, 4 + j, :]
                vm = VM[:, :, :].rearrange("p b n -> p (b n)")
                for y in range(2):
                    ins = mm(ps[:, (2, 0)[j % 2] + y, :], krow, vm[:, 512 * y:512 * (y + 1)], start=True, stop=True)
                ins.then_inc(st("samp_outer"), 1)

            def read_out(j):
                pe.wait_ge(st("samp_new"), j + 1)
                h = j % 4
                for b in range(NSAMP):
                    q = SMALL[:, 224 + 8 * h + b:225 + 8 * h + b] if j < 4 else C[:, h, PROMPT + b:PROMPT + b + 1]
                    ins = mm(ps[:, 6, 8 * j + b:8 * j + b + 1], SV(j)[:, b, :], q, start=True, stop=True)
                ins.then_inc(st("samp_o_mm"), 1)

            pe.wait_ge(st("inv"), LEVELS)
            for i, (c, h) in enumerate(ch):
                ins = tr(psA[:, i, :], C[:, 4 + h, c * P:(c + 1) * P], ident[:, :])
            ins.then_inc(st("kt_T"), 1)
            pe.wait_ge(st("hg_lvl"), LEVELS + 1)
            pe.wait_ge(st("hg_merge"), LEVELS + 1)
            for i in range(8):
                ins = tr(psC[:, i, :], KS[:, i * P:(i + 1) * P], ident[:, :])
            ins.then_inc(st("hkt_T"), 1)
            for h in range(4):
                ins = mm(psB[:, h, :], U[:, h, :], VT[:, h, :], start=True, stop=True)
            ins.then_inc(st("vn0_mm"), 1)
            pe.wait_ge(st("hvt"), 1)
            pe.wait_ge(st("hkt"), 1)
            pe.wait_ge(st("hg_merge"), LEVELS + 2)
            for y in range(2):
                for h in range(4):
                    ins = mm(ps[:, 2 + y, h * P:(h + 1) * P], HKT[:, 2 * h + y, :], HVT[:, 2 * h + y, :], start=True,
                             stop=True)
                ins.then_inc(st(("hs1_mm", "hs2_mm")[y]), 1)
            pe.wait_ge(st("kt"), 1)
            pe.wait_ge(st("vn0"), 1)
            for h in range(4):
                ins = mm(psA[:, h, :], KT[:, h, :], VN[:, h, :], start=True, stop=True)
            ins.then_inc(st("s1_mm"), 1)
            pe.wait_ge(st("hs1"), 1)
            for h in range(4):
                mm(psC[:, 2 * h, :], HVT[:, 2 * h, :], ATT[:, 2 * h, :], start=True, stop=True)
                q1 = QP[:, (2 * h + 1) * P:(2 * h + 2) * P]
                mm(psC[:, 2 * h + 1, :], HS1[:, h * P:(h + 1) * P], q1, start=True, stop=False)
                ins = mm(psC[:, 2 * h + 1, :], HVT[:, 2 * h + 1, :], ATT[:, 2 * h + 1, :], start=False, stop=True)
            ins.then_inc(st("ho_mm"), 1)
            pe.wait_ge(st("s1"), 1)
            for h in range(4):
                ins = mm(psB[:, 4 + h, :], C[:, 4 + h, P:2 * P], S1[:, h, :], start=True, stop=True)
            ins.then_inc(st("ks_mm"), 1)
            pe.wait_ge(st("hs2"), 1)
            outer(0)
            pe.wait_ge(st("rhs1"), 1)
            for h in range(4):
                ins = mm(psB[:, h, :], U[:, 4 + h, :], VT[:, 4 + h, :], start=True, stop=True)
            ins.then_inc(st("vn1_mm"), 1)
            pe.wait_ge(st("o_a"), 1)
            outer(1)
            pe.wait_ge(st("vn1"), 1)
            for h in range(4):
                ins = mm(psB[:, 4 + h, :], KT[:, 4 + h, :], VN[:, 4 + h, :], start=True, stop=True)
            ins.then_inc(st("s2_mm"), 1)
            pe.wait_ge(st("qe"), 1)
            for h in range(4):
                mm(psA[:, h, :], VN[:, h, :], DEC[:, h, :], start=True, stop=True)
            for h in range(4):
                mm(psA[:, 4 + h, :], S1[:, h, :], QE[:, h, :], start=True, stop=False)
                ins = mm(psA[:, 4 + h, :], VN[:, 4 + h, :], DEC[:, 4 + h, :], start=False, stop=True)
            ins.then_inc(st("o_mm"), 1)
            read_out(0)
            outer(2)
            read_out(1)
            outer(3)
            pe.wait_ge(st("o_sq"), 1)
            for d in range(8):
                ins = mm(ps[0:8, 5, 0:PROMPT], emean[:, d, :], hn[:, d, 0:PROMPT], start=d == 0, stop=d == 7)
            ins.then_inc(st("o_ss"), 1)
            read_out(2)
            read_out(3)
            for j in range(4, 8):
                pe.wait_ge(st(f"samp_in{j % 4}"), 32)
                for b in range(NSAMP):
                    h = j - 4
                    ins = mm(ps[:, 6, 64 + 8 * h + b:65 + 8 * h + b], SV(j)[:, b, :],
                             C[:, 4 + h, PROMPT + b:PROMPT + b + 1], start=True, stop=True)
            ins.then_inc(st("samp_ks"), 1)
            pe.wait_ge(st("o_r"), 1)

            def factors(y):
                for h in range(4):
                    ins = mm(ps[:, 4 + h // 2, h % 2 * PROMPT:(h % 2 + 1) * PROMPT],
                             ident[0:8, 4 * y + h:4 * y + h + 1].broadcast_to([8, P]), RN[:, 0:PROMPT], start=True,
                             stop=True)
                ins.then_inc(st("o_bc"), 1)

            factors(0)
            pe.wait_ge(st("samp_vn"), 1)
            pe.wait_ge(st("s2"), 1)
            for h in range(4):
                ins = tr(ps[0:8, 7, h * P:(h + 1) * P], SMALL[:, 160 + 8 * h:168 + 8 * h], ident[:, :])
            ins.then_inc(st("samp_vnT"), 1)
            outer(4)
            outer(5)
            read_out(4)
            pe.wait_ge(st("o_norm"), 1)
            factors(1)
            outer(6)
            read_out(5)
            outer(7)
            read_out(6)
            read_out(7)
            pe.wait_ge(st("so_sq"), 1)
            mm(ps[:, 6, 64:128], HM[:, :], SMALL[:, 256:320], start=True, stop=True).then_inc(st("so_ss"), 1)
            pe.wait_ge(st("o_norm"), 6)
            for n in range(4):
                for half in range(2):
                    s = S_WOUT + 2 * n + half
                    pe.wait_ge(lo_done, s + 1)
                    for k4 in range(4):
                        k = 4 * half + k4
                        if n == 0:
                            pe.wait_ge(st("o_lo"), k + 1)
                        for j in range(2):
                            ins = three(ps[:, 2 * n + j, 0:TOK], s, k4 * BLK + j * P, x_hi[:, k, :], x_lo[:, k, :],
                                        k == 0, k == KD - 1)
                    ins.then_inc(used, 1)
            norm(2)

        def odd_tensor(pe, mm, three, blk_slot, norm):
            tr = nc.tensor.transpose
            W = PAD + TOK
            up = PTf[:, 0:KD * W].rearrange("p (k t) -> p k t", k=KD)
            for n in range(4):
                for half in range(2):
                    kw = (lambda k: (xlo_done, 8 * 4 + k + 1)) if n == 0 else None
                    blk_slot(S_PIN + 2 * n + half, half, 2 * n, None, kw)
            pe.wait_ge(st("pool_u"), 4)
            pe.wait_ge(st("pbuf_in"), 16)
            pe.wait_ge(st("sel_ok"), 1)
            for d in range(KD):
                ins = mm(ps[:, 1, 8 * d:8 * d + 8], PBUFR[0:120, d * P:(d + 1) * P], SEL[0:120, d // 2, :],
                         start=True, stop=True)
            ins.then_inc(st("pool_hist"), 1)
            for d in range(KD):
                ins = tr(ps[0:23, 4 + d // 4, d % 4 * P:(d % 4 + 1) * P], up[:, d, PAD + PROMPT - PBUF:PAD + TOK],
                         ident[:, :])
            ins.then_inc(st("prow_T"), 1)
            pe.wait_ge(st("pool_d"), 8)
            pe.wait_ge(st("prow"), 1)
            for q in range(2):
                pe.wait_ge(lo_done, S_PGRP + q + 1)
                for g2 in range(2):
                    g = 2 * q + g2
                    for j in range(2):
                        for kk in range(2):
                            pe.wait_ge(st("pool_lo"), 2 * g + kk + 1)
                            ins = three(ps[:, 2 * g + j, 0:TOK], S_PGRP + q, (2 * g2 + kk) * BLK + j * P,
                                        x_hi[:, 2 * g + kk, :], x_lo[:, 2 * g + kk, :], kk == 0, kk == 1)
                ins.then_inc(used, 1)
            norm(5)

        @block.tensor
        def _(pe):
            mm = nc.tensor.matmul

            def three(out, s, c0, hi, lo, first, last):
                wh = w_hi[:, s % SPL, c0:c0 + P]
                wl = w_lo[:, s % SPL, c0:c0 + P]
                mm(out, wh, hi, start=first, stop=False)
                mm(out, wh, lo, start=False, stop=False)
                return mm(out, wl, hi, start=False, stop=last)

            def blk_slot(s, half, banks, i=None, k_wait=None):
                pe.wait_ge(lo_done, v(s + 1, i, 8))
                for k4 in range(4):
                    k = 4 * half + k4
                    if k_wait:
                        pe.wait_ge(*k_wait(k))
                    for j in range(2):
                        ins = three(ps[:, banks + j, 0:TOK], s, k4 * BLK + j * P, x_hi[:, k, :], x_lo[:, k, :],
                                    k == 0, k == KD - 1)
                ins.then_inc(used, 1)
                return ins

            def norm(n, frees_slot=False):
                for d in range(KD):
                    pe.wait_ge(sq_done, 8 * n + d + 1)
                    ins = mm(ps[:, 0, 0:TOK], mean_w[:, :], hn[:, d, :], start=d == 0, stop=d == KD - 1)
                    if d == 0 and frees_slot:
                        ins.then_inc(used, 1)
                ins.then_inc(ss_done, 1)

            def ffn(n):
                s0, b0, nn = S_FFN[n], NB * n, FFN_NORM[n]

                def blk(b, i=None):
                    s = s0 + 4 * (b - b0)
                    banks = 4 * ((b - b0) % 2)
                    for q in range(4):
                        if b and q == 0:
                            pe.wait_ge(silu_done, v(b, i, 2))
                        if b and q == 2:
                            pe.wait_ge(prod_done, v(b, i, 2))
                        kw = (lambda k: (xlo_done, 8 * nn + k + 1)) if (b == b0 and q < 2) else None
                        blk_slot(s + q, q % 2, banks + 2 * (q // 2), i, kw)

                blk(b0)
                with pe.Fori(0, NB // 2) as i:
                    blk(b0 + 1, i)
                    blk(b0 + 2, i)
                s1 = s0 + 4 * NB

                def down(f, ds, i=None):
                    hi, lo = (a_hi[:, f, :], a_lo[:, f, :]) if i is None else \
                        [a[:, bass.ds(i * 8 + f, 1), :].rearrange("p a t -> p (a t)") for a in (a_hi, a_lo)]
                    for d in ds:
                        ins = three(ps[:, d, 0:TOK], s1 + f, d * P, hi, lo, f == 0, f == KF - 1)
                    return ins

                pe.wait_ge(lo_done, s1 + 2)
                pe.wait_ge(alo_done, b0 + NB - 1)
                down(0, range(4, 8))
                down(1, range(4, 8))
                pe.wait_ge(prod_done, b0 + NB)
                down(0, range(4)).then_inc(used, 1)
                down(1, range(4)).then_inc(used, 1)
                with pe.Fori(0, 2) as i:
                    for f in range(2, 10):
                        pe.wait_ge(lo_done, v(s1 + f + 1, i, 8))
                        down(f, range(8), i).then_inc(used, 1)
                for f in range(18, KF - 2):
                    pe.wait_ge(lo_done, s1 + f + 1)
                    down(f, range(8)).then_inc(used, 1)
                pe.wait_ge(lo_done, s1 + KF)
                pe.wait_ge(alo_done, b0 + NB)
                for d in range(KD):
                    ins = down(KF - 2, [d])
                    if d == KD - 1:
                        ins.then_inc(used, 1)
                    down(KF - 1, [d]).then_inc(res_done, 1)
                norm(nn + 1, frees_slot=True)

            pe.wait_ge(st("ident_ok"), 1)
            pe.wait_ge(par_in, 16 * 11)
            nc.tensor.transpose(ps[:, 0, 0:NPAR], X[0:NPAR, 0, :], ident[0:NPAR, 0:NPAR]).then_inc(x_T, 1)
            pe.wait_ge(x_in, 48)
            pe.wait_ge(st("par_ok"), 1)
            for d in range(KD):
                for c in range(3):
                    n = P if c < CH else NSAMP
                    ins = nc.tensor.transpose(ps[:, d, c * P:c * P + n], PTf[0:n, c * D + d * P:c * D + (d + 1) * P],
                                              ident[0:n, 0:n])
            ins.then_inc(x_T, 1)
            pe.wait_ge(const_done, 1)
            norm(0)
            ffn(0)
            even_tensor(pe, mm, three, blk_slot, norm)
            ffn(1)
            ffn(2)
            odd_tensor(pe, mm, three, blk_slot, norm)
            ffn(3)
            pe.wait_ge(hn_done, 8 * 7)
            for c in range(3):
                n = P if c < CH else NSAMP
                for d in range(KD):
                    b = (0, 2, 4)[c] + d // 4
                    ins = nc.tensor.transpose(ps[0:n, b, d % 4 * P:(d % 4 + 1) * P], hn[:, d, c * P:c * P + n],
                                              ident[:, :])
                ins.then_inc(st("y_T"), 1)

        @block.gpsimd
        def _(pool):
            G = nc.gpsimd
            n_chain = [0]

            def link(ins):
                n_chain[0] += 1
                ins.then_inc(pool_chain, 1)
                pool.wait_ge(pool_chain, n_chain[0])

            prow = X[:, 0, :]
            rows = [(n_ffn1[0], 0), (n_mix[0], 1), (n_ffn2[0], 2), (n_ffn1[1], 3), (n_mix[1], 4), (n_ffn2[1], 5),
                    (n_fin, 6), (pool_scale[0], 7)]
            for src, r in rows:
                pool.dma_start(prow[8 * r:8 * r + 8, :], src.rearrange("(k p) -> k p", p=P)).then_inc(par_in, 16)
            pool.dma_start(prow[C_CONV:C_HGN, :], conv_w[0].rearrange("j (c p) -> (j c) p", p=P)).then_inc(par_in, 16)
            pool.dma_start(prow[C_HGN:C_HGN + 1, :], hgn).then_inc(par_in, 16)
            pool.dma_start(prow[C_GDN:C_GDN + 1, :], gdn_n).then_inc(par_in, 16)
            for c in range(2):
                pool.dma_start(PTf[:, c * D:(c + 1) * D], x_prompt[0, c * P:(c + 1) * P, :]).then_inc(x_in, 16)
            pool.dma_start(PTf[0:NSAMP, 2 * D:3 * D], x_sample[:, 0, :]).then_inc(x_in, 16)
            link(G.memset(ident[:, :], 0.0))
            G.affine_select(out=ident[:, :], in_=ident[:, :], compare_op=ALU.not_equal, fill=1.0, base=0,
                            pattern=[[-1, P]], channel_multiplier=1).then_inc(st("ident_ok"), 1)
            link(G.memset(ab8[:, :], 0.0))
            pool.dma_start(ab8[0:4, 0:1], dt_bias.rearrange("a h -> h a")).then_inc(st("ab_in"), 16)
            pool.dma_start(ab8[0:4, 1:2], a_log.rearrange("a h -> h a")).then_inc(st("ab_in"), 16)
            pool.dma_start(WAB[:, :, :], w_in[0, :, 4096:4104].rearrange("(k p) n -> p k n", p=P))\
                .then_inc(st("wab_in"), 16)
            G.memset(upper[:, :], 1.0)
            link(G.memset(strict[:, :], 1.0))
            G.affine_select(out=upper[:, :], in_=upper[:, :], compare_op=ALU.is_ge, fill=0.0, base=0,
                            pattern=[[1, P]], channel_multiplier=-1)
            G.affine_select(out=strict[:, :], in_=strict[:, :], compare_op=ALU.is_gt, fill=0.0, base=0,
                            pattern=[[1, P]], channel_multiplier=-1)
            G.memset(lvl[:, 0:2 * LEVELS, :], 0.0)
            link(G.tensor_copy(lvl[:, 2 * LEVELS, :], ident[:, :]))
            for l in range(LEVELS):
                h = 1 << l
                pat = [[-2 * h, P // (2 * h)], [0, h]]
                neg = [[2 * h, P // (2 * h)], [0, h]]
                for m, side, lo, hi in ((l, 1, 0, h - 1), (LEVELS + l, 0, h, 2 * h - 1)):
                    part = lvl[:, m, :].rearrange("p (j two r) -> p j two r", two=2, r=h)[:, :, side, :]
                    link(G.memset(part, 1.0))
                    link(G.affine_select(out=part, in_=part, compare_op=ALU.is_ge, fill=0.0, base=-lo,
                                         pattern=pat, channel_multiplier=1))
                    link(G.affine_select(out=part, in_=part, compare_op=ALU.is_ge, fill=0.0, base=hi,
                                         pattern=neg, channel_multiplier=-1))
            G.memset(HM[:, :], 1.0 / DH)
            link(G.memset(qscale[:, :], 1.0))
            G.affine_select(out=qscale[:, :], in_=qscale[:, :], compare_op=ALU.is_ge, fill=DH ** -0.5, base=-4,
                            pattern=[[0, 1]], channel_multiplier=1).then_inc(st("masks_ok"), 1)
            link(G.memset(SEL[:, :, :], 1.0))
            for gi, w in enumerate(WINDOWS):
                link(G.affine_select(out=SEL[:, gi, :], in_=SEL[:, gi, :], compare_op=ALU.is_ge, fill=0.0,
                                     base=-(PBUF - (w - 1)), pattern=[[-PBUF, NSAMP]], channel_multiplier=1))
                ins = G.affine_select(out=SEL[:, gi, :], in_=SEL[:, gi, :], compare_op=ALU.is_ge, fill=0.0,
                                      base=PBUF - 1, pattern=[[PBUF, NSAMP]], channel_multiplier=-1)
            ins.then_inc(st("sel_ok"), 1)
            outs = [0]

            def store(dst, src):
                outs[0] += 16
                pool.dma_start(dst, src).then_inc(st("stored"), 16)

            store(conv_s[0, :, 0:CONV - 2, :], state_conv[0, :, 1:CONV - 1, :])
            store(pool_s[0, :, 0:PBUF - 1, :], state_pool[0, :, 1:PBUF, :])
            pool.wait_ge(x_done, 8 * 2)
            pool.dma_start(ROWS2[0:24, 0:CT * P], state_conv[0].rearrange("b r n -> (b r) n"))\
                .then_inc(st("hist_in"), 16)
            link(G.memset(esel[:, :, :], 0.0))
            link(G.memset(emean[:, :, :], 0.0))
            for d in range(8):
                G.memset(esel[:, d, d:d + 1], 1.0)
                ins = G.memset(emean[:, d, d:d + 1], 1.0 / DH)
            ins.then_inc(st("esel_ok"), 1)

            def load_state(j):
                src = (state_hgrn if j < 4 else state_gdn)[0, :, j % 4]
                pool.dma_start(SV(j), src.rearrange("b k v -> k b v")).then_inc(st(f"samp_in{j % 4}"), 16)

            load_state(2)
            load_state(3)
            pool.wait_ge(st("crow"), 1)
            pool.dma_start(conv_p[0, 0], CROW[0:3, :]).then_inc(st("conv_rows_out"), 16)
            pool.dma_start(conv_s[0, :, CONV - 2, :], CROW[3:11, :]).then_inc(st("conv_rows_out"), 16)
            pool.wait_ge(used, S_PROJ + 32)
            load_state(0)
            load_state(1)
            pool.wait_ge(st("hs2"), 1)
            store(hg_p[0, 0].rearrange("h k v -> k h v"), HS2.rearrange("p (h n) -> p h n", h=4))

            def store_state(j):
                pool.wait_ge(st("samp_new"), j + 1)
                dst = (hg_s if j < 4 else gdn_s)[0, :, j % 4]
                pool.dma_start(dst.rearrange("b k v -> k b v"), SV(j)).then_inc(st(f"samp_out{j % 4}"), 16)

            def reload(j):
                pool.wait_ge(st(f"samp_out{j % 4}"), 16)
                pool.wait_ge(st("samp_o_mm"), j - 3)
                load_state(j)

            store_state(0)
            store_state(1)
            reload(4)
            store_state(2)
            reload(5)
            store_state(3)
            reload(6)
            reload(7)
            pool.wait_ge(st("s2"), 1)
            store(gdn_p[0, 0].rearrange("h k v -> k h v"), S2[:, :, :])
            for j in range(4, 8):
                store_state(j)
            pool.wait_ge(x_done, 8 * 5)
            pool.dma_start(PBUFR[0:NSAMP * PBUF, 0:D], state_pool[0].rearrange("b r n -> (b r) n"))\
                .then_inc(st("pbuf_in"), 16)
            pool.wait_ge(st("prow"), 1)
            prows = C[:, 0:4, 0:256]
            store(pool_p[0, 0].rearrange("t (a n) -> t a n", a=4), prows[0:PBUF])
            store(pool_s[0, :, PBUF - 1, :].rearrange("t (a n) -> t a n", a=4), prows[PBUF:PBUF + NSAMP])
            pool.wait_ge(st("stored"), outs[0])
            for c in range(3):
                pool.wait_ge(st("y_ok"), c + 1)
                if c < CH:
                    store(y_prompt[0, c * P:(c + 1) * P, :], PTf[:, c * D:(c + 1) * D])
                else:
                    store(y_sample[:, 0, :], PTf[0:NSAMP, c * D:(c + 1) * D])
            pool.wait_ge(st("stored"), outs[0])


_INS = ["x_prompt", "x_sample", "state_hgrn", "state_gdn", "state_gdn_conv", "state_pool", "w_in_even",
        "hgrn_norm_w", "gdn_conv_w", "gdn_a_log", "gdn_dt_bias", "gdn_norm_w", "w_out_even", "pool_w_in",
        "pool_w_group", "pool_scale", "norm_ffn1", "ffn1_w_gate", "ffn1_w_up", "ffn1_w_down", "norm_mix",
        "norm_ffn2", "ffn2_w_gate", "ffn2_w_up", "ffn2_w_down", "final_norm"]
_OUTS = [(1, PROMPT, D), (NSAMP, 1, D), (1, 1, HEADS, DH, DH), (1, 1, HEADS, DH, DH), (1, 1, CONV - 1, 3 * MIX),
         (1, 1, PBUF, D), (1, NSAMP, HEADS, DH, DH), (1, NSAMP, HEADS, DH, DH), (1, NSAMP, CONV - 1, 3 * MIX),
         (1, NSAMP, PBUF, D)]


def kernel(**inputs):
    from concourse import bacc
    from concourse.bass_utils import run_bass_kernel_spmd

    nc = bacc.Bacc("TRN2", target_bir_lowering=False, num_devices=1)
    arrays, ins, outs = {}, [], []
    for name in _INS:
        a = np.ascontiguousarray(inputs[name])
        arrays[f"in_{name}"] = a
        ins.append(nc.dram_tensor(f"in_{name}", a.shape, mybir.dt.from_np(a.dtype), kind="ExternalInput").ap())
    for i, shape in enumerate(_OUTS):
        outs.append(nc.dram_tensor(f"out_{i}", shape, F32, kind="ExternalOutput").ap())
    build(nc, ins, outs)
    r = run_bass_kernel_spmd(nc, [arrays], core_ids=[0])
    return tuple(r.results[0][f"out_{i}"] for i in range(len(_OUTS)))
```

```python
from contextlib import ExitStack

import numpy as np
import concourse.bass as bass
from concourse import mybir

F32 = mybir.dt.float32
F32R = mybir.dt.float32r
BF16 = mybir.dt.bfloat16
U16 = mybir.dt.uint16
ALU = mybir.AluOpType
ACT = mybir.ActivationFunctionType

P = 128
EPS = 1e-6
PROMPT, NSAMP = 256, 8
TOK = PROMPT + NSAMP
CH = PROMPT // P
D, DFF = 1024, 2816
KD, KF = D // P, DFF // P
BLK = 256
NB = DFF // BLK
HEADS, DH = 4, 128
MIX = D // 2
CONV = 4
CT = 3 * MIX // P
WINDOWS = (2, 4, 8, 16)
PBUF = max(WINDOWS) - 1
PAD = PBUF + 1
LEVELS = 7
SLOT = 1024
RAW, SPL = 4, 4
LEAD = SPL - 1
READ = {1: 4, 2: 5, 4: 6, 5: 7}
GROUPS = (3, 2, 1, 0)
ORDER5 = (6, 7, 4, 5, 2, 3, 0, 1)
SSB = 0
FFN_SLOTS = NB * 4 + KF
PROJ = [10, 11, 8, 9, 12, 13, 2, 3, 0, 1, 4, 5, 6, 7, 14, 15]
WO = [(0, 0), (1, 0), (0, 1), (1, 1), (2, 0), (2, 1), (3, 0), (3, 1)]
S_FFN = [0, FFN_SLOTS + 40, 2 * FFN_SLOTS + 40, 3 * FFN_SLOTS + 48]
S_PROJ = FFN_SLOTS
S_WOUT = S_PROJ + 32
S_PIN = 3 * FFN_SLOTS + 40
TOTAL = 4 * FFN_SLOTS + 48
assert S_PIN + 8 == S_FFN[3] and S_FFN[3] + FFN_SLOTS == TOTAL
C_NORM, C_SCALE, C_CONV, C_HGN, C_GDN, NPAR = 0, 56, 64, 112, 113, 114


def build(nc, A, O_):
    (x_prompt, x_sample, state_hgrn, state_gdn, state_conv, state_pool, w_in, hgn, conv_w, a_log,
     dt_bias, gdn_n, w_out, pool_in, pool_grp, pool_scale, n_ffn1, f1g, f1u, f1d, n_mix, n_ffn2, f2g, f2u,
     f2d, n_fin) = A
    (y_prompt, y_sample, hg_p, gdn_p, conv_p, pool_p, hg_s, gdn_s, conv_s, pool_s) = O_
    FFN_W = [(f1g[0], f1u[0], f1d[0]), (f2g[0], f2u[0], f2d[0]),
             (f1g[1], f1u[1], f1d[1]), (f2g[1], f2u[1], f2d[1])]
    FFN_NORM = [0, 2, 3, 5]

    ctx = ExitStack()
    with ctx:
        def sb(name, shape, dt=F32, on=None):
            return (on or ctx).enter_context(nc.sbuf_tensor(name, shape, dt))

        def sem(name):
            return ctx.enter_context(nc.semaphore(name))

        raw = sb("raw", [P, RAW, SLOT])
        w_hi = sb("w_hi", [P, SPL, SLOT], F32R)
        w_lo = sb("w_lo", [P, SPL, SLOT], F32R)
        x = sb("x", [P, KD, TOK])
        hn = sb("hn", [P, KD, TOK])
        rstd = sb("rstd", [P, TOK])
        ident = sb("ident", [P, P])
        mean_w = sb("mean_w", [P, P])
        ones = sb("ones", [P, P])
        upper = sb("upper", [P, P])
        strict = sb("strict", [P, P])
        lvl = sb("lvl", [P, 2 * LEVELS + 1, P], BF16)
        par = sb("par", [P, NPAR])
        eps = sb("eps", [P, 1])
        WAB = sb("WAB", [P, KD, 8])
        SEL = sb("SEL", [P, 4, NSAMP])
        ab8 = sb("ab8", [8, 8])

        with ExitStack() as ffn_space:
            x_hi = sb("x_hi", [P, KD, TOK], F32R, ffn_space)
            x_lo = sb("x_lo", [P, KD, TOK], F32R, ffn_space)
            a_hi = sb("a_hi", [P, KF, TOK], F32R, ffn_space)
            a_lo = sb("a_lo", [P, KF, TOK], F32R, ffn_space)
            sg = sb("sg", [P, 2, TOK], on=ffn_space)
            pr = sb("pr", [P, 2, TOK], on=ffn_space)
        XH = sb("XH", [P, KD * TOK])
        XL = sb("XL", [P, KD * TOK])
        HS1, HS2, TOTS = XL[:, 0:512], XL[:, 512:1024], XL[:, 1024:2048]
        PT = sb("PT", [P, 32, TOK])
        C = sb("C", [P, CT, TOK])
        O = sb("O", [P, KD, TOK])
        DEC = sb("DEC", [P, 8, P])
        AT = sb("AT", [P, 8, P])
        with ExitStack() as xw_space:
            xw_hi = sb("xw_hi", [P, KD, TOK], F32R, xw_space)
            xw_lo = sb("xw_lo", [P, KD, TOK], F32R, xw_space)
        TU = sb("TU", [P, 16, P])
        T = TU[:, 0:8, :]
        U = TU[:, 8:16, :]
        CROW = TU[:, :, :].rearrange("p i n -> p (i n)")[:, 0:CT * P]
        XVK = sb("XVK", [P, 24, P])
        X = XVK[:, 0:8, :]
        VT = XVK[:, 8:16, :]
        KT = XVK[:, 16:24, :]
        VN = sb("VN", [P, 8, P])
        QE = sb("QE", [P, 4, P])
        S1 = sb("S1", [P, 4, P])
        S2 = sb("S2", [P, 4, P])
        PTf = PT[:, :, :].rearrange("p a b -> p (a b)")
        QP, KS = PTf[:, 16 * TOK:16 * TOK + 1024], PTf[:, 16 * TOK + 1024:16 * TOK + 2048]
        ATT = PTf[:, 16 * TOK + 2048:16 * TOK + 3072].rearrange("p (i n) -> p i n", n=P)
        HVT = PTf[:, 0:1024].rearrange("p (i n) -> p i n", n=P)
        HKT = PTf[:, 1024:2048].rearrange("p (i n) -> p i n", n=P)
        GG = sb("GG", [P, 4, TOK])
        SBUFS = sb("SBUFS", [P, 2, NSAMP, P])

        def SV(j):
            if j in (2, 3):
                return O[:, :, :].rearrange("p a t -> p (a t)")[:, (j - 2) * 1024:(j - 1) * 1024]\
                    .rearrange("p (b n) -> p b n", n=P)
            if j in (4, 5):
                return XH[:, (j - 4) * 1024:(j - 3) * 1024].rearrange("p (b n) -> p b n", n=P)
            return SBUFS[:, j % 2]

        RN = sb("RN", [8, TOK])
        esel = sb("esel", [P, 8, 8])
        emean = sb("emean", [P, 8, 8])
        qscale = sb("qscale", [8, 1])
        RN2 = sb("RN2", [4, TOK])
        KVH = sb("KVH", [P, 2, 32], F32R)
        KV3 = sb("KV3", [P, 2, 3, 32])
        KM = sb("KM", [96, HEADS, P], F32R)
        VM = sb("VM", [96, NSAMP, P], F32R)
        fold = sb("fold", [96, 32])
        headm = sb("headm", [96, HEADS])
        diagm = sb("diagm", [96, NSAMP])
        WV = sb("WV", [P, 5, 32])
        CB = sb("CB", [P, CT, 24])
        SMALL = sb("SMALL", [P, 384])
        cnt = sb("cnt", [P, 4, 16])
        rinv = sb("rinv", [P, 3])
        GB = XVK[0:8, :, :].rearrange("p i n -> p (i n)")[:, 0:8 * TOK].rearrange("p (a t) -> p a t", a=8)
        ROWS2 = O[:, :, :].rearrange("p a b -> p (a b)")
        PBUFR = SBUFS[:, :, :, :].rearrange("p a b n -> p (a b n)")
        ps = ctx.enter_context(nc.psum_tensor("ps", [P, 8, 512], F32))
        psA = ps[:, 4:6, :].rearrange("p b (i n) -> p (b i) n", n=P)
        psC = ps[:, 0:2, :].rearrange("p b (i n) -> p (b i) n", n=P)
        psD = ps[:, 2:4, :].rearrange("p b (i n) -> p (b i) n", n=P)
        psB = ps[:, 6:8, :].rearrange("p b (i n) -> p (b i) n", n=P)
        psAf, psCf = [ps[:, b:b + 2, :].rearrange("p b n -> p (b n)") for b in (4, 0)]
        Xf = X.rearrange("p i n -> p (i n)")

        raw_in = [sem(f"raw_in{r}") for r in range(RAW)]
        (hi_done, lo_done, used, silu_done, prod_done, ahi_done, alo_done, res_done,
         x_done, sq_done, ss_done, root_done, rstd_done, hn_done, xhi_done, xlo_done, xwhi_done, xwlo_done,
         gate_done, sg_done, p_ready, const_done,
         par_in, x_in, x_T, dve_chain, act_chain, pool_chain) = [sem(n) for n in (
             "hi_done", "lo_done", "used", "silu_done", "prod_done", "ahi_done",
             "alo_done", "res_done", "x_done", "sq_done", "ss_done", "root_done", "rstd_done", "hn_done", "xhi_done",
             "xlo_done", "xwhi_done", "xwlo_done", "gate_done", "sg_done", "p_ready", "const_done", "par_in",
             "x_in", "x_T", "dve_chain",
             "act_chain", "pool_chain")]
        stage_sem = {}

        def st(name):
            if name not in stage_sem:
                stage_sem[name] = sem(name)
            return stage_sem[name]

        prow = X[:, 0, :]
        rows = [(n_ffn1[0], 0), (n_mix[0], 1), (n_ffn2[0], 2), (n_ffn1[1], 3), (n_mix[1], 4), (n_ffn2[1], 5),
                (n_fin, 6), (pool_scale[0], 7)]

        block = ctx.enter_context(nc.Block())

        rstd2 = rstd[:, :].unsqueeze(1).broadcast_to([P, 2, TOK])

        def group_w(half):
            return (DEC, AT)[half][:, :, :].rearrange("p a b -> p (a b)").rearrange("p (a n) -> p a n", n=256)

        def sum_bank(n):
            return 2 if n == 5 else SSB

        def v(base, i, per):
            return base if i is None else base + i * per

        def samples_stored(eng, bufs=range(6)):
            for r in bufs:
                eng.wait_ge(st(f"samp_out{r}"), 32 if r < 2 else 16)

        def mixer_space_free(eng):
            eng.wait_ge(st("stored"), 16 * 3)
            eng.wait_ge(st("hs2_out"), 16)
            samples_stored(eng)

        def half_cols(flat, l, side):
            return flat.rearrange("p (j two r) -> p j two r", two=2, r=1 << l)[:, :, side, :]

        @block.sync
        def _(sp):
            def load(s, src, i=None):
                if s >= RAW:
                    sp.wait_ge(lo_done, v(s - RAW + 1, i, 8))
                sp.dma_start(raw[:, s % RAW, :], src).then_inc(raw_in[s % RAW], 16)

            def cols(w, half, c0):
                return w[half * 512:(half + 1) * 512, :].rearrange("(k p) n -> p k n", p=P)[:, :, bass.ds(c0, BLK)]

            def load4(s, src, i=None):
                if s >= RAW:
                    sp.wait_ge(lo_done, v(s - RAW + 1, i, 8))
                sp.dma_start(raw[:, s % RAW, :].rearrange("p (k n) -> p k n", k=4), src)\
                    .then_inc(raw_in[s % RAW], 16)

            def ffn(n):
                s0 = S_FFN[n]
                wg, wu, wd = FFN_W[n]
                for q in range(4):
                    load4(s0 + q, cols((wg, wu)[q // 2], (q + (n == 3)) % 2, 0))
                with sp.Fori(0, NB // 2) as i:
                    for q in range(8):
                        c0 = i * (2 * BLK) + (1 + q // 4) * BLK
                        load4(s0 + 4 + q, cols((wg, wu)[q // 2 % 2], q % 2, c0), i)
                s1 = s0 + 4 * NB
                for f in range(6):
                    load(s1 + f, wd[f * P:(f + 1) * P, :])
                with sp.Fori(0, (KF - 6) // 8) as i:
                    for q in range(8):
                        load(s1 + 6 + q, wd[bass.ds(i * (8 * P) + (6 + q) * P, P), :], i)

            for c in range(2):
                sp.dma_start(PTf[:, c * D:(c + 1) * D], x_prompt[0, c * P:(c + 1) * P, :]).then_inc(x_in, 16)
            sp.dma_start(PTf[0:NSAMP, 2 * D:3 * D], x_sample[:, 0, :]).then_inc(x_in, 16)
            for src, r in rows[4:]:
                sp.dma_start(prow[8 * r:8 * r + 8, :], src.rearrange("(k p) -> k p", p=P)).then_inc(par_in, 16)
            ffn(0)
            for n, b in enumerate(PROJ):
                for half in range(2):
                    load4(S_PROJ + 2 * n + half, cols(w_in[0], half, b * BLK))
            for q, (n, half) in enumerate(WO):
                load4(S_WOUT + q, cols(w_out[0], half, n * BLK))
            ffn(1)
            ffn(2)
            for q in range(8):
                load4(S_PIN + q, cols(pool_in[0], q % 2, (3 - q // 2) * BLK))
            ffn(3)
            for c in range(3):
                sp.wait_ge(st(f"y_ok{c % 2}"), c // 2 + 1)
                if c < CH:
                    sp.dma_start(y_prompt[0, c * P:(c + 1) * P, :], PTf[:, c * D:(c + 1) * D]).then_inc(st("y_out"), 16)
                else:
                    sp.dma_start(y_sample[:, 0, :], PTf[0:NSAMP, c * D:(c + 1) * D]).then_inc(st("y_out"), 16)
            sp.wait_ge(st("y_out"), 16 * 3)

        def even_scalar(act, tick, link, norm, normed):
            A = nc.scalar

            def slots(lo, hi):
                for q in range(lo, hi):
                    tick(S_PROJ + q)
                    if q % 2 == 0 and q > 4:
                        evac(q // 2 - 1)

            def evac(n):
                b = PROJ[n]
                act.wait_ge(used, S_PROJ + 2 * n + 2)
                if n == 2:
                    act.wait_ge(p_ready, 2)
                z = 2 * ((n + 1) % 2)
                A.copy(PT[:, 2 * b:2 * b + 2, :], ps[:, z:z + 2, 0:TOK]).then_inc(p_ready, 1)

            def tap0(c0):
                act.wait_ge(p_ready, c0 // 2 + 2 if c0 == 8 else (2 if c0 == 4 else 4))
                for c in range(c0, c0 + 4):
                    w = C_CONV + (CONV - 1) * CT + c
                    ins = A.activation(C[:, c, 0:PROMPT], PT[:, 16 + c, 0:PROMPT], ACT.Identity, scale=par[:, w:w + 1])
                ins.then_inc(st("tap0"), 1)

            normed(1, S_PROJ)
            slots(2, 6)
            act.wait_ge(st("conv_hist_T"), 1)
            A.copy(CB[:, :, :], ps[:, 6, 0:CT * 24].rearrange("p (c r) -> p c r", c=CT)).then_inc(st("conv_hist"), 1)
            tap0(4)
            act.wait_ge(st("gb_u"), 1)
            A.activation(GB[:, 6, :], GB[:, 7, :], ACT.Sigmoid).then_inc(st("beta"), 1)
            link(A.activation(GB[:, 1, :], GB[:, 0, :], ACT.Abs))
            link(A.activation(GB[:, 3, :], GB[:, 1, :], ACT.Exp, scale=-1.0))
            A.activation(ab8[:, 2:3], ab8[:, 1:2], ACT.Exp)
            A.activation(GB[:, 4, :], GB[:, 3, :], ACT.Ln, bias=1.0).then_inc(st("gb_ln"), 1)
            slots(6, 10)
            tap0(0)
            slots(10, 14)
            tap0(8)
            act.wait_ge(st("conv"), 1)
            A.activation(C[:, 0:8, :], C[:, 0:8, :], ACT.Silu).then_inc(st("conv_silu"), 1)
            slots(14, 15)
            act.wait_ge(st("conv_silu"), 1)
            A.activation(hn[:, :, :], C[:, 0:8, :], ACT.Square).then_inc(st("norm_sq"), 1)
            slots(15, 16)
            act.wait_ge(st("tok_T"), 1)
            A.copy(SMALL[:, 0:32], ps[:, 6, 0:32]).then_inc(st("gb_tok"), 1)
            act.wait_ge(st("conv"), 2)
            A.activation(C[:, 8:12, :], C[:, 8:12, :], ACT.Silu).then_inc(st("conv_silu"), 1)
            act.wait_ge(st("gb_rows_mm"), 1)
            A.activation(SMALL[:, 96:128], ps[:, 7, 0:32], ACT.Exp)
            A.copy(SMALL[:, 128:160], ps[:, 7, 32:64]).then_inc(st("bs"), 1)
            act.wait_ge(st("brow"), 1)
            A.activation(QE[:, :, :], psA[:, 4:8, :], ACT.Exp)
            A.activation(SMALL[:, 64:72], psA[:, :, P - 1], ACT.Exp).then_inc(st("ebl"), 1)
            slots(16, 18)
            act.wait_ge(st("ncum"), 1)
            A.activation(SMALL[:, 48:56], SMALL[:, 40:48], ACT.Exp, scale=-1.0).then_inc(st("ebt"), 1)
            act.wait_ge(st("dec_diff"), 1)
            A.activation(DEC[:, :, :], DEC[:, :, :], ACT.Exp).then_inc(st("dec_exp"), 1)
            act.wait_ge(st("norm_ss"), 1)
            A.activation(RN[:, 0:TOK], ps[0:8, 7, 0:TOK], ACT.Sqrt, bias=eps[0:8, 0:1]).then_inc(st("norm_root"), 1)
            slots(18, 22)

            def decay_state(j):
                act.wait_ge(st(f"samp_in{j if j < 6 else j - 6}"), 16 if j < 6 else 32)
                h = j % 4
                for b in range(NSAMP):
                    col = SMALL[:, 96 + 8 * h + b:97 + 8 * h + b] if j < 4 else GG[:, h, PROMPT + b:PROMPT + b + 1]
                    ins = A.activation(SV(j)[:, b, :], SV(j)[:, b, :], ACT.Identity, scale=col)
                ins.then_inc(st("samp_dec"), 1)

            act.wait_ge(st("bs"), 1)
            for j in range(4):
                decay_state(j)
                slots(22 + j, 23 + j)
            act.wait_ge(p_ready, 10)
            act.wait_ge(st("conv"), 2)
            act.wait_ge(st("crow_T"), 1)
            qa, fa = PT[:, 0:4, :], PT[:, 4:8, :]
            qpv = QP.rearrange("p (h t) -> p h t", h=4)
            ksv = KS.rearrange("p (h t) -> p h t", h=4)
            A.activation(GG[:, :, :], fa, ACT.Sigmoid)
            A.activation(ksv, fa[:, :, 0:PROMPT], ACT.Sigmoid, scale=-1.0)
            A.activation(SMALL[:, 192:224].rearrange("p (h b) -> p h b", h=4), fa[:, :, PROMPT:TOK],
                         ACT.Sigmoid, scale=-1.0)
            slots(26, 27)
            act.wait_ge(st("vt_T"), 1)
            A.copy(VT[:, :, :], psB).then_inc(st("vt"), 1)
            slots(27, 28)
            A.activation(qpv, qa[:, :, 0:PROMPT], ACT.Silu)
            A.activation(SMALL[:, 224:256].rearrange("p (h b) -> p h b", h=4), qa[:, :, PROMPT:TOK],
                         ACT.Silu).then_inc(st("hg_in"), 1)
            slots(28, 31)
            act.wait_ge(st("hvt_T"), 1)
            act.wait_ge(st("hg_in"), 1)
            A.copy(HVT, psD).then_inc(st("hvt"), 1)
            act.wait_ge(st("samp_vn"), 1)
            A.copy(KVH[:, 0, :].rearrange("p (h b) -> p h b", h=4), C[:, 4:8, PROMPT:TOK])
            A.copy(KVH[:, 1, :], WV[:, 0, :]).then_inc(st("kv_hi"), 1)
            slots(31, 32)
            evac(15)

            gates = [lambda: A.activation(PT[:, 12:16, :], PT[:, 12:16, :], ACT.Sigmoid),
                     lambda: A.activation(PT[:, 28:32, :], PT[:, 28:32, :], ACT.Silu).then_inc(st("gates"), 1)]
            for l in range(1, LEVELS):
                act.wait_ge(st("inv_x"), l)
                if l == 1:
                    act.wait_ge(st("inv"), 1)
                A.copy(half_cols(Xf, l, 0), half_cols(psAf, l, 0)).then_inc(st("inv_xc"), 1)
                if l == 3:
                    gates[0]()
                if l == 1:
                    act.wait_ge(st("kv3"), 1)
                    A.copy(KVH[:, 0, :], SMALL[:, 192:224])
                    A.copy(KVH[:, 1, :].rearrange("p (h b) -> p h b", h=4), PT[:, 8:12, PROMPT:TOK])\
                        .then_inc(st("kv_hi"), 1)
                if l == LEVELS - 1:
                    gates[1]()
                    act.wait_ge(st("gates"), 1)
                    A.activation(PT[:, 12:16, :], PT[:, 12:16, :], ACT.Identity, scale=par[:, C_HGN:C_HGN + 1])
                    A.activation(PT[:, 28:32, :], PT[:, 28:32, :], ACT.Identity, scale=par[:, C_GDN:C_GDN + 1])\
                        .then_inc(st("gates"), 1)
                if l in READ:
                    decay_state(READ[l])
                if l < LEVELS - 1:
                    act.wait_ge(st("inv_u"), l)
                    A.copy(U[:, :, :], psC).then_inc(st("inv"), 1)
            act.wait_ge(st("hkt_T"), 1)
            A.copy(HKT, psC).then_inc(st("hkt"), 1)
            act.wait_ge(st("hs1_mm"), 1)
            A.copy(HS1, ps[:, 2, :]).then_inc(st("hs1"), 1)
            act.wait_ge(st("s1_mm"), 1)
            A.copy(S1[:, :, :], psA[:, 0:4, :]).then_inc(st("s1"), 1)
            act.wait_ge(st("ho_mm"), 1)
            samples_stored(act, (2, 3))
            A.copy(O[:, 0:4, 0:PROMPT], psC.rearrange("p (h c) t -> p h (c t)", h=4)).then_inc(st("o_a"), 1)
            act.wait_ge(st("o_a"), 1)
            act.wait_ge(st("so"), 2)
            act.wait_ge(st("norm_ss"), 1)
            A.activation(hn[:, 0:4, :], O[:, 0:4, :], ACT.Square).then_inc(st("norm_sq"), 1)
            act.wait_ge(st("norm_ss"), 2)
            act.wait_ge(st("qk_n"), 2)
            A.activation(RN[0:4, :], ps[0:4, 0, 0:TOK], ACT.Sqrt, bias=eps[0:4, 0:1]).then_inc(st("norm_root"), 1)
            act.wait_ge(st("o_mm"), 1)
            A.copy(O[:, 4:8, 0:P], psA[:, 0:4, :])
            A.copy(O[:, 4:8, P:2 * P], psA[:, 4:8, :]).then_inc(st("o_b"), 1)
            act.wait_ge(st("o_b"), 1)
            A.activation(hn[:, 4:8, :], O[:, 4:8, :], ACT.Square).then_inc(st("norm_sq"), 1)
            act.wait_ge(st("norm_ss"), 3)
            A.activation(RN2[:, :], ps[0:4, 6, 0:TOK], ACT.Sqrt, bias=eps[0:4, 0:1]).then_inc(st("norm_root"), 1)
            samples_stored(act, (4, 5))
            for k in range(KD):
                if k % 4 == 0:
                    act.wait_ge(st("o_norm"), 2 * (k // 4) + 2)
                A.copy(x_hi[:, k, :], O[:, k, :]).then_inc(st("o_hi"), 1)
            for q in range(8):
                tick(S_WOUT + q)
                if q in (3, 4):
                    norm(2, range(2 * q - 6, 2 * q - 4))
            norm(2, range(4, 8))

        def odd_scalar(act, tick, norm, root):
            tick(S_PIN)
            root(4)
            for q in range(1, 4):
                tick(S_PIN + q)
            for q in range(4, 8):
                tick(S_PIN + q)
            act.wait_ge(st("prow_T"), 1)
            nc.scalar.copy(C[0:23, 0:4, 0:256], ps[0:23, 0:2, :].rearrange("p b (i n) -> p (b i) n", n=256))\
                .then_inc(st("prow"), 1)
            norm(5)

        @block.scalar
        def _(act):
            chain = [0]

            def link(ins):
                chain[0] += 1
                ins.then_inc(act_chain, 1)
                act.wait_ge(act_chain, chain[0])

            def tick(s, i=None):
                w = s + LEAD
                if w >= TOTAL:
                    return
                if w >= SPL:
                    act.wait_ge(used, v(w - SPL + 1, i, 8))
                act.wait_ge(raw_in[w % RAW], v(16 * (w // RAW + 1), i, 16 * 8 // RAW))
                nc.scalar.copy(w_hi[:, w % SPL, :], raw[:, w % RAW, :]).then_inc(hi_done, 1)

            def square(n, z, d):
                act.wait_ge(x_done, 8 * n + z + 1)
                nc.scalar.activation(hn[:, d, :], x[:, d, :], ACT.Square).then_inc(sq_done, 1)

            def round_h(k):
                act.wait_ge(hn_done, k + 1)
                nc.scalar.copy(x_hi[:, k, :], hn[:, k, :]).then_inc(xhi_done, 1)

            def norm(n, tiles=range(KD)):
                for z in tiles:
                    d = ORDER5[z] if n == 5 else z
                    square(n, z, d)
                    out = xw_hi[:, d, :] if n < 6 else XH[:, d * TOK:(d + 1) * TOK]
                    nc.scalar.activation(out, x[:, d, :], ACT.Identity,
                                         scale=par[:, 8 * n + d:8 * n + d + 1]).then_inc(xwhi_done, 1)

            def root(n):
                act.wait_ge(ss_done, n + 1)
                nc.scalar.activation(rstd[:, :], ps[:, sum_bank(n), 0:TOK], ACT.Sqrt, bias=eps[:, 0:1])\
                    .then_inc(root_done, 1)

            def normed(n, s):
                tick(s)
                root(n)
                for k in range(KD):
                    round_h(k)
                    if k == 3:
                        tick(s + 1)

            def ffn(n):
                s0, b0 = S_FFN[n], NB * n

                def silu(b, i=None):
                    act.wait_ge(gate_done, v(b + 1, i, 2))
                    if b:
                        act.wait_ge(prod_done, v(b, i, 2))
                    nc.scalar.activation(sg[:, :, :], pr[:, :, :], ACT.Silu).then_inc(silu_done, 1)

                def round_a(b, i=None):
                    act.wait_ge(prod_done, v(b + 1, i, 2))
                    f = 2 * (b - b0) if i is None else i * 4 + 2 * (b - b0)
                    nc.scalar.copy(a_hi[:, bass.ds(f, 2), :], pr[:, :, :]).then_inc(ahi_done, 1)

                def blk(b, i=None):
                    s = s0 + 4 * (b - b0)
                    tick(s, i)
                    if b > b0:
                        round_a(b - 1, i)
                    else:
                        root(FFN_NORM[n])
                    tick(s + 1, i)
                    tick(s + 2, i)
                    silu(b, i)
                    tick(s + 3, i)

                blk(b0)
                with act.Fori(0, NB // 2) as i:
                    blk(b0 + 1, i)
                    blk(b0 + 2, i)
                s1 = s0 + 4 * NB
                tick(s1)
                round_a(b0 + NB - 1)
                for f in range(1, 5):
                    tick(s1 + f)
                with act.Fori(0, 2 if n < 3 else 1) as i:
                    for f in range(5, 13):
                        tick(s1 + f, i)
                for f in range(13, KF - 1 if n == 3 else 13):
                    tick(s1 + f)
                norm(FFN_NORM[n] + 1)
                tick(s1 + KF - 1)

            for src, r in rows[:4]:
                act.dma_start(prow[8 * r:8 * r + 8, :], src.rearrange("(k p) -> k p", p=P)).then_inc(par_in, 16)
            for s in range(-LEAD, 0):
                tick(s)
            act.wait_ge(x_T, 3)
            nc.scalar.copy(par[:, :], ps[:, 7, 0:NPAR]).then_inc(st("par_ok"), 1)
            act.wait_ge(st("par_ok"), 1)
            act.wait_ge(const_done, 1)
            norm(0)
            ffn(0)
            even_scalar(act, tick, link, norm, normed)
            mixer_space_free(act)
            ffn(1)
            ffn(2)
            odd_scalar(act, tick, norm, root)
            act.wait_ge(st("stored"), 16 * 5)
            ffn(3)
            root(6)
            act.wait_ge(rstd_done, 7)
            for c in (0, 2):
                n = P if c < CH else NSAMP
                act.wait_ge(st("y_T"), c + 1)
                nc.scalar.activation(PTf[0:n, c * D:(c + 1) * D].rearrange("p (a b) -> p a b", a=2),
                                     ps[0:n, 2 + 2 * c:4 + 2 * c, :], ACT.Identity, scale=rinv[0:n, c:c + 1])\
                    .then_inc(st(f"y_ok{c % 2}"), 1)

        def even_vector(dve, tick, link, residual, weighted, normed):
            V = nc.vector

            def slots(lo, hi):
                for q in range(lo, hi):
                    tick(S_PROJ + q)

            def conv(c0, n):
                dve.wait_ge(st("tap0"), n)
                for j in range(CONV - 2, -1, -1):
                    back = CONV - 1 - j
                    for c in range(c0, c0 + 4):
                        w = C_CONV + j * CT + c
                        ins = V.scalar_tensor_tensor(C[:, c, back:PROMPT], PT[:, 16 + c, 0:PROMPT - back],
                                                     par[:, w:w + 1], C[:, c, back:PROMPT], ALU.mult, ALU.add)
                    if j:
                        link(ins)
                return ins

            def evac(n):
                dve.wait_ge(used, S_PROJ + 2 * n + 2)
                b, z = PROJ[n], 2 * ((n + 1) % 2)
                V.tensor_tensor(PT[:, 2 * b:2 * b + 2, :], ps[:, z:z + 2, 0:TOK], rstd2, ALU.mult)\
                    .then_inc(p_ready, 1)

            normed(1, S_PROJ, evac)
            slots(2, 4)
            evac(1)
            slots(4, 6)
            dve.wait_ge(st("gb_mm"), 1)
            dve.wait_ge(st("ab_in"), 48)
            dve.wait_ge(st("consts"), 2)
            link(V.tensor_copy(GB[:, 7, :], ps[0:8, 7, 0:TOK]))
            V.tensor_scalar(GB[:, 0, :], GB[:, 7, :], ab8[:, 0:1], None, ALU.add).then_inc(st("gb_u"), 1)
            dve.wait_ge(st("gb_u"), 1)
            link(V.tensor_scalar(GB[:, 2, :], GB[:, 0, :], 0.0, None, ALU.max))
            link(conv(4, 1))
            slots(6, 8)
            dve.wait_ge(st("gb_ln"), 1)
            link(V.tensor_tensor(GB[:, 2, :], GB[:, 2, :], GB[:, 4, :], ALU.add))
            V.tensor_scalar(GB[:, 5, :], GB[:, 2, :], ab8[:, 2:3], -1.0, ALU.mult, ALU.mult).then_inc(st("gb_g"), 1)
            slots(8, 10)
            link(conv(0, 2))
            slots(10, 12)
            dve.wait_ge(st("conv_hist"), 1)
            dve.wait_ge(p_ready, 6)

            def wall(j):
                return par[:, C_CONV + j * CT:C_CONV + (j + 1) * CT].unsqueeze(2).broadcast_to([P, CT, NSAMP])
            cs = C[:, :, PROMPT:TOK]
            hist = CB[:, :, :].rearrange("p c (b r) -> p c b r", r=CONV - 1)
            tmp = SMALL[:, 256:256 + CT * NSAMP].rearrange("p (c b) -> p c b", c=CT)
            link(V.tensor_tensor(cs, PT[:, 16:28, PROMPT:TOK], wall(CONV - 1), ALU.mult))
            for j in range(CONV - 1):
                link(V.tensor_tensor(tmp, hist[:, :, :, j], wall(j), ALU.mult))
                ins = V.tensor_tensor(cs, cs, tmp, ALU.add)
                if j < CONV - 2:
                    link(ins)
            ins.then_inc(st("conv"), 1)
            slots(12, 14)
            dve.wait_ge(st("conv"), 1)
            conv(8, 3).then_inc(st("conv"), 1)
            dve.wait_ge(st("crow_T"), 1)
            V.tensor_copy(CROW[0:11, :].rearrange("p (b n) -> p b n", n=512), ps[0:11, 4:7, :]).then_inc(st("crow"), 1)
            slots(14, 16)
            dve.wait_ge(st("gb_tok"), 1)
            tokv = SMALL[:, 0:32].rearrange("p (c y j) -> p c y j", c=2, y=2)
            beta = SMALL[:, 56:64]
            V.tensor_copy(beta.rearrange("p (c h) -> p c h", c=2), tokv[:, :, 1, 4:8])
            link(V.tensor_scalar(SMALL[:, 72:80].rearrange("p (c h) -> p c h", c=2), tokv[:, :, 1, 4:8], -1.0,
                                 None, ALU.mult))
            dve.wait_ge(st("cum_mm"), 1)
            V.tensor_scalar(SMALL[:, 40:48], ps[:, 6, 32:40], -1.0, None, ALU.mult).then_inc(st("ncum"), 1)
            dve.wait_ge(st("ncum"), 1)
            dve.wait_ge(st("ebl"), 1)
            for i in range(8):
                ins = V.tensor_scalar(DEC[:, i, :], psA[:, i, :], SMALL[:, 40 + i:41 + i], 0.0, ALU.add, ALU.min)
            ins.then_inc(st("dec_diff"), 1)
            slots(16, 18)
            dve.wait_ge(st("norm_root"), 1)
            link(V.reciprocal(RN[:, 0:TOK], RN[:, 0:TOK]))
            V.tensor_scalar(RN[:, 0:TOK], RN[:, 0:TOK], qscale[:, 0:1], None, ALU.mult).then_inc(st("norm_r"), 1)
            slots(18, 20)
            dve.wait_ge(st("dec_exp"), 1)
            link(V.tensor_copy(SMALL[:, 80:88], DEC[:, :, P - 1]))
            link(V.tensor_tensor(AT[:, :, :], DEC[:, :, :], strict[:, :].unsqueeze(1).broadcast_to([P, 8, P]),
                                 ALU.mult))
            link(V.tensor_tensor(DEC[:, :, :], DEC[:, :, :], upper[:, :].unsqueeze(1).broadcast_to([P, 8, P]),
                                 ALU.mult))
            for y, t0 in ((0, 4), (1, 0)):
                dve.wait_ge(st("norm_bc"), y + 1)
                V.tensor_tensor(C[:, t0:t0 + 4, :], C[:, t0:t0 + 4, :], ps[:, 4:8, 0:TOK], ALU.mult)\
                    .then_inc(st("qk_n"), 1)
                slots(20 + y, 21 + y)
            slots(22, 24)
            dve.wait_ge(st("kk_mm"), 1)
            for i in range(8):
                ins = V.scalar_tensor_tensor(AT[:, i, :], psA[:, i, :], SMALL[:, 72 + i:73 + i], AT[:, i, :],
                                             ALU.mult, ALU.mult)
            ins.then_inc(st("at"), 1)
            slots(24, 25)
            dve.wait_ge(st("kq_mm"), 1)
            V.tensor_tensor(DEC[:, :, :], DEC[:, :, :], psB, ALU.mult).then_inc(st("aqk"), 1)
            slots(25, 26)
            dve.wait_ge(st("ebl"), 1)
            dve.wait_ge(st("qk_n"), 2)
            V.tensor_tensor(QE[:, :, :], QE[:, :, :], C[:, 0:4, P:2 * P], ALU.mult).then_inc(st("qe"), 1)
            smp = slice(PROMPT, TOK)

            def hb(ap):
                return ap.rearrange("p (h b) -> p h b", h=4)
            vn, kq, tmp2 = WV[:, 0, :], WV[:, 1, :], WV[:, 2, :]
            V.tensor_tensor(hb(kq), C[:, 4:8, smp], C[:, 0:4, smp], ALU.mult).then_inc(st("samp_kq"), 1)
            rd = ps[:, 7, 32:96].rearrange("p (h b y) -> p h b y", h=4, y=2)

            def kv_parts(y, keys, values):
                dve.wait_ge(st("kv_hi"), y + 1)
                if y:
                    dve.wait_ge(st("kv_T"), 1)
                hi = KVH[:, :, :].bitcast(F32)
                k3, v3 = KV3[:, 0], KV3[:, 1]
                V.tensor_copy(k3[:, 0:2, :], hi[:, 0, :].unsqueeze(1).broadcast_to([P, 2, 32]))
                V.tensor_copy(v3[:, 0:3:2, :], hi[:, 1, :].unsqueeze(1).broadcast_to([P, 2, 32]))
                V.tensor_tensor(hb(k3[:, 2, :]), keys, hb(hi[:, 0, :]), ALU.subtract)
                V.tensor_tensor(hb(v3[:, 1, :]), values, hb(hi[:, 1, :]), ALU.subtract).then_inc(st("kv3"), 1)

            def kv_rows(y):
                dve.wait_ge(st("kv_T"), y + 1)
                if y:
                    dve.wait_ge(st("samp_outer"), 4)
                V.tensor_tensor(KM[:, :, :], ps[0:96, 7, 256:384].unsqueeze(1).broadcast_to([96, HEADS, P]),
                                headm[:, :].unsqueeze(2).broadcast_to([96, HEADS, P]), ALU.mult)
                V.tensor_tensor(VM[:, :, :], ps[0:96, 7, 384:512].unsqueeze(1).broadcast_to([96, NSAMP, P]),
                                diagm[:, :].unsqueeze(2).broadcast_to([96, NSAMP, P]), ALU.mult)\
                    .then_inc(st("kv_rows"), 1)
            idb = ident[:, :].unsqueeze(1).broadcast_to([P, 8, P])

            def mask(m):
                return lvl[:, m, :].bitcast(U16).unsqueeze(1).broadcast_to([P, 8, P])
            dve.wait_ge(st("conv_rows_out"), 32)
            V.tensor_copy(T[:, :, :], idb)
            slots(26, 27)
            link(V.tensor_copy(U[:, :, :], idb))
            slots(27, 28)
            dve.wait_ge(st("at"), 1)
            V.copy_predicated(U[:, :, :], mask(0), AT[:, :, :])
            slots(28, 29)
            dve.wait_ge(st("a_T"), 1)
            V.copy_predicated(T[:, :, :], mask(LEVELS), psA).then_inc(st("inv_tc"), 1)
            dve.wait_ge(st("tok_T"), 1)
            dve.wait_ge(st("gb_rows_mm"), 1)
            V.memset(X[:, :, :], 0.0).then_inc(st("inv"), 1)
            slots(29, 30)
            dve.wait_ge(st("hg_in"), 1)
            link(V.tensor_scalar(SMALL[:, 224:256], SMALL[:, 224:256], DH ** -0.5, None, ALU.mult))
            V.tensor_tensor(WV[:, 3, :], SMALL[:, 192:224], SMALL[:, 224:256], ALU.mult).then_inc(st("samp_kq"), 1)
            V.tensor_scalar(QP, QP, DH ** -0.5, None, ALU.mult).then_inc(st("hg_q"), 1)
            slots(30, 31)
            V.memset(ATT[:, :, :], 0.0).then_inc(st("hg_merge"), 1)
            dve.wait_ge(st("samp_read"), 4)
            link(V.tensor_tensor(hb(tmp2), C[:, 8:12, smp], rd[:, :, :, 1], ALU.subtract))
            V.tensor_tensor(vn, tmp2, SMALL[:, 128:160], ALU.mult).then_inc(st("samp_vn"), 1)
            kv_parts(0, C[:, 4:8, smp], hb(vn))
            slots(31, 32)

            g = GG[:, :, 0:PROMPT]
            tots = []

            def level_update(l):
                half = 1 << l
                n = 1024 // (2 * half)
                off = sum(1024 >> (m + 1) for m in range(l))
                if l == 0:
                    gv = g.rearrange("p h (j two) -> p h j two", two=2)
                    left, right = gv[:, :, :, 0], gv[:, :, :, 1]
                    nxt = TOTS[:, 0:n].rearrange("p (h j) -> p h j", h=4)
                    q4 = QP.rearrange("p (h j two) -> p h j two", h=4, two=2)[:, :, :, 1]
                    k4 = KS.rearrange("p (h j two) -> p h j two", h=4, two=2)[:, :, :, 0]
                    lb, rb = left, right
                else:
                    tv = tots[-1].rearrange("p (j two) -> p j two", two=2)
                    left, right, nxt = tv[:, :, 0], tv[:, :, 1], TOTS[:, off:off + n]
                    q4 = QP.rearrange("p (j two r) -> p j two r", two=2, r=half)[:, :, 1, :]
                    k4 = KS.rearrange("p (j two r) -> p j two r", two=2, r=half)[:, :, 0, :]
                    lb = left.unsqueeze(2).broadcast_to([P, n, half])
                    rb = right.unsqueeze(2).broadcast_to([P, n, half])
                V.tensor_tensor(q4, q4, lb, ALU.mult)
                V.tensor_tensor(k4, k4, rb, ALU.mult)
                V.tensor_tensor(nxt, left, right, ALU.mult).then_inc(st("hg_lvl"), 1)
                tots.append(TOTS[:, off:off + n])

            dve.wait_ge(used, S_PROJ + 32)
            def halves(m, l, side):
                return half_cols(lvl[:, m, :].bitcast(U16), l, side).unsqueeze(1)\
                    .broadcast_to([P, 8, P >> (l + 1), 1 << l])

            def merge(tile, m, l, side, flat):
                return V.copy_predicated(
                    tile.rearrange("p i (j two r) -> p i j two r", two=2, r=1 << l)[:, :, :, side, :],
                    halves(m, l, side),
                    flat.rearrange("p (i j two r) -> p i j two r", i=8, two=2, r=1 << l)[:, :, :, side, :])

            def new_state(j):
                dve.wait_ge(st("samp_dec"), j + 1)
                dve.wait_ge(st("samp_outer"), j + 1)
                V.tensor_tensor(SV(j), SV(j), psD, ALU.add).then_inc(st("samp_new"), 1)

            kv_rows(0)
            for r in range(LEVELS + 1):
                dve.wait_ge(st("hg_att"), r + 1)
                if r == 0:
                    dve.wait_ge(st("hg_merge"), 1)
                    V.copy_predicated(ATT[:, :, :], mask(2 * LEVELS), psC).then_inc(st("hg_merge"), 1)
                    V.tensor_tensor(QP.rearrange("p (h t) -> p h t", h=4), QP.rearrange("p (h t) -> p h t", h=4), g,
                                    ALU.mult).then_inc(st("hg_lvl"), 1)
                else:
                    dve.wait_ge(st("hg_lvl"), r)
                    dve.wait_ge(st("hg_merge"), r + 1)
                    merge(ATT, r - 1, r - 1, 1, psCf).then_inc(st("hg_merge"), 1)
                if 1 <= r < LEVELS - 1:
                    dve.wait_ge(st("inv_t"), r)
                    merge(T, LEVELS + r, r, 0, psAf).then_inc(st("inv_tc"), 1)
                elif r == LEVELS - 1:
                    dve.wait_ge(st("inv_u"), r)
                    dve.wait_ge(st("inv"), r)
                    merge(U, r, r, 1, psAf).then_inc(st("inv"), 1)
                if r:
                    level_update(r - 1)
                new_state(r)
                if r == 1:
                    kv_parts(1, hb(SMALL[:, 192:224]), PT[:, 8:12, smp])
                if r == 3:
                    kv_rows(1)
            dve.wait_ge(st("kt_T"), 1)
            V.tensor_tensor(KT[:, :, :], psA, SMALL[:, 80:88].unsqueeze(2).broadcast_to([P, 8, P]), ALU.mult)\
                .then_inc(st("kt"), 1)
            dve.wait_ge(st("vn0_mm"), 1)
            V.tensor_tensor(VN[:, 0:4, :], psB[:, 0:4, :], beta[:, 0:4].unsqueeze(2).broadcast_to([P, 4, P]), ALU.mult)\
                .then_inc(st("vn0"), 1)
            samples_stored(dve, (2, 3))
            dve.wait_ge(st("samp_kq_mm"), 2)
            dve.wait_ge(st("samp_read"), 8)
            V.tensor_tensor(WV[:, 2, :], ps[:, 7, 128:160], vn, ALU.mult)
            link(V.tensor_tensor(hb(WV[:, 4, :]), hb(ps[:, 7, 160:192]), PT[:, 8:12, smp], ALU.mult))
            V.tensor_tensor(O[:, 4:8, smp], rd[:, :, :, 0], hb(WV[:, 2, :]), ALU.add).then_inc(st("so"), 1)
            V.tensor_tensor(O[:, 0:4, smp], hb(ps[:, 7, 0:32]), hb(WV[:, 4, :]), ALU.add).then_inc(st("so"), 1)
            totc = tots[-1].rearrange("p (h c) -> p h c", h=4)[:, :, 1:2].broadcast_to([P, 4, P])
            hs1v, hs2v = [a.rearrange("p (h n) -> p h n", h=4) for a in (HS1, HS2)]
            dve.wait_ge(st("hs1"), 1)
            dve.wait_ge(st("hg_lvl"), LEVELS + 1)
            link(V.tensor_tensor(hs2v, hs1v, totc, ALU.mult))
            dve.wait_ge(st("hs2_mm"), 1)
            V.tensor_tensor(HS2, HS2, ps[:, 3, :], ALU.add).then_inc(st("hs2"), 1)
            dve.wait_ge(st("ks_mm"), 1)
            dve.wait_ge(st("ebt"), 1)
            link(V.tensor_tensor(VN[:, 4:8, :], psA[:, 4:8, :],
                                 SMALL[:, 52:56].unsqueeze(2).broadcast_to([P, 4, P]), ALU.mult))
            V.tensor_tensor(VT[:, 4:8, :], VT[:, 4:8, :], VN[:, 4:8, :], ALU.subtract).then_inc(st("rhs1"), 1)
            dve.wait_ge(st("vn1_mm"), 1)
            dve.wait_ge(st("rhs1"), 1)
            V.tensor_tensor(VN[:, 4:8, :], psB[:, 0:4, :], beta[:, 4:8].unsqueeze(2).broadcast_to([P, 4, P]), ALU.mult)\
                .then_inc(st("vn1"), 1)
            link(V.tensor_tensor(S2[:, :, :], S1[:, :, :], SMALL[:, 68:72].unsqueeze(2).broadcast_to([P, 4, P]),
                                 ALU.mult))
            def gated(y):
                o, gate = O[:, 4 * y:4 * y + 4, :], PT[:, 12 + 16 * y:16 + 16 * y, :]
                dve.wait_ge(st("norm_root"), y + 2)
                if y:
                    dve.wait_ge(st("gates"), 2)
                f = RN2[:, :] if y else RN[0:4, :]
                V.reciprocal(f, f).then_inc(st("norm_r"), 1)
                dve.wait_ge(st("norm_bc"), y + 3)
                V.tensor_tensor(o, o, ps[:, 4 * y:4 * y + 4, 0:TOK], ALU.mult).then_inc(st("o_norm"), 1)
                dve.wait_ge(st("gates"), 2)
                dve.wait_ge(st("o_norm"), 2 * y + 1)
                V.tensor_tensor(o, o, gate, ALU.mult).then_inc(st("o_norm"), 1)
                for k in range(4 * y, 4 * y + 4):
                    dve.wait_ge(st("o_hi"), k + 1)
                    V.tensor_tensor(x_lo[:, k, :], O[:, k, :], x_hi[:, k, :].bitcast(F32), ALU.subtract)\
                        .then_inc(st("o_lo"), 1)

            dve.wait_ge(st("hs2_out"), 16)
            gated(0)
            dve.wait_ge(st("s2_mm"), 1)
            V.tensor_tensor(S2[:, :, :], S2[:, :, :], psB[:, 4:8, :], ALU.add).then_inc(st("s2"), 1)
            gated(1)

            def out_ended(d):
                return used, S_WOUT + WO.index((d // 2, 1)) + 1
            for q in range(8):
                tick(S_WOUT + q)
                if q in (3, 4, 6):
                    residual(1.0, out_ended, None, {3: range(0, 2), 4: range(2, 4), 6: range(4, 6)}[q])
                if q in (4, 6):
                    for d in range(q - 4, q - 2):
                        weighted(2, d)
            residual(1.0, out_ended, None, range(6, 8))
            for d in range(4, 8):
                weighted(2, d)

        def odd_vector(dve, tick, link, residual, root_inverse):
            V = nc.vector
            W = PAD + TOK
            up = PTf[:, 0:KD * W].rearrange("p (k t) -> p k t", k=KD)
            wa = PTf[:, KD * W:2 * KD * W].rearrange("p (k t) -> p k t", k=KD)
            wb = PTf[:, 2 * KD * W:3 * KD * W].rearrange("p (k t) -> p k t", k=KD)
            dve.wait_ge(x_done, 8 * 5)
            tick(S_PIN)
            root_inverse(4)
            link(V.memset(up[:, :, 0:PAD], 0.0))
            tick(S_PIN + 1)
            dve.wait_ge(st("pool_hist"), 1)
            V.tensor_copy(SMALL[:, 64:128], ps[:, 1, 0:64]).then_inc(st("hist_sums"), 1)
            end = PAD + PROMPT

            for m, gi in enumerate(GROUPS):
                pair, w = slice(2 * gi, 2 * gi + 2), WINDOWS[gi]
                dve.wait_ge(used, S_PIN + 2 * m + 2)
                z = (2 * m + 2) % 8
                V.tensor_tensor(up[:, pair, PAD:], ps[:, z:z + 2, 0:TOK], rstd2, ALU.mult).then_inc(st("pool_u"), 1)
                dve.wait_ge(st("pool_u"), m + 1)
                if m < 3:
                    tick(S_PIN + 2 * m + 2)
                src, dst = up, wa
                for step in range(gi + 1):
                    back = 1 << step
                    lo = 2 * back - 1
                    link(V.tensor_tensor(dst[:, pair, lo:end], src[:, pair, lo:end], src[:, pair, lo - back:end - back],
                                         ALU.add))
                    src, dst = dst, (wb if dst is wa else wa)
                win = src[:, pair, PAD:PAD + PROMPT]
                u = up[:, pair, PAD:PAD + PROMPT]
                out = hn[:, pair, :]
                V.scalar_tensor_tensor(out[:, :, 16:PROMPT], win[:, :, 16:], 1.0 / w, u[:, :, 16:], ALU.mult,
                                       ALU.subtract)
                us = up[:, pair, PAD + PROMPT:]
                hs = SMALL[:, 64 + 16 * gi:80 + 16 * gi].rearrange("p (k b) -> p k b", k=2)
                V.tensor_tensor(out[:, :, 0:16], win[:, :, 0:16],
                                cnt[:, gi, :].unsqueeze(1).broadcast_to([P, 2, 16]), ALU.mult)
                dve.wait_ge(st("hist_sums"), 1)
                link(V.tensor_tensor(hs, hs, us, ALU.add))
                V.tensor_tensor(out[:, :, 0:16], out[:, :, 0:16], u[:, :, 0:16], ALU.subtract)
                V.scalar_tensor_tensor(out[:, :, PROMPT:TOK], hs, 1.0 / w, us, ALU.mult, ALU.subtract)\
                    .then_inc(st("pool_d"), 1)
                if m < 3:
                    tick(S_PIN + 2 * m + 3)
            residual(par[:, C_SCALE:C_SCALE + 8], lambda d: (st("group_done"), GROUPS.index(d // 2) + 1), 5)

        @block.vector
        def _(dve):
            chain = [0]

            def link(ins):
                chain[0] += 1
                ins.then_inc(dve_chain, 1)
                dve.wait_ge(dve_chain, chain[0])

            def tick(s, i=None):
                w = s + LEAD
                if w >= TOTAL:
                    return
                dve.wait_ge(hi_done, v(w + 1, i, 8))
                nc.vector.tensor_tensor(w_lo[:, w % SPL, :], raw[:, w % RAW, :],
                                        w_hi[:, w % SPL, :].bitcast(F32), ALU.subtract).then_inc(lo_done, 1)

            def lo_h(k):
                dve.wait_ge(xhi_done, k + 1)
                nc.vector.tensor_tensor(x_lo[:, k, :], hn[:, k, :], x_hi[:, k, :].bitcast(F32), ALU.subtract)\
                    .then_inc(xlo_done, 1)

            def residual(scale, ended, n=None, tiles=range(KD)):
                for z in tiles:
                    d = ORDER5[z] if n == 5 else z
                    dve.wait_ge(*ended(d))
                    sc = scale if isinstance(scale, float) else scale[:, d:d + 1]
                    bank = (z + 2) % 8 if n == 5 else d
                    nc.vector.scalar_tensor_tensor(x[:, d, :], ps[:, bank, 0:TOK], sc, x[:, d, :], ALU.mult, ALU.add)\
                        .then_inc(x_done, 1)
                    if n is not None and n < 6 and z > tiles[0]:
                        weighted(n, z - 1)
                if n is not None and n < 6:
                    weighted(n, tiles[-1])

            def weighted(n, z):
                dve.wait_ge(xwhi_done, 8 * n + z + 1)
                d = ORDER5[z] if n == 5 else z
                nc.vector.scalar_tensor_tensor(xw_lo[:, d, :], x[:, d, :], par[:, 8 * n + d:8 * n + d + 1],
                                               xw_hi[:, d, :].bitcast(F32), ALU.mult, ALU.subtract)\
                    .then_inc(xwlo_done, 1)

            def root_inverse(n):
                dve.wait_ge(root_done, n + 1)
                nc.vector.reciprocal(rstd[:, :], rstd[:, :]).then_inc(rstd_done, 1)
                dve.wait_ge(rstd_done, n + 1)

            def normed(n, s, evac):
                tick(s)
                root_inverse(n)
                for k in range(KD):
                    nc.vector.scalar_tensor_tensor(hn[:, k, :], x[:, k, :], par[:, 8 * n + k:8 * n + k + 1],
                                                   rstd[:, :], ALU.mult, ALU.mult).then_inc(hn_done, 1)
                    if k:
                        lo_h(k - 1)
                    if k == 2:
                        evac(0)
                    if k == 4:
                        tick(s + 1)
                lo_h(KD - 1)

            def ffn(n):
                s0, b0 = S_FFN[n], NB * n

                def gate(b, i=None):
                    dve.wait_ge(used, v(s0 + 4 * (b - b0) + 2, i, 8))
                    if b > b0:
                        dve.wait_ge(alo_done, v(b, i, 2))
                    st4 = 4 * ((b - b0 + 1) % 2)
                    nc.vector.tensor_tensor(pr[:, :, :], ps[:, st4:st4 + 2, 0:TOK], rstd2, ALU.mult)\
                        .then_inc(gate_done, 1)

                def factor(b, i=None):
                    dve.wait_ge(silu_done, v(b + 1, i, 2))
                    nc.vector.tensor_tensor(sg[:, :, :], sg[:, :, :], rstd2, ALU.mult).then_inc(sg_done, 1)

                def prod(b, i=None):
                    dve.wait_ge(sg_done, v(b + 1, i, 2))
                    dve.wait_ge(used, v(s0 + 4 * (b - b0) + 4, i, 8))
                    st4 = 4 * ((b - b0 + 1) % 2) + 2
                    nc.vector.tensor_tensor(pr[:, :, :], sg[:, :, :], ps[:, st4:st4 + 2, 0:TOK], ALU.mult)\
                        .then_inc(prod_done, 1)

                def lo_a(b, i=None):
                    dve.wait_ge(ahi_done, v(b + 1, i, 2))
                    f = 2 * (b - b0) if i is None else i * 4 + 2 * (b - b0)
                    nc.vector.tensor_tensor(a_lo[:, bass.ds(f, 2), :], pr[:, :, :],
                                            a_hi[:, bass.ds(f, 2), :].bitcast(F32), ALU.subtract)\
                        .then_inc(alo_done, 1)

                def blk(b, i=None):
                    s = s0 + 4 * (b - b0)
                    if b > b0:
                        prod(b - 1, i)
                    tick(s, i)
                    tick(s + 1, i)
                    if b > b0:
                        lo_a(b - 1, i)
                    else:
                        root_inverse(FFN_NORM[n])
                    gate(b, i)
                    tick(s + 2, i)
                    factor(b, i)
                    tick(s + 3, i)

                blk(b0)
                with dve.Fori(0, NB // 2) as i:
                    blk(b0 + 1, i)
                    blk(b0 + 2, i)
                s1 = s0 + 4 * NB
                prod(b0 + NB - 1)
                tick(s1)
                lo_a(b0 + NB - 1)
                for f in range(1, 5):
                    tick(s1 + f)
                dve.wait_ge(alo_done, b0 + NB)
                with dve.Fori(0, 2 if n < 3 else 1) as i:
                    for f in range(5, 13):
                        tick(s1 + f, i)
                for f in range(13, KF - 1 if n == 3 else 13):
                    tick(s1 + f)
                residual(0.5, lambda d: (res_done, 8 * n + d + 1), FFN_NORM[n] + 1)
                tick(s1 + KF - 1)

            nc.vector.memset(mean_w[:, :], 1.0 / D)
            nc.vector.memset(eps[:, :], EPS)
            nc.vector.memset(ones[:, :], 1.0).then_inc(const_done, 1)
            dve.wait_ge(st("consts"), 1)
            link(nc.vector.tensor_tensor(fold[:, :], ident[0:96, 0:32], ident[0:96, 32:64], ALU.add))
            link(nc.vector.tensor_tensor(fold[:, :], fold[:, :], ident[0:96, 64:96], ALU.add))
            f3 = fold[:, :].rearrange("p (h b) -> p h b", h=4)
            nc.vector.tensor_tensor(headm[:, :], f3[:, :, 0], f3[:, :, 1], ALU.add)
            link(nc.vector.tensor_tensor(diagm[:, :], f3[:, 0, :], f3[:, 1, :], ALU.add))
            for b in range(2, NSAMP):
                if b < 4:
                    nc.vector.tensor_tensor(diagm[:, :], diagm[:, :], f3[:, b, :], ALU.add)
                ins = nc.vector.tensor_tensor(headm[:, :], headm[:, :], f3[:, :, b], ALU.add)
                if b < NSAMP - 1:
                    link(ins)
            ins.then_inc(st("fold_ok"), 1)
            for gi, w in enumerate(WINDOWS):
                link(nc.vector.memset(cnt[:, gi, :], 1.0 / w))
                for t in range(w - 1):
                    ins = nc.vector.memset(cnt[:, gi, t:t + 1], 1.0 / (t + 1))
                link(ins)
            for d in range(KD):
                dve.wait_ge(x_T, 1 + d // 4)
                nc.vector.tensor_copy(x[:, d, :], ps[:, d, 0:TOK]).then_inc(x_done, 1)
            dve.wait_ge(st("par_ok"), 1)
            for s in range(-LEAD, 0):
                tick(s)
            for d in range(KD):
                weighted(0, d)
            ffn(0)
            even_vector(dve, tick, link, residual, weighted, normed)
            mixer_space_free(dve)
            ffn(1)
            ffn(2)
            odd_vector(dve, tick, link, residual, root_inverse)
            dve.wait_ge(st("stored"), 16 * 5)
            ffn(3)
            dve.wait_ge(st("root_T"), 1)
            nc.vector.reciprocal(rinv[:, 0:2], ps[:, 1, 0:2])
            nc.vector.reciprocal(rinv[0:NSAMP, 2:3], ps[0:NSAMP, 1, 2:3]).then_inc(rstd_done, 1)
            dve.wait_ge(rstd_done, 7)
            dve.wait_ge(st("y_T"), 2)
            nc.vector.tensor_scalar(PTf[:, D:2 * D].rearrange("p (a b) -> p a b", a=2), ps[:, 4:6, :], rinv[:, 1:2],
                                    None, ALU.mult).then_inc(st("y_ok1"), 1)

        def even_tensor(pe, mm, three, blk_slot, first_slot, xw_slot, norm):
            tr = nc.tensor.transpose
            nwait = (lambda k: (xlo_done, k + 1))
            first_slot(S_PROJ, 2, 1)
            xw_slot(S_PROJ + 1, 1, 2, 1)
            pe.wait_ge(root_done, 2)
            for q in range(2):
                xw_slot(S_PROJ + 2 + q, q, 0)

            def slots(lo, hi):
                for q in range(lo, hi):
                    n = q // 2
                    if n >= 2 and q % 2 == 0:
                        pe.wait_ge(p_ready, n - 1)
                    blk_slot(S_PROJ + q, q % 2, 2 * ((n + 1) % 2), None, nwait if n == 2 else None)

            ch = [(c, h) for c in range(2) for h in range(4)]
            hc = [(h, c) for h in range(4) for c in range(2)]
            slots(4, 6)
            pe.wait_ge(st("consts"), 2)
            pe.wait_ge(st("hist_in"), 16)
            for c in range(CT):
                ins = tr(ps[:, 6, c * 24:(c + 1) * 24], ROWS2[0:24, c * P:(c + 1) * P], ident[0:24, 0:24])
            ins.then_inc(st("conv_hist_T"), 1)
            pe.wait_ge(st("ab_in"), 48)
            for k in range(KD):
                ins = mm(ps[0:8, 7, 0:TOK], WAB[:, k, :], hn[:, k, :], start=k == 0, stop=k == KD - 1)
            ins.then_inc(st("gb_mm"), 1)
            slots(6, 14)
            pe.wait_ge(p_ready, 6)
            pe.wait_ge(st("conv_hist"), 1)
            for c in range(CT):
                ins = tr(ps[0:11, 4 + c // 4, c % 4 * P:(c % 4 + 1) * P], PT[:, 16 + c, PROMPT - 3:TOK], ident[:, :])
            ins.then_inc(st("crow_T"), 1)
            slots(14, 16)
            pe.wait_ge(st("beta"), 1)
            pe.wait_ge(st("gb_g"), 1)
            pe.wait_ge(st("crow"), 1)
            for c in range(2):
                for y, row in ((0, 5), (1, 6)):
                    ins = tr(ps[:, 6, 16 * c + 8 * y:16 * c + 8 * y + 8], GB[:, row, c * P:(c + 1) * P], ident[0:8, 0:8])
            ins.then_inc(st("tok_T"), 1)
            for j in range(8):
                ins = mm(ps[:, 7, 8 * j:8 * j + 8], ident[0:8, j:j + 1].broadcast_to([8, P]),
                         GB[:, 5 if j < 4 else 6, PROMPT:TOK], start=True, stop=True)
            ins.then_inc(st("gb_rows_mm"), 1)
            slots(16, 17)
            pe.wait_ge(st("gb_tok"), 1)
            gt = SMALL[:, 0:32].rearrange("p (c y j) -> p c y j", c=2, y=2)
            mm(ps[:, 6, 32:40].rearrange("p (c h) -> p c h", c=2), upper[:, :], gt[:, :, 0, 0:4], start=True,
               stop=True).then_inc(st("cum_mm"), 1)
            for i, (c, h) in enumerate(ch):
                ins = mm(psA[:, i, :], gt[:, c, 0, h:h + 1].broadcast_to([P, P]), upper[:, :], start=True, stop=True)
            ins.then_inc(st("brow"), 1)
            pe.wait_ge(st("norm_sq"), 1)
            pe.wait_ge(st("consts"), 4)
            pe.wait_ge(st("bs"), 1)
            for d in range(8):
                ins = mm(ps[0:8, 7, 0:TOK], esel[:, d, :], hn[:, d, :], start=d == 0, stop=d == 7)
            ins.then_inc(st("norm_ss"), 1)
            slots(17, 20)
            pe.wait_ge(st("norm_r"), 1)
            pe.wait_ge(st("dec_diff"), 1)
            pe.wait_ge(st("ebl"), 1)
            pe.wait_ge(st("ncum"), 1)
            for y, t0 in ((0, 4), (1, 0)):
                if y:
                    pe.wait_ge(st("qk_n"), 1)
                for h in range(4):
                    ins = mm(ps[:, 4 + h, 0:TOK], ident[0:8, t0 + h:t0 + h + 1].broadcast_to([8, P]), RN[:, 0:TOK],
                             start=True, stop=True)
                ins.then_inc(st("norm_bc"), 1)
                slots(20 + y, 21 + y)
            pe.wait_ge(st("qk_n"), 2)
            for i, (c, h) in enumerate(ch):
                kk = C[:, 4 + h, c * P:(c + 1) * P]
                ins = mm(psA[:, i, :], kk, kk, start=True, stop=True)
            ins.then_inc(st("kk_mm"), 1)
            for i, (c, h) in enumerate(ch):
                ins = mm(psB[:, i, :], C[:, 4 + h, c * P:(c + 1) * P], C[:, h, c * P:(c + 1) * P], start=True,
                         stop=True)
            ins.then_inc(st("kq_mm"), 1)
            slots(22, 26)
            pe.wait_ge(st("aqk"), 1)
            pe.wait_ge(st("conv_silu"), 2)
            for i, (c, h) in enumerate(ch):
                ins = tr(psB[:, i, :], C[:, 8 + h, c * P:(c + 1) * P], ident[:, :])
            ins.then_inc(st("vt_T"), 1)
            slots(26, 27)
            pe.wait_ge(st("at"), 1)
            for i in range(8):
                ins = tr(psA[:, i, :], AT[:, i, :], ident[:, :])
            ins.then_inc(st("a_T"), 1)
            def key_query(y):
                pe.wait_ge(st("samp_kq"), y + 1)
                mm(ps[:, 7, 128 + 32 * y:160 + 32 * y], ones[:, :], WV[:, 1 + 2 * y, :], start=True, stop=True)\
                    .then_inc(st("samp_kq_mm"), 1)

            def kv_rows(y):
                pe.wait_ge(st("kv3"), y + 1)
                if y:
                    pe.wait_ge(st("kv_rows"), 1)
                for z in range(2):
                    ins = tr(ps[0:96, 7, 256 + 128 * z:384 + 128 * z], KV3[:, z].rearrange("p a b -> p (a b)"),
                             ident[:, :])
                ins.then_inc(st("kv_T"), 1)

            slots(27, 28)
            pe.wait_ge(st("vt"), 1)
            key_query(0)
            for h in range(4):
                if h:
                    slots(27 + h, 28 + h)
                pe.wait_ge(st("samp_dec"), h + 1)
                for b in range(NSAMP):
                    ins = mm(ps[:, 7, 32 + 16 * h + 2 * b:34 + 16 * h + 2 * b], SV(h)[:, b, :],
                             C[:, h:h + 5:4, PROMPT + b], start=True, stop=True)
                ins.then_inc(st("samp_read"), 1)

            pe.wait_ge(p_ready, 15)
            for i, (h, c) in enumerate(hc):
                ins = tr(psD[:, i, :], PT[:, 8 + h, c * P:(c + 1) * P], ident[:, :])
            ins.then_inc(st("hvt_T"), 1)
            slots(31, 32)
            kv_rows(0)
            pe.wait_ge(p_ready, 16)

            for r in range(LEVELS + 1):
                inverse = 1 <= r < LEVELS
                if inverse:
                    pe.wait_ge(st("inv_tc"), r)
                    for i in range(8):
                        ins = mm(psA[:, i, :], AT[:, i, :], T[:, i, :], start=True, stop=True)
                    ins.then_inc(st("inv_x"), 1)
                if r == 0:
                    pe.wait_ge(st("hg_q"), 1)
                    pe.wait_ge(st("hvt"), 1)
                else:
                    pe.wait_ge(st("hg_lvl"), r)
                    pe.wait_ge(st("hg_merge"), r + 1)
                    if r >= 2:
                        pe.wait_ge(st("inv"), min(r, LEVELS - 1))
                for i in range(8):
                    ins = mm(psC[:, i, :], KS[:, i * P:(i + 1) * P], QP[:, i * P:(i + 1) * P], start=True, stop=True)
                ins.then_inc(st("hg_att"), 1)
                if inverse:
                    pe.wait_ge(st("inv_xc"), r)
                    pe.wait_ge(st("inv"), r)
                    for i in range(8):
                        l, m = (U, X) if r < LEVELS - 1 else (X, U)
                        ins = mm(psA[:, i, :], l[:, i, :], m[:, i, :], start=True, stop=True)
                    ins.then_inc(st("inv_t" if r < LEVELS - 1 else "inv_u"), 1)
                if r == 2:
                    key_query(1)
                    kv_rows(1)
                pe.wait_ge(st("kv_rows"), r // 4 + 1)
                if r - 1 in READ:
                    j = READ[r - 1]
                    pe.wait_ge(st("samp_dec"), j + 1)
                    for b in range(NSAMP):
                        c = 8 * (j - 4) + b
                        ins = mm(ps[:, 7, c:c + 1], SV(j)[:, b, :], SMALL[:, 224 + c:225 + c], start=True, stop=True)
                    ins.then_inc(st("samp_read"), 1)
                if r:
                    pe.wait_ge(st("samp_new"), r)
                vm = VM[:, :, :].rearrange("p b n -> p (b n)")
                for y in range(2):
                    ins = mm(ps[:, 2 + y, :], KM[:, r % 4, :], vm[:, 512 * y:512 * (y + 1)], start=True, stop=True)
                ins.then_inc(st("samp_outer"), 1)
                if 1 <= r < LEVELS - 1:
                    pe.wait_ge(st("inv_tc"), r + 1)
                    pe.wait_ge(st("hg_merge"), r + 2)
                    for i in range(8):
                        ins = tr(psC[:, i, :], T[:, i, :], ident[:, :])
                    ins.then_inc(st("inv_u"), 1)

            pe.wait_ge(st("inv"), LEVELS)
            for i, (c, h) in enumerate(ch):
                ins = tr(psA[:, i, :], C[:, 4 + h, c * P:(c + 1) * P], ident[:, :])
            ins.then_inc(st("kt_T"), 1)
            pe.wait_ge(st("hg_lvl"), LEVELS + 1)
            pe.wait_ge(st("hg_merge"), LEVELS + 2)
            for i in range(8):
                ins = tr(psC[:, i, :], KS[:, i * P:(i + 1) * P], ident[:, :])
            ins.then_inc(st("hkt_T"), 1)
            for h in range(4):
                ins = mm(psB[:, h, :], U[:, h, :], VT[:, h, :], start=True, stop=True)
            ins.then_inc(st("vn0_mm"), 1)
            pe.wait_ge(st("hvt"), 1)
            pe.wait_ge(st("hkt"), 1)
            pe.wait_ge(st("samp_new"), 8)
            for y in range(2):
                for h in range(4):
                    ins = mm(ps[:, 2 + y, h * P:(h + 1) * P], HKT[:, 2 * h + y, :], HVT[:, 2 * h + y, :], start=True,
                             stop=True)
                ins.then_inc(st(("hs1_mm", "hs2_mm")[y]), 1)
            pe.wait_ge(st("kt"), 1)
            pe.wait_ge(st("vn0"), 1)
            for h in range(4):
                ins = mm(psA[:, h, :], KT[:, h, :], VN[:, h, :], start=True, stop=True)
            ins.then_inc(st("s1_mm"), 1)
            pe.wait_ge(st("hs1"), 1)
            for h in range(4):
                mm(psC[:, 2 * h, :], HVT[:, 2 * h, :], ATT[:, 2 * h, :], start=True, stop=True)
                q1 = QP[:, (2 * h + 1) * P:(2 * h + 2) * P]
                mm(psC[:, 2 * h + 1, :], HS1[:, h * P:(h + 1) * P], q1, start=True, stop=False)
                ins = mm(psC[:, 2 * h + 1, :], HVT[:, 2 * h + 1, :], ATT[:, 2 * h + 1, :], start=False, stop=True)
            ins.then_inc(st("ho_mm"), 1)
            pe.wait_ge(st("s1"), 1)
            for h in range(4):
                ins = mm(psA[:, 4 + h, :], C[:, 4 + h, P:2 * P], S1[:, h, :], start=True, stop=True)
            ins.then_inc(st("ks_mm"), 1)
            pe.wait_ge(st("rhs1"), 1)
            for h in range(4):
                ins = mm(psB[:, h, :], U[:, 4 + h, :], VT[:, 4 + h, :], start=True, stop=True)
            ins.then_inc(st("vn1_mm"), 1)

            def mean_squares(y, bank):
                pe.wait_ge(st("norm_sq"), y + 2)
                for d in range(4):
                    ins = mm(ps[0:4, bank, 0:TOK], emean[:, d, 0:4], hn[:, 4 * y + d, :], start=d == 0, stop=d == 3)
                ins.then_inc(st("norm_ss"), 1)

            def factors(y, f):
                pe.wait_ge(st("norm_r"), y + 2)
                for h in range(4):
                    ins = mm(ps[:, 4 * y + h, 0:TOK], ident[0:4, h:h + 1].broadcast_to([4, P]), f, start=True,
                             stop=True)
                ins.then_inc(st("norm_bc"), 1)

            mean_squares(0, 0)
            pe.wait_ge(st("vn1"), 1)
            pe.wait_ge(st("qe"), 1)
            for h in range(4):
                mm(psA[:, h, :], VN[:, h, :], DEC[:, h, :], start=True, stop=True)
            for h in range(4):
                mm(psA[:, 4 + h, :], S1[:, h, :], QE[:, h, :], start=True, stop=False)
                ins = mm(psA[:, 4 + h, :], VN[:, 4 + h, :], DEC[:, 4 + h, :], start=False, stop=True)
            ins.then_inc(st("o_mm"), 1)
            pe.wait_ge(st("so"), 2)
            for h in range(4):
                ins = mm(psB[:, 4 + h, :], KT[:, 4 + h, :], VN[:, 4 + h, :], start=True, stop=True)
            ins.then_inc(st("s2_mm"), 1)
            pe.wait_ge(st("hs2"), 1)
            factors(0, RN[0:4, :])
            mean_squares(1, 6)
            for q, (n, half) in enumerate(WO):
                if q == 1:
                    pe.wait_ge(st("o_b"), 1)
                    pe.wait_ge(st("s2"), 1)
                    factors(1, RN2[:, :])
                s = S_WOUT + q
                pe.wait_ge(lo_done, s + 1)
                for k4 in range(4):
                    k = 4 * half + k4
                    pe.wait_ge(st("o_lo"), k + 1)
                    for j in range(2):
                        ins = three(ps[:, 2 * n + j, 0:TOK], s, k4 * BLK + j * P, x_hi[:, k, :], x_lo[:, k, :],
                                    k == 0, k == KD - 1)
                ins.then_inc(used, 1)
            norm(2)

        def odd_tensor(pe, mm, three, first_slot, xw_slot, norm):
            tr = nc.tensor.transpose
            W = PAD + TOK
            up = PTf[:, 0:KD * W].rearrange("p (k t) -> p k t", k=KD)
            first_slot(S_PIN, 2, 4)
            pe.wait_ge(st("pbuf_in"), 16)
            pe.wait_ge(st("consts"), 3)
            for d in range(KD):
                ins = mm(ps[:, 1, 8 * d:8 * d + 8], PBUFR[0:120, d * P:(d + 1) * P], SEL[0:120, d // 2, :],
                         start=True, stop=True)
            ins.then_inc(st("pool_hist"), 1)
            for q in range(1, 8):
                banks = (2 * (q // 2) + 2) % 8
                if banks == SSB and q % 2 == 0:
                    pe.wait_ge(root_done, 5)
                    pe.wait_ge(st("hist_sums"), 1)
                elif q % 2 == 0:
                    pe.wait_ge(x_done, 8 * 4 + banks + 2)
                xw_slot(S_PIN + q, q % 2, banks, 4 if q == 1 else None)
            pe.wait_ge(st("grp_in"), 32)
            for m, g in enumerate(GROUPS):
                if m == 3:
                    pe.wait_ge(st("pool_u"), 4)
                    for d in range(KD):
                        ins = tr(ps[0:23, d // 4, d % 4 * P:(d % 4 + 1) * P], up[:, d, PAD + PROMPT - PBUF:PAD + TOK],
                                 ident[:, :])
                    ins.then_inc(st("prow_T"), 1)
                    pe.wait_ge(st("prow"), 1)
                pe.wait_ge(st("pool_d"), m + 1)
                for j in range(2):
                    for kk in range(2):
                        w = group_w(g // 2)[:, 2 * (g % 2) + kk, j * P:(j + 1) * P]
                        ins = mm(ps[:, (2 * m + 2) % 8 + j, 0:TOK], w, hn[:, 2 * g + kk, :], start=kk == 0,
                                 stop=kk == 1)
                ins.then_inc(st("group_done"), 1)
            norm(5)

        @block.tensor
        def _(pe):
            mm = nc.tensor.matmul

            def three(out, s, c0, hi, lo, first, last):
                wh = w_hi[:, s % SPL, c0:c0 + P]
                wl = w_lo[:, s % SPL, c0:c0 + P]
                mm(out, wh, hi, start=first, stop=False)
                mm(out, wh, lo, start=False, stop=False)
                return mm(out, wl, hi, start=False, stop=last)

            def blk_slot(s, half, banks, i=None, k_wait=None, hi=x_hi, lo=x_lo, order=range(KD)):
                pe.wait_ge(lo_done, v(s + 1, i, 8))
                for k in order[4 * half:4 * half + 4]:
                    if k_wait:
                        pe.wait_ge(*k_wait(k))
                    for j in range(2):
                        ins = three(ps[:, banks + j, 0:TOK], s, k % 4 * BLK + j * P, hi[:, k, :], lo[:, k, :],
                                    k == order[0], k == order[-1])
                ins.then_inc(used, 1)
                return ins

            def xw_slot(s, half, banks, n=None, i=None):
                order = ORDER5 if n == 5 else range(KD)
                blk_slot(s, half, banks, i, n is not None and (lambda k: (xwlo_done, 8 * n + order.index(k) + 1)),
                         xw_hi, xw_lo, order)

            def norm(n, tiles=range(4), frees_slot=False):
                for z in tiles:
                    d = ORDER5[z] if n == 5 else z
                    pe.wait_ge(sq_done, 8 * n + z + 1)
                    ins = mm(ps[:, sum_bank(n), 0:TOK], mean_w[:, :], hn[:, d, :], start=z == 0, stop=z == KD - 1)
                    if z == 0 and frees_slot:
                        ins.then_inc(used, 1)
                    if z == KD - 1:
                        ins.then_inc(ss_done, 1)

            def first_slot(s, banks, n):
                pe.wait_ge(x_done, 8 * n + (4 if n == 5 else banks + 2))
                xw_slot(s, 0, banks, n)
                norm(n, range(4, KD))

            def ffn(n):
                s0, b0, nn = S_FFN[n], NB * n, FFN_NORM[n]

                def blk(b, i=None):
                    s = s0 + 4 * (b - b0)
                    banks = 4 * ((b - b0 + 1) % 2)
                    for q in range(4):
                        if b and q == 0:
                            pe.wait_ge(silu_done, v(b, i, 2))
                        if b and q == 2:
                            pe.wait_ge(prod_done, v(b, i, 2))
                        if b == b0 and q == 0:
                            first_slot(s, banks, nn)
                        else:
                            if b == b0 and q == 2:
                                pe.wait_ge(x_done, 8 * nn + 8)
                            xw_slot(s + q, q % 2, banks + 2 * (q // 2),
                                    nn if b == b0 and (q == 1 or nn == 5) else None, i)

                blk(b0)
                pe.wait_ge(root_done, nn + 1)
                with pe.Fori(0, NB // 2) as i:
                    blk(b0 + 1, i)
                    blk(b0 + 2, i)
                s1 = s0 + 4 * NB

                def down(f, ds, i=None):
                    hi, lo = (a_hi[:, f, :], a_lo[:, f, :]) if i is None else \
                        [a[:, bass.ds(i * 8 + f, 1), :].rearrange("p a t -> p (a t)") for a in (a_hi, a_lo)]
                    for d in ds:
                        ins = three(ps[:, d, 0:TOK], s1 + f, d * P, hi, lo, f == 0, f == KF - 1)
                    return ins

                pe.wait_ge(lo_done, s1 + 2)
                pe.wait_ge(alo_done, b0 + NB - 1)
                down(0, range(4))
                down(1, range(4))
                pe.wait_ge(prod_done, b0 + NB)
                down(0, range(4, 8)).then_inc(used, 1)
                down(1, range(4, 8)).then_inc(used, 1)
                with pe.Fori(0, 2) as i:
                    for f in range(2, 10):
                        pe.wait_ge(lo_done, v(s1 + f + 1, i, 8))
                        down(f, range(8), i).then_inc(used, 1)
                for f in range(18, KF - 2):
                    pe.wait_ge(lo_done, s1 + f + 1)
                    down(f, range(8)).then_inc(used, 1)
                pe.wait_ge(lo_done, s1 + KF)
                pe.wait_ge(alo_done, b0 + NB)
                for d in range(KD):
                    ins = down(KF - 2, [d])
                    if d == KD - 1:
                        ins.then_inc(used, 1)
                    down(KF - 1, [d]).then_inc(res_done, 1)
                norm(nn + 1, frees_slot=True)

            pe.wait_ge(st("consts"), 1)
            pe.wait_ge(x_in, 48)
            for d in range(KD):
                for c in range(3):
                    n = P if c < CH else NSAMP
                    ins = nc.tensor.transpose(ps[:, d, c * P:c * P + n], PTf[0:n, c * D + d * P:c * D + (d + 1) * P],
                                              ident[0:n, 0:n])
                if d == 3:
                    ins.then_inc(x_T, 1)
            ins.then_inc(x_T, 1)
            pe.wait_ge(par_in, 16 * 8)
            pe.wait_ge(st("conv_par_in"), 16 * 3)
            pe.wait_ge(x_done, 8)
            nc.tensor.transpose(ps[:, 7, 0:NPAR], prow[0:NPAR, :], ident[0:NPAR, 0:NPAR]).then_inc(x_T, 1)
            pe.wait_ge(const_done, 1)
            norm(0)
            ffn(0)
            even_tensor(pe, mm, three, blk_slot, first_slot, xw_slot, norm)
            ffn(1)
            ffn(2)
            odd_tensor(pe, mm, three, first_slot, xw_slot, norm)
            ffn(3)
            def back(c, half):
                n = P if c < CH else NSAMP
                for d in range(4 * half, 4 * half + 4):
                    ins = nc.tensor.transpose(ps[0:n, 2 + 2 * c + half, d % 4 * P:(d % 4 + 1) * P],
                                              XH[:, d * TOK + c * P:d * TOK + c * P + n], ident[:, :])
                return ins

            pe.wait_ge(xwhi_done, 8 * 6 + 4)
            pe.wait_ge(x_done, 8 * 6 + 7)
            for c in range(2):
                back(c, 0)
            norm(6, range(4, KD))
            back(2, 0)
            pe.wait_ge(xwhi_done, 8 * 7)
            pe.wait_ge(x_done, 8 * 7)
            back(0, 1).then_inc(st("y_T"), 1)
            pe.wait_ge(root_done, 7)
            for c in range(3):
                n = P if c < CH else NSAMP
                ins = mm(ps[0:n, 1, c:c + 1], rstd[0:1, c * P:c * P + n], ones[0:1, 0:1], start=True, stop=True)
            ins.then_inc(st("root_T"), 1)
            for c in range(1, 3):
                back(c, 1).then_inc(st("y_T"), 1)

        @block.gpsimd
        def _(pool):
            G = nc.gpsimd
            n_chain = [0]

            def link(ins):
                n_chain[0] += 1
                ins.then_inc(pool_chain, 1)
                pool.wait_ge(pool_chain, n_chain[0])

            link(G.memset(ident[:, :], 0.0))
            G.affine_select(out=ident[:, :], in_=ident[:, :], compare_op=ALU.not_equal, fill=1.0, base=0,
                            pattern=[[-1, P]], channel_multiplier=1).then_inc(st("consts"), 1)
            pool.dma_start(prow[C_CONV:C_HGN, :], conv_w[0].rearrange("j (c p) -> (j c) p", p=P))\
                .then_inc(st("conv_par_in"), 16)
            pool.dma_start(prow[C_HGN:C_HGN + 1, :], hgn).then_inc(st("conv_par_in"), 16)
            pool.dma_start(prow[C_GDN:C_GDN + 1, :], gdn_n).then_inc(st("conv_par_in"), 16)
            link(G.memset(ab8[:, :], 0.0))
            pool.dma_start(ab8[0:4, 0:1], dt_bias.rearrange("a h -> h a")).then_inc(st("ab_in"), 16)
            pool.dma_start(ab8[0:4, 1:2], a_log.rearrange("a h -> h a")).then_inc(st("ab_in"), 16)
            pool.dma_start(WAB[:, :, :], w_in[0, :, 4096:4104].rearrange("(k p) n -> p k n", p=P))\
                .then_inc(st("ab_in"), 16)
            G.memset(upper[:, :], 1.0)
            link(G.memset(strict[:, :], 1.0))
            G.affine_select(out=upper[:, :], in_=upper[:, :], compare_op=ALU.is_ge, fill=0.0, base=0,
                            pattern=[[1, P]], channel_multiplier=-1)
            G.affine_select(out=strict[:, :], in_=strict[:, :], compare_op=ALU.is_gt, fill=0.0, base=0,
                            pattern=[[1, P]], channel_multiplier=-1)
            G.memset(lvl[:, 0:2 * LEVELS, :], 0.0)
            link(G.tensor_copy(lvl[:, 2 * LEVELS, :], ident[:, :]))
            for l in range(LEVELS):
                h = 1 << l
                pat = [[-2 * h, P // (2 * h)], [0, h]]
                neg = [[2 * h, P // (2 * h)], [0, h]]
                for m, side, lo, hi in ((l, 1, 0, h - 1), (LEVELS + l, 0, h, 2 * h - 1)):
                    part = lvl[:, m, :].rearrange("p (j two r) -> p j two r", two=2, r=h)[:, :, side, :]
                    link(G.memset(part, 1.0))
                    link(G.affine_select(out=part, in_=part, compare_op=ALU.is_ge, fill=0.0, base=-lo,
                                         pattern=pat, channel_multiplier=1))
                    link(G.affine_select(out=part, in_=part, compare_op=ALU.is_ge, fill=0.0, base=hi,
                                         pattern=neg, channel_multiplier=-1))
            link(G.memset(qscale[:, :], 1.0))
            G.affine_select(out=qscale[:, :], in_=qscale[:, :], compare_op=ALU.is_ge, fill=DH ** -0.5, base=-4,
                            pattern=[[0, 1]], channel_multiplier=1).then_inc(st("consts"), 1)
            link(G.memset(SEL[:, :, :], 1.0))
            for gi, w in enumerate(WINDOWS):
                link(G.affine_select(out=SEL[:, gi, :], in_=SEL[:, gi, :], compare_op=ALU.is_ge, fill=0.0,
                                     base=-(PBUF - (w - 1)), pattern=[[-PBUF, NSAMP]], channel_multiplier=1))
                ins = G.affine_select(out=SEL[:, gi, :], in_=SEL[:, gi, :], compare_op=ALU.is_ge, fill=0.0,
                                      base=PBUF - 1, pattern=[[PBUF, NSAMP]], channel_multiplier=-1)
            ins.then_inc(st("consts"), 1)
            outs = [0]

            def store(dst, src):
                outs[0] += 16
                pool.dma_start(dst, src).then_inc(st("stored"), 16)

            store(conv_s[0, :, 0:CONV - 2, :], state_conv[0, :, 1:CONV - 1, :])
            store(pool_s[0, :, 0:PBUF - 1, :], state_pool[0, :, 1:PBUF, :])
            pool.wait_ge(x_done, 8 * 2)
            pool.dma_start(ROWS2[0:24, 0:CT * P], state_conv[0].rearrange("b r n -> (b r) n"))\
                .then_inc(st("hist_in"), 16)
            link(G.memset(esel[:, :, :], 0.0))
            link(G.memset(emean[:, :, :], 0.0))
            for d in range(8):
                G.memset(esel[:, d, d:d + 1], 1.0)
                ins = G.memset(emean[:, d, d:d + 1], 1.0 / DH)
            ins.then_inc(st("consts"), 1)

            def load_state(j):
                src = (state_gdn if j < 4 else state_hgrn)[0, :, j % 4]
                pool.dma_start(SV(j), src.rearrange("b k v -> k b v"))\
                    .then_inc(st(f"samp_in{j if j < 6 else j - 6}"), 16)

            load_state(0)
            load_state(1)
            pool.wait_ge(st("conv_hist_T"), 1)
            load_state(2)
            load_state(3)
            pool.wait_ge(st("crow"), 1)
            pool.dma_start(conv_p[0, 0], CROW[0:3, :]).then_inc(st("conv_rows_out"), 16)
            pool.dma_start(conv_s[0, :, CONV - 2, :], CROW[3:11, :]).then_inc(st("conv_rows_out"), 16)
            pool.wait_ge(used, S_PROJ + 32)
            load_state(4)
            load_state(5)
            for j in range(8):
                pool.wait_ge(st("samp_new"), j + 1)
                dst = (gdn_s if j < 4 else hg_s)[0, :, j % 4]
                pool.dma_start(dst.rearrange("b k v -> k b v"), SV(j))\
                    .then_inc(st(f"samp_out{j if j < 6 else j - 6}"), 16)
                if 1 <= j <= 2:
                    pool.wait_ge(st(f"samp_out{j - 1}"), 16)
                    load_state(j + 5)
            pool.wait_ge(st("hs2"), 1)
            pool.dma_start(hg_p[0, 0].rearrange("h k v -> k h v"), HS2.rearrange("p (h n) -> p h n", h=4))\
                .then_inc(st("hs2_out"), 16)
            pool.wait_ge(st("s2"), 1)
            store(gdn_p[0, 0].rearrange("h k v -> k h v"), S2[:, :, :])
            pool.wait_ge(x_done, 8 * 3)
            for half in range(2):
                pool.dma_start(group_w(half), pool_grp[0, 2 * half:2 * half + 2]
                               .rearrange("g (k p) n -> p (g k) n", p=P)).then_inc(st("grp_in"), 16)
            samples_stored(pool, (0, 1))
            pool.dma_start(PBUFR[0:NSAMP * PBUF, 0:D], state_pool[0].rearrange("b r n -> (b r) n"))\
                .then_inc(st("pbuf_in"), 16)
            pool.wait_ge(st("prow"), 1)
            prows = C[:, 0:4, 0:256]
            store(pool_p[0, 0].rearrange("t (a n) -> t a n", a=4), prows[0:PBUF])
            store(pool_s[0, :, PBUF - 1, :].rearrange("t (a n) -> t a n", a=4), prows[PBUF:PBUF + NSAMP])
            pool.wait_ge(st("stored"), outs[0])


_INS = ["x_prompt", "x_sample", "state_hgrn", "state_gdn", "state_gdn_conv", "state_pool", "w_in_even",
        "hgrn_norm_w", "gdn_conv_w", "gdn_a_log", "gdn_dt_bias", "gdn_norm_w", "w_out_even", "pool_w_in",
        "pool_w_group", "pool_scale", "norm_ffn1", "ffn1_w_gate", "ffn1_w_up", "ffn1_w_down", "norm_mix",
        "norm_ffn2", "ffn2_w_gate", "ffn2_w_up", "ffn2_w_down", "final_norm"]
_OUTS = [(1, PROMPT, D), (NSAMP, 1, D), (1, 1, HEADS, DH, DH), (1, 1, HEADS, DH, DH), (1, 1, CONV - 1, 3 * MIX),
         (1, 1, PBUF, D), (1, NSAMP, HEADS, DH, DH), (1, NSAMP, HEADS, DH, DH), (1, NSAMP, CONV - 1, 3 * MIX),
         (1, NSAMP, PBUF, D)]


def kernel(**inputs):
    from concourse import bacc
    from concourse.bass_utils import run_bass_kernel_spmd

    nc = bacc.Bacc("TRN2", target_bir_lowering=False, num_devices=1)
    arrays, ins, outs = {}, [], []
    for name in _INS:
        a = np.ascontiguousarray(inputs[name])
        arrays[f"in_{name}"] = a
        ins.append(nc.dram_tensor(f"in_{name}", a.shape, mybir.dt.from_np(a.dtype), kind="ExternalInput").ap())
    for i, shape in enumerate(_OUTS):
        outs.append(nc.dram_tensor(f"out_{i}", shape, F32, kind="ExternalOutput").ap())
    build(nc, ins, outs)
    r = run_bass_kernel_spmd(nc, [arrays], core_ids=[0])
    return tuple(r.results[0][f"out_{i}"] for i in range(len(_OUTS)))
```
